# Optimizing a Trainium2 kernel written in Bass

```python
import math
import jax, jax.numpy as jnp
from jax import lax
import numpy as np

D_MODEL = 1024
BATCH = 1
SEQ = 256
DEPTH = 2

MEM_LEN = 256
CONV_WIDTH = D_MODEL // 2
CONV_KERNEL = 31
SSM_WIDTH = D_MODEL // 2
SSM_GROUP = 16
SSM_GROUPS = SSM_WIDTH // SSM_GROUP
SSM_STATE = 64
XATTN_HEADS = 4
XATTN_HEAD_DIM = D_MODEL // XATTN_HEADS
D_FF = 2816
N_EXPERTS = 8
TOP_K = 2
D_FF_EXPERT = 3584
N_MOE = DEPTH // 2
N_DENSE = DEPTH - N_MOE
IN_COLS = 2 * CONV_WIDTH + SSM_WIDTH + 2 * D_MODEL
RMS_EPS = 1e-6
LN_EPS = 1e-5
DT_MIN = 1e-3
DT_MAX = 1e-1

kernel_name = "hybrid_conv_s5_xattn_moe_trunk"

def rmsnorm(x, g):
    xf = x.astype(jnp.float32)
    y = xf * lax.rsqrt(jnp.mean(xf * xf, axis=-1, keepdims=True) + RMS_EPS)
    return (y * g.astype(jnp.float32)).astype(x.dtype)

def layernorm(x, g, b):
    xf = x.astype(jnp.float32)
    mu = jnp.mean(xf, axis=-1, keepdims=True)
    xc = xf - mu
    y = xc * lax.rsqrt(jnp.mean(xc * xc, axis=-1, keepdims=True) + LN_EPS)
    return (y * g.astype(jnp.float32) + b.astype(jnp.float32)).astype(x.dtype)

def causal_depthwise_conv(u, w, b):
    c = u.shape[-1]
    y = lax.conv_general_dilated(
        u, w[:, None, :].astype(u.dtype), window_strides=(1,),
        padding=[(CONV_KERNEL - 1, 0)],
        dimension_numbers=("NWC", "WIO", "NWC"),
        feature_group_count=c)
    return y + b.astype(u.dtype)

def conv_branch(u_glu, conv_w, conv_b, ln_g, ln_b, w_pw):
    a, gate = jnp.split(u_glu, 2, axis=-1)
    u = a * jax.nn.sigmoid(gate)
    u = causal_depthwise_conv(u, conv_w, conv_b)
    u = jax.nn.silu(layernorm(u, ln_g, ln_b))
    return u @ w_pw

def ssm_branch(u, lam_re, lam_im, log_dt, b_re, b_im, c_re, c_im, d_skip, w_glu):
    dtype = u.dtype
    bsz, s, _ = u.shape
    uf = u.astype(jnp.float32).reshape(bsz, s, SSM_GROUPS, SSM_GROUP)
    lr = lam_re.astype(jnp.float32)
    li = lam_im.astype(jnp.float32)
    dt = jnp.exp(log_dt.astype(jnp.float32))[:, None]
    mag = jnp.exp(lr * dt)
    ar = mag * jnp.cos(li * dt)
    ai = mag * jnp.sin(li * dt)
    den = lr * lr + li * li
    xr = ar - 1.0
    kr = (xr * lr + ai * li) / den
    ki = (ai * lr - xr * li) / den
    br = b_re.astype(jnp.float32)
    bi = b_im.astype(jnp.float32)
    bbar_r = kr[..., None] * br - ki[..., None] * bi
    bbar_i = kr[..., None] * bi + ki[..., None] * br
    bu_r = jnp.einsum("bsgh,gph->bsgp", uf, bbar_r)
    bu_i = jnp.einsum("bsgh,gph->bsgp", uf, bbar_i)
    a_r = jnp.broadcast_to(ar[None, None], (1, s, SSM_GROUPS, SSM_STATE))
    a_i = jnp.broadcast_to(ai[None, None], (1, s, SSM_GROUPS, SSM_STATE))

    def combine(e1, e2):
        a1r, a1i, b1r, b1i = e1
        a2r, a2i, b2r, b2i = e2
        return (a2r * a1r - a2i * a1i,
                a2r * a1i + a2i * a1r,
                a2r * b1r - a2i * b1i + b2r,
                a2r * b1i + a2i * b1r + b2i)

    _, _, h_r, h_i = lax.associative_scan(combine, (a_r, a_i, bu_r, bu_i), axis=1)
    y = (jnp.einsum("bsgp,ghp->bsgh", h_r, c_re.astype(jnp.float32))
         - jnp.einsum("bsgp,ghp->bsgh", h_i, c_im.astype(jnp.float32))
         + d_skip.astype(jnp.float32) * uf)
    y = jax.nn.gelu(y).reshape(bsz, s, SSM_WIDTH).astype(dtype)
    za, zg = jnp.split(y @ w_glu, 2, axis=-1)
    return za * jax.nn.sigmoid(zg)

def cross_attention(hn, mem_n, w_q, w_kv, w_o):
    bsz, s, _ = hn.shape
    m = mem_n.shape[1]
    q = (hn @ w_q).reshape(bsz, s, XATTN_HEADS, XATTN_HEAD_DIM)
    k, v = jnp.split(mem_n @ w_kv, 2, axis=-1)
    k = k.reshape(bsz, m, XATTN_HEADS, XATTN_HEAD_DIM)
    v = v.reshape(bsz, m, XATTN_HEADS, XATTN_HEAD_DIM)
    scores = jnp.einsum("bshd,bmhd->bhsm", q, k).astype(jnp.float32) / math.sqrt(XATTN_HEAD_DIM)
    p = jax.nn.softmax(scores, axis=-1).astype(v.dtype)
    o = jnp.einsum("bhsm,bmhd->bshd", p, v).reshape(bsz, s, D_MODEL)
    return o @ w_o

def swiglu(x, w_gate_up, w_down):
    g, u = jnp.split(x @ w_gate_up, 2, axis=-1)
    return (jax.nn.silu(g) * u) @ w_down

def moe_swiglu(x, router_w, router_b, w_gate_up, w_down):
    bsz, s, d = x.shape
    t = x.reshape(bsz * s, d)
    logits = (t @ router_w).astype(jnp.float32) + router_b.astype(jnp.float32)
    top_vals, top_idx = lax.top_k(logits, TOP_K)
    top_w = jax.nn.softmax(top_vals, axis=-1)
    gates = jnp.sum(jax.nn.one_hot(top_idx, N_EXPERTS, dtype=jnp.float32) * top_w[..., None], axis=1)
    out = jnp.zeros((bsz * s, d), jnp.float32)
    for e in range(N_EXPERTS):
        out = out + gates[:, e:e + 1] * swiglu(t, w_gate_up[e], w_down[e]).astype(jnp.float32)
    return out.astype(x.dtype).reshape(bsz, s, d)

def setup_inputs(seed: int = 0) -> dict:
    key = jax.random.key(seed)
    ks = iter(jax.random.split(key, 40))
    f32 = jnp.float32
    L = DEPTH

    def nrm(shape, scale):
        return jax.random.normal(next(ks), shape, f32) * scale

    def gain(shape):
        return 1.0 + 0.02 * jax.random.normal(next(ks), shape, f32)

    lam_im0 = jnp.pi * jnp.arange(SSM_STATE, dtype=f32)
    return {
        "x": nrm((BATCH, SEQ, D_MODEL), 1.0),
        "mem": nrm((BATCH, MEM_LEN, D_MODEL), 1.0),
        "mem_norm_g": gain((D_MODEL,)),
        "norm_mix_g": gain((L, D_MODEL)),
        "w_in": nrm((L, D_MODEL, IN_COLS), D_MODEL ** -0.5),
        "conv_w": nrm((L, CONV_KERNEL, CONV_WIDTH), CONV_KERNEL ** -0.5),
        "conv_b": nrm((L, CONV_WIDTH), 0.02),
        "conv_ln_g": gain((L, CONV_WIDTH)),
        "conv_ln_b": nrm((L, CONV_WIDTH), 0.02),
        "w_conv_pw": nrm((L, CONV_WIDTH, D_MODEL), CONV_WIDTH ** -0.5),
        "ssm_lambda_re": -0.5 + nrm((L, SSM_GROUPS, SSM_STATE), 0.01),
        "ssm_lambda_im": lam_im0 + nrm((L, SSM_GROUPS, SSM_STATE), 0.01),
        "ssm_log_dt": jax.random.uniform(next(ks), (L, SSM_GROUPS), f32,
                                         math.log(DT_MIN), math.log(DT_MAX)),
        "ssm_b_re": nrm((L, SSM_GROUPS, SSM_STATE, SSM_GROUP), (2 * SSM_GROUP) ** -0.5),
        "ssm_b_im": nrm((L, SSM_GROUPS, SSM_STATE, SSM_GROUP), (2 * SSM_GROUP) ** -0.5),
        "ssm_c_re": nrm((L, SSM_GROUPS, SSM_GROUP, SSM_STATE), SSM_STATE ** -0.5),
        "ssm_c_im": nrm((L, SSM_GROUPS, SSM_GROUP, SSM_STATE), SSM_STATE ** -0.5),
        "ssm_d": nrm((L, SSM_GROUPS, SSM_GROUP), 1.0),
        "w_ssm_glu": nrm((L, SSM_WIDTH, 2 * D_MODEL), SSM_WIDTH ** -0.5),
        "w_out": nrm((L, D_MODEL, D_MODEL), D_MODEL ** -0.5),
        "norm_xattn_g": gain((L, D_MODEL)),
        "w_q": nrm((L, D_MODEL, D_MODEL), D_MODEL ** -0.5),
        "w_kv": nrm((L, D_MODEL, 2 * D_MODEL), D_MODEL ** -0.5),
        "w_o": nrm((L, D_MODEL, D_MODEL), D_MODEL ** -0.5),
        "norm_ffn_g": gain((L, D_MODEL)),
        "ffn_w_gate_up": nrm((N_DENSE, D_MODEL, 2 * D_FF), D_MODEL ** -0.5),
        "ffn_w_down": nrm((N_DENSE, D_FF, D_MODEL), D_FF ** -0.5),
        "router_w": nrm((N_MOE, D_MODEL, N_EXPERTS), D_MODEL ** -0.5),
        "router_b": nrm((N_MOE, N_EXPERTS), 0.01),
        "moe_w_gate_up": nrm((N_MOE, N_EXPERTS, D_MODEL, 2 * D_FF_EXPERT), D_MODEL ** -0.5),
        "moe_w_down": nrm((N_MOE, N_EXPERTS, D_FF_EXPERT, D_MODEL), D_FF_EXPERT ** -0.5),
        "final_norm_g": gain((D_MODEL,)),
    }

def reference(x, mem, mem_norm_g, norm_mix_g, w_in, conv_w, conv_b, conv_ln_g, conv_ln_b,
              w_conv_pw, ssm_lambda_re, ssm_lambda_im, ssm_log_dt, ssm_b_re, ssm_b_im,
              ssm_c_re, ssm_c_im, ssm_d, w_ssm_glu, w_out, norm_xattn_g, w_q, w_kv, w_o,
              norm_ffn_g, ffn_w_gate_up, ffn_w_down, router_w, router_b, moe_w_gate_up,
              moe_w_down, final_norm_g):
    mem_n = rmsnorm(mem, mem_norm_g)
    c0 = 2 * CONV_WIDTH
    c1 = c0 + SSM_WIDTH
    h = x
    for i in range(DEPTH):
        hn = rmsnorm(h, norm_mix_g[i])
        proj = hn @ w_in[i]
        u_conv = proj[..., :c0]
        u_ssm = proj[..., c0:c1]
        g_a, g_b = jnp.split(jax.nn.sigmoid(proj[..., c1:]), 2, axis=-1)
        y_a = conv_branch(u_conv, conv_w[i], conv_b[i], conv_ln_g[i], conv_ln_b[i], w_conv_pw[i])
        y_b = ssm_branch(u_ssm, ssm_lambda_re[i], ssm_lambda_im[i], ssm_log_dt[i],
                         ssm_b_re[i], ssm_b_im[i], ssm_c_re[i], ssm_c_im[i], ssm_d[i],
                         w_ssm_glu[i])
        h = h + (g_a * y_a + g_b * y_b) @ w_out[i]
        h = h + cross_attention(rmsnorm(h, norm_xattn_g[i]), mem_n, w_q[i], w_kv[i], w_o[i])
        hn = rmsnorm(h, norm_ffn_g[i])
        j = i // 2
        if i % 2 == 0:
            h = h + swiglu(hn, ffn_w_gate_up[j], ffn_w_down[j])
        else:
            h = h + moe_swiglu(hn, router_w[j], router_b[j], moe_w_gate_up[j], moe_w_down[j])
    return rmsnorm(h, final_norm_g)


_drawn_inputs = setup_inputs


def setup_inputs(seed=0):
    import zlib

    import numpy as np

    out = dict(_drawn_inputs(seed))
    spreads = {}
    factors = {'mem_norm_g': 3.55,
     'ssm_lambda_re': 64.0,
     'norm_xattn_g': 4.242,
     'router_b': 27.229,
     'final_norm_g': 8.413,
     'norm_ffn_g': 2.869}
    for name, (base, spread) in spreads.items():
        noise = np.random.default_rng([zlib.crc32(name.encode()), seed]).standard_normal(out[name].shape)
        drawn = base * np.exp(spread * noise) if base else spread * noise
        out[name] = __import__('jax').numpy.asarray(drawn.astype(out[name].dtype))
    for name, factor in factors.items():
        out[name] = (out[name] * factor).astype(out[name].dtype)
    return out
```

```python
import math
from contextlib import ExitStack

import concourse.bass as bass
from concourse import mybir

F32 = mybir.dt.float32
I32 = mybir.dt.int32
U32 = mybir.dt.uint32
ALU = mybir.AluOpType
ACT = mybir.ActivationFunctionType
AX_X = mybir.AxisListType.X

P = 128
T = 256
TT = T // P
D = 1024
KD = D // P
L = 2
CW = 512
CT_ = CW // P
TAPS = 31
PAD = TAPS - 1
G = 32
GH = 16
NS = 64
ST = G * NS // P
PAIRS = ST // 2
H = 4
HD = D // H
FF = 2816
FE = 3584
NE = 8
BLK = 512
CHUNK = 2048
SLOTS = 6
RING_BANKS = 6
C0 = 2 * CW
C1 = C0 + G * GH
RMS_EPS = 1e-6
LN_EPS = 1e-5
FBLK = FF // 256
EBLK = FE // 256
FT = FF // P
ET = FE // P
MAGIC = 12582912.0
TWO_PI_A = 6.28125
TWO_PI_B = 0.0019350051879882812
TWO_PI_C = 2 * math.pi - TWO_PI_A - TWO_PI_B
PI_BELOW = 3.1415925

ROW_MIX, ROW_X, ROW_FFN, ROW_CB, ROW_LG, ROW_LB, ROW_D, ROW_MEM = 0, 8, 16, 24, 28, 32, 36, 40
ROW_LR, ROW_LI, ROW_DT = 48, 64, 96
ROWS = 112


SMALL = ["ldt", "lr", "li", "dt", "lrdt", "lidt", "mag", "ang", "aabs", "s1", "c1", "ar", "ai", "xr", "den",
         "rden", "kr", "ki", "t1", "t2", "rnd"]


def make_plan():
    plan = []
    for l in range(L):
        plan += [("hT", l, i) for i in range(4)]
        plan += [("cg", l, i) for i in range(2)] + [("ca", l, i) for i in range(2)]
        plan += [("us", l, i) for i in range(2)]
        plan += [("bd", l, r) for r in range(2)] + [("ct", l, r) for r in range(2)]
        if l == 0:
            plan += [("memT", i) for i in range(4)]
        for p in range(PAIRS):
            plan += [("bu", l, p, r) for r in range(2)]
            kind = "gt" if p < 4 else "k" if p < 6 else "v"
            plan += [(kind, l, p % 4 if p < 4 else p % 2, i) for i in range(2)]
        plan += [("mean", l)]
        plan += [("zg", l, 0, t) for t in range(TT)] + [("za", l, 0, t) for t in range(TT)]
        plan += [("var", l)]
        plan += [("zg", l, 1, t) for t in range(TT)] + [("za", l, 1, t) for t in range(TT)]
        plan += [("ya", l, n, t) for n in range(2) for t in range(TT)]
        plan += [("mT", l, i) for i in range(4)]
        plan += [("out", l, n, t) for n in range(2) for t in range(TT)]
        plan += [("hT2", l, i) for i in range(4)]
        plan += [("q", l, n, i) for n in range(2) for i in range(2)]
        for h in range(H + 1):
            if h < H:
                plan += [("sc", l, h)]
            if h >= 1:
                plan += [("pT", l, h - 1), ("oT", l, h - 1)]
        plan += [("o", l, n, t) for n in range(2) for t in range(TT)]
        plan += [("hT3", l, i) for i in range(4)]
        if l == 0:
            for b in range(FBLK + 1):
                if b < FBLK:
                    plan += [("fgu", b, t) for t in range(TT)]
                if b >= 1:
                    plan += [("fT", b - 1)]
            plan += [("fdn", t, n) for t in range(TT) for n in range(2)]
    plan += [("rt",), ("pos",)] + [("ga0", i) for i in range(2)]
    loop = [("gu", 0), ("gu", 1)]
    for i in range(EBLK // 2 - 1):
        loop += [("gu", 2 * i + 2), ("eT", i), ("gu", 2 * i + 3)]
    loop += [("ga", i) for i in range(2)] + [("eT", EBLK // 2 - 1), ("gT",)]
    loop += [("edn", n) for n in range(2)] + [("add", t, n) for t in range(TT) for n in range(2)]
    return plan, loop


PLAN, LOOP = make_plan()
AT = {name: i for i, name in enumerate(PLAN)}
LAT = {name: len(PLAN) + j for j, name in enumerate(LOOP)}
PER = len(LOOP)
assert PER % RING_BANKS == 0
GU_CHUNKS = 2 * EBLK
DN_CHUNKS = ET // 2
E_CHUNKS = GU_CHUNKS + DN_CHUNKS
assert E_CHUNKS % SLOTS == 0
TRUNK_CHUNKS = L * 40 + 2 * FBLK + FT // 2


class Signal:

    def __init__(self, sem):
        self.sem, self.n = sem, 0

    def by(self, ins, k=1):
        ins.then_inc(self.sem, k)
        self.n += k
        return self.n


def trunk_kernel(nc, a, out):
    with ExitStack() as ctx:
        def sb(name, shape, dt=F32):
            return ctx.enter_context(nc.sbuf_tensor(name, shape, dt))

        def sem(name):
            return ctx.enter_context(nc.semaphore(name))

        ring = sb("ring", [P, SLOTS, CHUNK])
        h = sb("h", [P, TT, D])
        hn = sb("hn", [P, TT, D])
        xT = sb("xT", [P, KD, T])
        memT = sb("memT", [P, KD, T])
        kT = sb("kT", [P, KD, T])
        v = sb("v", [P, TT, D])
        cosT = sb("cosT", [P, ST, T])
        sinT = sb("sinT", [P, ST, T])
        ident = sb("ident", [P, P])
        tri = sb("tri", [P, P])
        ones = sb("ones", [P, P])
        iota = sb("iota", [P, P])
        neg_half = sb("neg_half", [P, T])
        half_pi = sb("half_pi", [P, 1])
        cols = sb("cols", [P, L, P])
        taps = sb("taps", [P, L, TAPS * CT_])
        braw = sb("braw", [P, 2, ST, GH])
        craw = sb("craw", [P, 2, CT_, NS])
        ptmp = sb("ptmp", [P, 2, 4, T // 2])
        sm = sb("sm", [P, 21, L * ST])
        iota_i = ptmp[:, 0, 0, :].bitcast(I32)
        w2 = sb("w2", [P, 2, 4, 4])
        blkm = sb("blkm", [P, 8])
        evod = sb("evod", [P, 2])
        ssq = sb("ssq", [P, TT])
        rstd = sb("rstd", [P, TT])
        mssq = sb("mssq", [P, TT])
        mrstd = sb("mrstd", [P, TT])
        smx = sb("smx", [P, H, TT])
        snb = sb("snb", [P, H, TT])
        ssum = sb("ssum", [P, H, TT])
        srec = sb("srec", [P, H, TT])
        dtq = sb("dtq", [P, L, 2])
        ARENA = 15950
        arena = sb("arena", [P, ARENA])

        class Area:

            def __init__(self):
                self.at = 0

            def cut(self, n):
                self.at += n
                assert self.at <= ARENA, self.at
                return arena[:, self.at - n:self.at]

        mx = Area()
        gates = mx.cut(TT * 2 * D).rearrange("p (t n) -> p t n", t=TT)
        upad = mx.cut(CT_ * (PAD + T)).rearrange("p (c n) -> p c n", c=CT_)
        conv = mx.cut(CT_ * T).rearrange("p (c n) -> p c n", c=CT_)
        us = mx.cut(CT_ * T).rearrange("p (c n) -> p c n", c=CT_)
        yT = mx.cut(CT_ * T).rearrange("p (c n) -> p c n", c=CT_)
        tp = mx.cut(4 * 512).rearrange("p (i n) -> p i n", i=4)
        rin = mx.cut(2 * 512).rearrange("p (i n) -> p i n", i=2)
        gsc = rin
        hst = mx.cut(4 * 512).rearrange("p (b i n) -> p b i n", b=2, i=2)
        bdT = mx.cut(2 * CT_ * P).rearrange("p (r i n) -> p r i n", r=2, i=CT_)
        cT = mx.cut(2 * CT_ * P).rearrange("p (r i n) -> p r i n", r=2, i=CT_)
        tg = rin
        bd = gates[:, 0, 0:1024].rearrange("p (r j q h) -> p r j q h", r=2, j=ST, q=2)
        xc = gates[:, 0, 1024:2048].rearrange("p (m q n) -> p m q n", m=8, q=2)
        bt = gates[:, 1, 0:512].rearrange("p (i j h) -> p i j h", i=2, j=ST)
        merged = hn

        xa = Area()
        qT = xa.cut(KD * T).rearrange("p (k n) -> p k n", k=KD)
        oT = xa.cut(KD * T).rearrange("p (k n) -> p k n", k=KD)
        prob = xa.cut(H * TT * T).rearrange("p (h t n) -> p h t n", h=H, t=TT)
        pT = xa.cut(H * TT * T).rearrange("p (h m n) -> p h m n", h=H, m=TT)

        fa = Area()
        sil = fa.cut(4 * 256).rearrange("p (b n) -> p b n", b=4)
        h1 = fa.cut(4 * 256).rearrange("p (b n) -> p b n", b=4)
        h1T = fa.cut(FT * T).rearrange("p (f n) -> p f n", f=FT)
        xgT = fa.cut(KD * P).rearrange("p (k n) -> p k n", k=KD)
        eT = fa.cut(ET * P).rearrange("p (f n) -> p f n", f=ET)
        pick = fa.cut(TT * P).rearrange("p (t n) -> p t n", t=TT)
        pickg = fa.cut(TT * P).rearrange("p (t n) -> p t n", t=TT)
        gT = fa.cut(TT * P).rearrange("p (t n) -> p t n", t=TT)
        ye = fa.cut(D)
        rw = fa.cut(KD * NE).rearrange("p (k n) -> p k n", k=KD)
        rb = fa.cut(NE)
        lg = fa.cut(TT * NE).rearrange("p (t n) -> p t n", t=TT)
        top = fa.cut(TT * 8).rearrange("p (t n) -> p t n", t=TT)
        topi = fa.cut(TT * 8).rearrange("p (t n) -> p t n", t=TT)
        oneh = fa.cut(2 * TT * NE).rearrange("p (i t n) -> p i t n", i=2, t=TT)
        tw = fa.cut(4 * TT).rearrange("p (i t) -> p i t", i=4)
        mask = fa.cut(TT * 17).rearrange("p (t n) -> p t n", t=TT)
        gate = fa.cut(TT * 17).rearrange("p (t n) -> p t n", t=TT)
        slot = fa.cut(TT * 17).rearrange("p (t n) -> p t n", t=TT)
        fg = fa.cut(D)
        tot = fa.cut(2)
        topu = sb("topu", [P, TT, 8], U32)
        over = sb("over", [P, 1], I32)
        prow = arena[:, 0:L * 2 * P].rearrange("p (l m n) -> p l m n", l=L, m=2)
        mem = kT[:, :, :].rearrange("p (t a) n -> p t (a n)", t=TT)

        ps = ctx.enter_context(nc.psum_tensor("ps", [P, 8, 512], F32))

        def bank(i):
            return ps[:, i % RING_BANKS, :]

        slot_loaded = [sem(f"slot_loaded{i}") for i in range(SLOTS)]
        down_used = sem("down_used")
        mm_done = sem("mm_done")
        bank_free = [sem(f"bank_free{i}") for i in range(RING_BANKS)]
        x_loaded = sem("x_loaded")
        mem_loaded = sem("mem_loaded")
        rows_loaded = sem("rows_loaded")
        bc_loaded = sem("bc_loaded")
        late_loaded = sem("late_loaded")
        rows_cleared = sem("rows_cleared")
        consts_ready = sem("consts_ready")
        rows_ready = sem("rows_ready")
        par_done = sem("par_done")
        cols_ready = sem("cols_ready")
        ssm_act = sem("ssm_act")
        ssm_arg = sem("ssm_arg")
        trig_seed = sem("trig_seed")
        trig_pool = sem("trig_pool")
        trig_dve = sem("trig_dve")
        bc_used = sem("bc_used")
        bd_ready = sem("bd_ready")
        bdT_ready = sem("bdT_ready")
        cT_ready = sem("cT_ready")
        h_ready = sem("h_ready")
        ssq_ready = sem("ssq_ready")
        rstd_ready = sem("rstd_ready")
        hn_ready = sem("hn_ready")
        mssq_ready = sem("mssq_ready")
        mrstd_ready = sem("mrstd_ready")
        mn_ready = sem("mn_ready")
        xT_act = sem("xT_act")
        xT_dve = sem("xT_dve")
        memT_act = sem("memT_act")
        memT_dve = sem("memT_dve")
        tanh_ready = sem("tanh_ready")
        tanh_used = sem("tanh_used")
        us_ready = sem("us_ready")
        gates_ready = sem("gates_ready")
        kv_ready = sem("kv_ready")
        rot_in = sem("rot_in")
        rin_ready = sem("rin_ready")
        rot_out = sem("rot_out")
        hst_ready = sem("hst_ready")
        y_done = sem("y_done")
        y_read = sem("y_read")
        ypre_ready = sem("ypre_ready")
        yT_ready = sem("yT_ready")
        conv_step = sem("conv_step")
        conv_ready = sem("conv_ready")
        xc_ready = sem("xc_ready")
        sq_ready = sem("sq_ready")
        var_ready = sem("var_ready")
        lnr_ready = sem("lnr_ready")
        lnz_ready = sem("lnz_ready")
        lnt_ready = sem("lnt_ready")
        uact_ready = sem("uact_ready")
        merged_ready = sem("merged_ready")
        q_ready = sem("q_ready")
        nb_ready = sem("nb_ready")
        exp_ready = sem("exp_ready")
        prob_ready = sem("prob_ready")
        pT_ready = sem("pT_ready")
        oT_ready = sem("oT_ready")
        sil_ready = sem("sil_ready")
        h1_ready = sem("h1_ready")
        h1T_ready = sem("h1T_ready")
        topd_ready = sem("topd_ready")
        tope_ready = sem("tope_ready")
        mask_ready = sem("mask_ready")
        over_ready = sem("over_ready")
        pick_ready = sem("pick_ready")
        pickg_ready = sem("pickg_ready")
        xg_ready = sem("xg_ready")
        gT_ready = sem("gT_ready")
        ye_ready = sem("ye_ready")
        out_ready = sem("out_ready")
        out_stored = sem("out_stored")
        dve_step = sem("dve_step")
        pool_step = sem("pool_step")
        act_step = sem("act_step")

        block = ctx.enter_context(nc.Block())

        def wait_bank(eng, i):
            if i >= RING_BANKS:
                eng.wait_ge(bank_free[i % RING_BANKS], i // RING_BANKS)

        def freed(ins, i):
            ins.then_inc(bank_free[i % RING_BANKS], 1)

        def y_skip(dve, link, note, l, i):
            V = nc.vector
            u = l * CT_ + i
            dve.wait_ge(y_done, l * PAIRS + 2 * i + 2)
            link(V.scalar_tensor_tensor(yT[:, i, :], us[:, i, :], cols[:, l, ROW_D + i:ROW_D + i + 1],
                                        ps[:, 6 + u % 2, 0:T], ALU.mult, ALU.add))
            V.sem_inc(y_read, 1)
            V.sem_inc(ypre_ready, 1)

        def residual(kind, l, dve, note, result, link, free_bank):
            V = nc.vector
            for n_ in range(2):
                for t in range(TT):
                    n = AT[(kind, l, n_, t)]
                    o = result(n)
                    dst = h[:, t, n_ * BLK:(n_ + 1) * BLK]
                    link(V.tensor_tensor(dst, dst, o, ALU.add))
                    free_bank(n)
                    if n_ == 1:
                        V.sem_inc(h_ready, 1)

        def trig(E, link, l, i, tmp, mul, m):
            S = {name: sm[:, k, :] for k, name in enumerate(SMALL)}
            j0 = 4 * i
            c, s = cosT[:, j0:j0 + 4, :], sinT[:, j0:j0 + 4, :]
            c1, s1 = (S[n][:, l * ST + j0:l * ST + j0 + 4].unsqueeze(2) for n in ("c1", "s1"))
            A = tmp[:, 0, :] if len(tmp.shape) == 3 else tmp[:, 0, :, :].rearrange("p j n -> p (j n)")
            B = tmp[:, 1, :] if len(tmp.shape) == 3 else tmp[:, 1, :, :].rearrange("p j n -> p (j n)")
            link(E.memset(c[:, :, 0:1], 1.0))
            link(E.memset(s[:, :, 0:1], 0.0))
            link(E.tensor_copy(c[:, :, 1:2], c1))
            link(E.tensor_copy(s[:, :, 1:2], s1))
            n = 2
            while n < T:
                ch, sh = c[:, :, n // 2:n // 2 + 1], s[:, :, n // 2:n // 2 + 1]
                wc, ws, x, y = (mul[:, m, k, :].unsqueeze(2) for k in range(4))
                link(E.tensor_tensor(x, ch, ch, ALU.mult))
                link(E.tensor_tensor(y, sh, sh, ALU.mult))
                link(E.tensor_tensor(wc, x, y, ALU.subtract))
                link(E.tensor_tensor(x, ch, sh, ALU.mult))
                link(E.tensor_tensor(ws, x, x, ALU.add))
                a_ = A[:, 0:4 * n].rearrange("p (j n) -> p j n", j=4)
                b_ = B[:, 0:4 * n].rearrange("p (j n) -> p j n", j=4)
                wcb, wsb = wc.to_broadcast([P, 4, n]), ws.to_broadcast([P, 4, n])
                link(E.tensor_tensor(a_, c[:, :, 0:n], wcb, ALU.mult))
                link(E.tensor_tensor(b_, s[:, :, 0:n], wsb, ALU.mult))
                link(E.tensor_tensor(c[:, :, n:2 * n], a_, b_, ALU.subtract))
                link(E.tensor_tensor(a_, c[:, :, 0:n], wsb, ALU.mult))
                link(E.tensor_tensor(b_, s[:, :, 0:n], wcb, ALU.mult))
                link(E.tensor_tensor(s[:, :, n:2 * n], a_, b_, ALU.add))
                n *= 2

        def a_block(w, n0, kt=KD):
            view = w.rearrange("(k p) n -> p k n", p=P)
            return [[((0, 4, 0, BLK), view[:, 4 * c:4 * c + 4, n0:n0 + BLK])] for c in range(kt // 4)]

        def gu_block(w, f, b):
            view = w.rearrange("(k p) n -> p k n", p=P)
            return [[((0, 4, 256 * g, 256), view[:, 4 * c:4 * c + 4, g * f + 256 * b:g * f + 256 * b + 256])
                     for g in range(2)] for c in range(2)]

        def down_chunk(w, c):
            view = w.rearrange("(k p) n -> p k n", p=P)
            return [((0, 2, 0, D), view[:, 2 * c:2 * c + 2, :])]

        def trunk_chunks():
            found = []

            def add(blocks, last):
                found.extend((x, mm_done, AT[last] + 1) for x in blocks)

            for l in range(L):
                w_in, wg = a["w_in"][l], a["w_ssm_glu"][l]
                add(a_block(w_in, CW), ("cg", l, 1))
                add(a_block(w_in, 0), ("ca", l, 1))
                add(a_block(w_in, C0), ("us", l, 1))
                for p in range(4):
                    add(a_block(w_in, C1 + BLK * p), ("gt", l, p, 1))
                for p in range(4):
                    add(a_block(a["w_kv"][l], BLK * p), ("k" if p < 2 else "v", l, p % 2, 1))
                for n in range(2):
                    add(a_block(wg, D + BLK * n, 4), ("zg", l, n, 1))
                    add(a_block(wg, BLK * n, 4), ("za", l, n, 1))
                for n in range(2):
                    add(a_block(a["w_conv_pw"][l], BLK * n, 4), ("ya", l, n, 1))
                for name, kind in (("w_out", "out"), ("w_q", "q"), ("w_o", "o")):
                    for n in range(2):
                        add(a_block(a[name][l], BLK * n), (kind, l, n, 1))
                if l == 0:
                    for b in range(FBLK):
                        add(gu_block(a["ffn_w_gate_up"][0], FF, b), ("fgu", b, 1))
                    for c in range(FT // 2):
                        found.append((down_chunk(a["ffn_w_down"][0], c), down_used, c + 1) if c < FT // 2 - 1 else
                                     (down_chunk(a["ffn_w_down"][0], c), mm_done, AT[("fdn", 1, 1)] + 1))
            return found

        def load_chunk(eng, s, parts):
            for (k0, k1, c0, cn), src in parts:
                n = (CHUNK // (k1 - k0))
                dst = ring[:, s, :].rearrange("p (k n) -> p k n", n=n)[:, k0:k1, c0:c0 + cn]
                eng.dma_start(dst, src).then_inc(slot_loaded[s], 32 // len(parts))

        @block.sync
        def _(sp):
            chunks = trunk_chunks()
            assert len(chunks) == TRUNK_CHUNKS
            for n, (parts, _, _) in enumerate(chunks):
                if n >= SLOTS:
                    sp.wait_ge(*chunks[n - SLOTS][1:])
                load_chunk(sp, n % SLOTS, parts)

            def expert_chunk(e, c):
                gu, dn = a["moe_w_gate_up"][0, e], a["moe_w_down"][0, e]
                parts = gu_block(gu, FE, c // 2)[c % 2] if c < GU_CHUNKS else down_chunk(dn, c - GU_CHUNKS)
                load_chunk(sp, (TRUNK_CHUNKS + c) % SLOTS, parts)

            def released(it, c):
                if c < GU_CHUNKS:
                    sp.wait_ge(mm_done, it * PER + (LAT[("gu", c // 2)] + 1))
                elif c < E_CHUNKS - 1:
                    sp.wait_ge(down_used, it * (DN_CHUNKS - 1) + (FT // 2 + c - GU_CHUNKS))
                else:
                    sp.wait_ge(mm_done, it * PER + (LAT[("edn", 1)] + 1))

            def rest(e, it):
                for c in range(SLOTS, E_CHUNKS):
                    released(it, c - SLOTS)
                    expert_chunk(e, c)

            def head(e, it_before):
                for c in range(SLOTS):
                    released(it_before, E_CHUNKS - SLOTS + c)
                    expert_chunk(e, c)

            def all_experts(it0):
                with sp.Fori(0, NE - 1) as e:
                    rest(e, e + it0)
                    head(e + 1, e + it0)
                rest(NE - 1, NE - 1 + it0)

            for c in range(SLOTS):
                sp.wait_ge(*chunks[TRUNK_CHUNKS - SLOTS + c][1:])
                expert_chunk(0, c)
            all_experts(0)
            sp.wait_ge(over_ready, 1)
            most = sp.value_load(over[0:1, 0:1], min_val=0, max_val=T)
            with sp.If(most > P):
                head(0, NE - 1)
                all_experts(NE)
            for t in range(TT):
                sp.wait_ge(out_ready, t + 1)
                sp.dma_start(out[0, t * P:(t + 1) * P, :], hn[:, t, :]).then_inc(out_stored, 16)
            sp.wait_ge(out_stored, 16 * TT)

        @block.tensor
        def _(pe):
            task = [0]
            chunk = [0]
            sig = {}

            def need(sema, k):
                sig[id(sema)] = sig.get(id(sema), 0) + k
                pe.wait_ge(sema, sig[id(sema)])

            def begin(name):
                assert PLAN[task[0]] == name, (PLAN[task[0]], name)
                wait_bank(pe, task[0])
                return bank(task[0])

            def end(ins):
                ins.then_inc(mm_done, 1)
                task[0] += 1

            def next_chunks(k):
                got = []
                for _ in range(k):
                    n = chunk[0]
                    pe.wait_ge(slot_loaded[n % SLOTS], 32 * (n // SLOTS + 1))
                    got.append(ring[:, n % SLOTS, :])
                    chunk[0] += 1
                return got

            def token_major(names, lhs, ktiles, after=None):
                got = next_chunks(ktiles // 4)
                for t, name in enumerate(names):
                    o = begin(name)
                    for k in range(ktiles):
                        ins = pe.matmul(o, lhs[:, k, t * P:(t + 1) * P], got[k // 4][:, (k % 4) * BLK:(k % 4 + 1) * BLK],
                                        start=(k == 0), stop=(k == ktiles - 1))
                    end(ins)

            def channel_major(names, rhs):
                got = next_chunks(2)
                for i, name in enumerate(names):
                    o = begin(name)
                    for j in range(2):
                        c = 2 * i + j
                        for k in range(KD):
                            ins = pe.matmul(o[:, j * T:(j + 1) * T],
                                            got[k // 4][:, (k % 4) * BLK + c * P:(k % 4) * BLK + (c + 1) * P],
                                            rhs[:, k, :], start=(k == 0), stop=(k == KD - 1))
                    end(ins)

            def transposes(names, src, ready, per_t=True):
                for i, name in enumerate(names):
                    o = begin(name)
                    for t in range(TT):
                        if i == 0:
                            need(ready, 1)
                        for j in range(2):
                            ins = pe.transpose(o[:, j * T + t * P:j * T + (t + 1) * P],
                                               src[:, t, (2 * i + j) * P:(2 * i + j + 1) * P], ident[:, :])
                    end(ins)

            pe.wait_ge(consts_ready, 1)
            pe.wait_ge(rows_ready, 1)
            o = ps[:, 6, :]
            for l in range(L):
                pe.transpose(o[:, l * P:l * P + ROWS], prow[0:ROWS, l, 0, :], ident[0:ROWS, 0:ROWS])
                ins = pe.transpose(o[:, (2 + l) * P:(2 + l) * P + TAPS * CT_], prow[0:TAPS * CT_, l, 1, :],
                                   ident[0:TAPS * CT_, 0:TAPS * CT_])
            ins.then_inc(par_done, 1)

            for l in range(L):
                transposes([("hT", l, i) for i in range(4)], hn, hn_ready)
                need(xT_act, 4)
                need(xT_dve, 2)
                channel_major([("cg", l, i) for i in range(2)], xT)
                channel_major([("ca", l, i) for i in range(2)], xT)
                channel_major([("us", l, i) for i in range(2)], xT)
                need(bd_ready, 2)
                for r in range(2):
                    o = begin(("bd", l, r))
                    for i in range(CT_):
                        ins = pe.transpose(o[:, i * P:(i + 1) * P],
                                           bd[:, r, 4 * i:4 * i + 4, :, :].rearrange("p j q h -> p (j q h)"), ident[:, :])
                    end(ins)
                for r in range(2):
                    o = begin(("ct", l, r))
                    for i in range(CT_):
                        ins = pe.transpose(o[:, i * P:(i + 1) * P],
                                           xc[:, 4 * r + i, :, :].rearrange("p q n -> p (q n)"), ident[:, :])
                    end(ins)
                if l == 0:
                    for i in range(4):
                        o = begin(("memT", i))
                        for t in range(TT):
                            if i == 0:
                                need(mn_ready, 1)
                            for j in range(2):
                                ins = pe.transpose(o[:, j * T + t * P:j * T + (t + 1) * P],
                                                   mem[:, t, (2 * i + j) * P:(2 * i + j + 1) * P], ident[:, :])
                        end(ins)

                def y_pair(p):
                    i = p // 2
                    u = l * CT_ + i
                    if p % 2 == 0 and u >= 2:
                        pe.wait_ge(y_read, u - 1)
                    if p == 0:
                        need(cT_ready, 2)
                    need(hst_ready, 2)
                    for s in range(2):
                        jj = (2 * p + s) % 4
                        for r in range(2):
                            ins = pe.matmul(ps[32 * jj:32 * jj + 32, 6 + u % 2, 0:T], cT[:, r, i, 32 * jj:32 * jj + 32],
                                            hst[:, p % 2, r, s * T:(s + 1) * T], start=(r == 0), stop=(r == 1),
                                            tile_position=(0, 32 * jj))
                    ins.then_inc(y_done, 1)

                need(us_ready, 2)
                need(bdT_ready, 2)
                for p in range(PAIRS):
                    for s in range(2):
                        o = begin(("bu", l, p, s))
                        j = 2 * p + s
                        q0 = 32 * (j % 4)
                        for r in range(2):
                            ins = pe.matmul(o[:, r * T:(r + 1) * T], bdT[q0:q0 + 32, r, j // 4, :],
                                            us[q0:q0 + 32, j // 4, :], start=True, stop=True,
                                            tile_position=(q0, 0))
                        end(ins)
                    if p < 4:
                        token_major([("gt", l, p, t) for t in range(TT)], xT, KD)
                    else:
                        if l == 0 and p == 4:
                            need(memT_act, 4)
                            need(memT_dve, 2)
                        if p < 6:
                            channel_major([("k", l, p - 4, i) for i in range(2)], memT)
                        else:
                            token_major([("v", l, p - 6, t) for t in range(TT)], memT, KD)
                    if p >= 1:
                        y_pair(p - 1)
                y_pair(PAIRS - 1)

                o = begin(("mean", l))
                need(conv_ready, 1)
                for c in range(CT_):
                    ins = pe.matmul(o[:, 0:T], ones[:, :], conv[:, c, :], start=(c == 0), stop=(c == CT_ - 1))
                end(ins)
                need(yT_ready, CT_)
                for n in range(2):
                    if n == 1:
                        o = begin(("var", l))
                        need(sq_ready, 1)
                        sq = tp[:, 0:2, :].rearrange("p i n -> p (i n)").rearrange("p (c n) -> p c n", c=CT_)
                        for c in range(CT_):
                            ins = pe.matmul(o[:, 0:T], ones[:, :], sq[:, c, :], start=(c == 0), stop=(c == CT_ - 1))
                        end(ins)
                    for kind in ("zg", "za"):
                        token_major([(kind, l, n, t) for t in range(TT)], yT, CT_)
                need(uact_ready, 1)
                for n in range(2):
                    token_major([("ya", l, n, t) for t in range(TT)], conv, CT_)
                transposes([("mT", l, i) for i in range(4)], merged, merged_ready)
                need(xT_act, 4)
                need(xT_dve, 2)
                for n in range(2):
                    token_major([("out", l, n, t) for t in range(TT)], xT, KD)

                transposes([("hT2", l, i) for i in range(4)], hn, hn_ready)
                need(xT_act, 4)
                need(xT_dve, 2)
                for n in range(2):
                    channel_major([("q", l, n, i) for i in range(2)], xT)
                need(q_ready, 4)
                need(kv_ready, 8)
                for hh in range(H + 1):
                    if hh < H:
                        o = begin(("sc", l, hh))
                        for t in range(TT):
                            for k in range(2):
                                ins = pe.matmul(o[:, t * T:(t + 1) * T], qT[:, 2 * hh + k, t * P:(t + 1) * P],
                                                kT[:, 2 * hh + k, :], start=(k == 0), stop=(k == 1))
                        end(ins)
                    if hh >= 1:
                        g = hh - 1
                        o = begin(("pT", l, g))
                        need(prob_ready, TT)
                        for t in range(TT):
                            for m in range(TT):
                                ins = pe.transpose(o[:, m * T + t * P:m * T + (t + 1) * P],
                                                   prob[:, g, t, m * P:(m + 1) * P], ident[:, :])
                        end(ins)
                        o = begin(("oT", l, g))
                        need(pT_ready, 1)
                        for dtile in range(2):
                            for m in range(TT):
                                c0 = g * HD + dtile * P
                                ins = pe.matmul(o[:, dtile * T:(dtile + 1) * T], v[:, m, c0:c0 + P], pT[:, g, m, :],
                                                start=(m == 0), stop=(m == TT - 1))
                        end(ins)
                need(oT_ready, H)
                for n in range(2):
                    token_major([("o", l, n, t) for t in range(TT)], oT, KD)
                transposes([("hT3", l, i) for i in range(4)], hn, hn_ready)
                need(xT_act, 4)
                need(xT_dve, 2)
                if l == 0:
                    for b in range(FBLK + 1):
                        if b < FBLK:
                            token_major([("fgu", b, t) for t in range(TT)], xT, KD)
                        if b >= 1:
                            o = begin(("fT", b - 1))
                            need(h1_ready, TT)
                            for t in range(TT):
                                for f in range(2):
                                    ins = pe.transpose(o[:, f * T + t * P:f * T + (t + 1) * P],
                                                       h1[:, (2 * (b - 1) + t) % 4, f * P:(f + 1) * P], ident[:, :])
                            end(ins)
                    need(h1T_ready, FBLK)
                    first = task[0]
                    for i in range(4):
                        wait_bank(pe, first + i)
                    for c in range(FT // 2):
                        got = next_chunks(1)[0]
                        for k in range(2):
                            f = 2 * c + k
                            for t in range(TT):
                                for n in range(2):
                                    ins = pe.matmul(bank(first + 2 * t + n), h1T[:, f, t * P:(t + 1) * P],
                                                    got[:, k * D + n * BLK:k * D + (n + 1) * BLK],
                                                    start=(f == 0), stop=(f == FT - 1))
                                    if f == FT - 1:
                                        end(ins)
                        if c < FT // 2 - 1:
                            ins.then_inc(down_used, 1)

            o = begin(("rt",))
            pe.wait_ge(late_loaded, 16 * 3)
            for t in range(TT):
                for k in range(KD):
                    ins = pe.matmul(o[:, t * NE:(t + 1) * NE], xT[:, k, t * P:(t + 1) * P], rw[:, k, :],
                                    start=(k == 0), stop=(k == KD - 1))
            end(ins)
            o = begin(("pos",))
            pe.wait_ge(mask_ready, 1)
            pe.matmul(o[:, 0:NE], tri[:, :], mask[:, 0, 0:NE], start=True, stop=True)
            for base, w in ((NE, tri), (2 * NE, ones)):
                pe.matmul(o[:, base:base + NE], ones[:, :], mask[:, 0, 0:NE], start=True, stop=False)
                ins = pe.matmul(o[:, base:base + NE], w[:, :], mask[:, 1, 0:NE], start=False, stop=True)
            end(ins)

            def gather(o, i):
                for j in range(4):
                    k = 4 * i + j
                    for t in range(TT):
                        ins = pe.matmul(o[:, j * P:(j + 1) * P], hn[:, t, k * P:(k + 1) * P], pick[:, t, :],
                                        start=(t == 0), stop=(t == TT - 1))
                return ins

            pe.wait_ge(pick_ready, 1)
            for i in range(2):
                end(gather(begin(("ga0", i)), i))
            assert task[0] == len(PLAN) and chunk[0] == TRUNK_CHUNKS
            h1_0, h1T_0 = sig[id(h1_ready)], sig[id(h1T_ready)]

            pe.wait_ge(over_ready, 1)
            most = pe.value_load(over[0:1, 0:1], min_val=0, max_val=T)

            def expert(it):
                def lbegin(name):
                    i = LAT[name]
                    pe.wait_ge(bank_free[i % RING_BANKS], it * (PER // RING_BANKS) + i // RING_BANKS)
                    return bank(i)

                def loaded(c):
                    n = TRUNK_CHUNKS + c
                    pe.wait_ge(slot_loaded[n % SLOTS], it * (32 * E_CHUNKS // SLOTS) + 32 * (n // SLOTS + 1))
                    return ring[:, n % SLOTS, :]

                for name in LOOP:
                    if name[0] == "gu":
                        b = name[1]
                        if b == 0:
                            pe.wait_ge(xg_ready, it * 2 + 2)
                        o = lbegin(name)
                        for c in range(2):
                            got = loaded(2 * b + c)
                            for k in range(4):
                                ins = pe.matmul(o, xgT[:, 4 * c + k, :], got[:, k * BLK:(k + 1) * BLK],
                                                start=(c + k == 0), stop=(c == 1 and k == 3))
                        ins.then_inc(mm_done, 1)
                    elif name[0] == "eT":
                        i = name[1]
                        o = lbegin(name)
                        pe.wait_ge(h1_ready, it * EBLK + (h1_0 + 2 * i + 2))
                        for b in range(2):
                            for f in range(2):
                                ins = pe.transpose(o[:, (2 * b + f) * P:(2 * b + f + 1) * P],
                                                   h1[:, (2 * i + b) % 4, f * P:(f + 1) * P], ident[:, :])
                        ins.then_inc(mm_done, 1)
                    elif name[0] == "ga":
                        o = lbegin(name)
                        if name[1] == 0:
                            pe.wait_ge(pick_ready, it + 2)
                        gather(o, name[1]).then_inc(mm_done, 1)
                    elif name[0] == "gT":
                        o = lbegin(name)
                        pe.wait_ge(pickg_ready, it + 1)
                        for t in range(TT):
                            ins = pe.transpose(o[:, t * P:(t + 1) * P], pickg[:, t, :], ident[:, :])
                        ins.then_inc(mm_done, 1)
                    elif name == ("edn", 0):
                        os = [lbegin(("edn", n)) for n in range(2)]
                        pe.wait_ge(h1T_ready, it * (EBLK // 2) + (h1T_0 + EBLK // 2))
                        for c in range(DN_CHUNKS):
                            got = loaded(GU_CHUNKS + c)
                            for k in range(2):
                                f = 2 * c + k
                                for n in range(2):
                                    ins = pe.matmul(os[n], eT[:, f, :], got[:, k * D + n * BLK:k * D + (n + 1) * BLK],
                                                    start=(f == 0), stop=(f == ET - 1))
                                    if f == ET - 1:
                                        ins.then_inc(mm_done, 1)
                            if c < DN_CHUNKS - 1:
                                ins.then_inc(down_used, 1)
                    elif name[0] == "add":
                        _, t, n = name
                        o = lbegin(name)
                        if t == 0 and n == 0:
                            pe.wait_ge(gT_ready, it + 1)
                            pe.wait_ge(ye_ready, it * 2 + 2)
                        pe.matmul(o, gT[:, t, :], ye[:, n * BLK:(n + 1) * BLK], start=True, stop=True).then_inc(mm_done, 1)

            with pe.Fori(0, NE) as e:
                expert(e)
            with pe.If(most > P):
                with pe.Fori(0, NE) as e:
                    expert(e + NE)

        @block.scalar
        def _(act):
            act.wait_ge(rows_cleared, 1)
            act.dma_start(h[:, :, :], a["x"][0].rearrange("(t p) n -> p t n", p=P)).then_inc(x_loaded, 16)
            for l in range(L):
                for row, name in ((ROW_MIX, "norm_mix_g"), (ROW_X, "norm_xattn_g"), (ROW_FFN, "norm_ffn_g"),
                                  (ROW_CB, "conv_b"), (ROW_LG, "conv_ln_g"), (ROW_LB, "conv_ln_b")):
                    src = a[name][l].rearrange("(r n) -> r n", n=P)
                    act.dma_start(prow[row:row + src.shape[0], l, 0, :], src).then_inc(rows_loaded, 16)
                act.dma_start(prow[ROW_D:ROW_D + 4, l, 0, :],
                              a["ssm_d"][l].rearrange("(r g) n -> r (g n)", r=4)).then_inc(rows_loaded, 16)
                act.dma_start(prow[ROW_MEM:ROW_MEM + 8, l, 0, :],
                              a["mem_norm_g"].rearrange("(r n) -> r n", n=P)).then_inc(rows_loaded, 16)
                for row, name in ((ROW_LR, "ssm_lambda_re"), (ROW_LI, "ssm_lambda_im")):
                    act.dma_start(prow[row:row + ST, l, 0, :],
                                  a[name][l].rearrange("(j q) n -> j (q n)", q=2)).then_inc(rows_loaded, 16)
                act.dma_start(dtq[ROW_DT:ROW_DT + ST, l, :],
                              a["ssm_log_dt"][l].rearrange("(j q) -> j q", q=2)).then_inc(rows_loaded, 16)
                act.dma_start(prow[0:TAPS * CT_, l, 1, :],
                              a["conv_w"][l].rearrange("k (c n) -> (k c) n", n=P)).then_inc(rows_loaded, 16)
            act.dma_start(mem, a["mem"][0].rearrange("(t p) n -> p t n", p=P)).then_inc(mem_loaded, 16)

            done = {}

            def result(i):
                act.wait_ge(mm_done, i + 1)
                return bank(i)

            steps = Signal(act_step)

            def square_sums(src, scratch, dst, ready):
                for t in range(TT):
                    ready(t)
                    nc.scalar.activation(scratch[:, t, :], src[:, t, :], ACT.Square,
                                         accum_out=dst[:, t:t + 1]).then_inc(ssq_ready if dst is ssq else mssq_ready, 1)

            hr = [0]

            def h_sums(first=False):
                def ready(t):
                    if first:
                        if t == 0:
                            act.wait_ge(x_loaded, 16)
                    else:
                        hr[0] += 1
                        act.wait_ge(h_ready, hr[0])
                square_sums(h, hn, ssq, ready)

            def gained(l, row, i, o, dst, sema):
                for j in range(2):
                    k = 2 * i + j
                    ins = nc.scalar.activation(dst[:, k, :], o[:, j * T:(j + 1) * T], ACT.Copy,
                                               scale=cols[:, l, row + k:row + k + 1])
                    ins.then_inc(sema, 1)
                return ins

            def note(sema, k):
                done[id(sema)] = done.get(id(sema), 0) + k
                act.wait_ge(sema, done[id(sema)])

            def free_bank(i):
                act.sem_inc(bank_free[i % RING_BANKS], 1)

            def xT_from(kind, l, row):
                for i in (0, 2):
                    n = AT[(kind, l, i)]
                    o = result(n)
                    for j in range(2):
                        k = 2 * i + j
                        nc.scalar.activation(xT[:, k, :], o[:, j * T:(j + 1) * T], ACT.Copy,
                                             scale=cols[:, l, row + k:row + k + 1]).then_inc(xT_act, 1)
                    note(xT_act, 2)
                    free_bank(n)

            def copy_out(n, dst, sema, func=ACT.Copy, scale=1.0):
                o = result(n)
                nc.scalar.activation(dst, o[:, 0:512], func, scale=scale).then_inc(sema, 1)
                note(sema, 1)
                free_bank(n)

            h_sums(first=True)
            square = None
            act.wait_ge(mem_loaded, 16)
            for t in range(TT):
                nc.scalar.activation(v[:, t, :], mem[:, t, :], ACT.Square,
                                     accum_out=mssq[:, t:t + 1]).then_inc(mssq_ready, 1)
            act.wait_ge(cols_ready, 2)

            S = {n: sm[:, i, :] for i, n in enumerate(SMALL)}
            lay = lambda x: x.rearrange("p (l j) -> p l j", l=L)
            act.wait_ge(cols_ready, 3)
            nc.scalar.activation(S["dt"], S["ldt"], ACT.Exp).then_inc(ssm_act, 1)
            act.wait_ge(ssm_arg, 1)
            nc.scalar.activation(S["mag"], S["lrdt"], ACT.Exp).then_inc(ssm_act, 1)
            act.wait_ge(ssm_arg, 2)
            nc.scalar.activation(S["s1"], S["ang"], ACT.Sin).then_inc(ssm_act, 1)
            nc.scalar.activation(S["aabs"], S["ang"], ACT.Abs).then_inc(ssm_act, 1)
            act.wait_ge(ssm_act, 4)
            nc.scalar.activation(S["c1"], S["aabs"], ACT.Sin, scale=-1.0, bias=half_pi[:, 0:1]).then_inc(ssm_act, 1)

            for l in range(L):
                if l > 0:
                    h_sums()
                xT_from("hT", l, ROW_MIX)
                for i in range(2):
                    if l > 0 or i > 0:
                        pass
                    copy_out(AT[("cg", l, i)], tg[:, i, :], tanh_ready, ACT.Tanh, 0.5)
                for i in range(2):
                    copy_out(AT[("us", l, i)], us[:, 2 * i:2 * i + 2, :].rearrange("p c n -> p (c n)"), us_ready)
                for r in range(2):
                    copy_out(AT[("ct", l, r)], cT[:, r, :, :].rearrange("p i n -> p (i n)"), cT_ready,
                             scale=(1.0, -1.0)[r])
                if l == 0:
                    for i in (0, 2):
                        n = AT[("memT", i)]
                        o = result(n)
                        for j in range(2):
                            k = 2 * i + j
                            nc.scalar.activation(memT[:, k, :], o[:, j * T:(j + 1) * T], ACT.Copy,
                                                 scale=cols[:, 0, ROW_MEM + k:ROW_MEM + k + 1]).then_inc(memT_act, 1)
                        note(memT_act, 2)
                        free_bank(n)
                for p in range(PAIRS):
                    for i in range(2):
                        if p < 4:
                            copy_out(AT[("gt", l, p, i)], gates[:, i, p * BLK:(p + 1) * BLK], gates_ready, ACT.Tanh, 0.5)
                        elif p < 6:
                            c = 4 * (p - 4) + 2 * i
                            copy_out(AT[("k", l, p - 4, i)], kT[:, c:c + 2, :].rearrange("p c n -> p (c n)"), kv_ready)
                        else:
                            copy_out(AT[("v", l, p - 6, i)], v[:, i, (p - 6) * BLK:(p - 5) * BLK], kv_ready)
                for i in range(CT_):
                    note(ypre_ready, 1)
                    nc.scalar.activation(yT[:, i, :], yT[:, i, :], ACT.Gelu_apprx_tanh).then_inc(yT_ready, 1)
                note(xc_ready, 1)
                nc.scalar.activation(tp[:, 0:2, :].rearrange("p i n -> p (i n)"),
                                     conv[:, :, :].rearrange("p c n -> p (c n)"), ACT.Square).then_inc(sq_ready, 1)
                for n in range(2):
                    for t in range(TT):
                        u = (l * 2 + n) * TT + t
                        if u >= 2:
                            act.wait_ge(tanh_used, u - 1)
                        copy_out(AT[("zg", l, n, t)], tg[:, t, :], tanh_ready, ACT.Tanh, 0.5)
                    if n == 0:
                        note(lnz_ready, 1)
                        nc.scalar.activation(tp[:, 0:2, :].rearrange("p i n -> p (i n)"),
                                             conv[:, :, :].rearrange("p c n -> p (c n)"), ACT.Tanh,
                                             scale=0.5).then_inc(lnt_ready, 1)
                for i in (0, 2):
                    copy_out(AT[("mT", l, i)], xT[:, 2 * i:2 * i + 2, :].rearrange("p c n -> p (c n)"), xT_act, scale=0.25)
                    nc.scalar.sem_inc(xT_act, 1)
                    done[id(xT_act)] += 1
                h_sums()
                xT_from("hT2", l, ROW_X)
                for n in range(2):
                    for i in range(2):
                        c = 4 * n + 2 * i
                        copy_out(AT[("q", l, n, i)], qT[:, c:c + 2, :].rearrange("p c n -> p (c n)"), q_ready)
                for hh in range(H + 1):
                    if hh < H:
                        n = AT[("sc", l, hh)]
                        note(nb_ready, 1)
                        for t in range(TT):
                            nc.scalar.activation(prob[:, hh, t, :], bank(n)[:, t * T:(t + 1) * T], ACT.Exp,
                                                 scale=1.0 / math.sqrt(HD), bias=snb[:, hh, t:t + 1],
                                                 accum_out=ssum[:, hh, t:t + 1]).then_inc(exp_ready, 1)
                        note(exp_ready, TT)
                        free_bank(n)
                    if hh >= 1:
                        g = hh - 1
                        copy_out(AT[("oT", l, g)], oT[:, 2 * g:2 * g + 2, :].rearrange("p c n -> p (c n)"), oT_ready)
                h_sums()
                xT_from("hT3", l, ROW_FFN)
                if l == 0:
                    for b in range(FBLK + 1):
                        for t in range(TT):
                            if b < FBLK:
                                u = 2 * b + t
                                n = AT[("fgu", b, t)]
                                if u >= 4:
                                    act.wait_ge(h1_ready, u - 3)
                                o = result(n)
                                nc.scalar.activation(sil[:, u % 4, :], o[:, 0:256], ACT.Silu).then_inc(sil_ready, 1)
                        if b >= 1:
                            copy_out(AT[("fT", b - 1)], h1T[:, 2 * b - 2:2 * b, :].rearrange("p f n -> p (f n)"), h1T_ready)

            act.wait_ge(topd_ready, 1)
            nc.scalar.activation(tw[:, 1, :], tw[:, 0, :], ACT.Exp).then_inc(tope_ready, 1)
            act.wait_ge(over_ready, 1)
            most = act.value_load(over[0:1, 0:1], min_val=0, max_val=T)
            sil_0, h1_0, h1T_0 = 2 * FBLK, 2 * FBLK, FBLK

            def expert(it):
                def lresult(name):
                    i = LAT[name]
                    act.wait_ge(mm_done, it * PER + i + 1)
                    return bank(i)

                for name in LOOP:
                    i = LAT[name]
                    if name[0] == "gu":
                        b = name[1]
                        act.wait_ge(h1_ready, it * EBLK + (h1_0 + b - 3))
                        o = lresult(name)
                        nc.scalar.activation(sil[:, b % 4, :], o[:, 0:256], ACT.Silu).then_inc(sil_ready, 1)
                    elif name[0] == "eT":
                        o = lresult(name)
                        j = name[1]
                        nc.scalar.activation(eT[:, 4 * j:4 * j + 4, :].rearrange("p f n -> p (f n)"), o[:, 0:512],
                                             ACT.Copy).then_inc(h1T_ready, 1)
                        act.wait_ge(h1T_ready, it * (EBLK // 2) + (h1T_0 + j + 1))
                        act.sem_inc(bank_free[i % RING_BANKS], 1)
                    elif name[0] == "edn":
                        o = lresult(name)
                        n = name[1]
                        nc.scalar.activation(ye[:, n * BLK:(n + 1) * BLK], o[:, 0:512], ACT.Copy).then_inc(ye_ready, 1)
                        act.wait_ge(ye_ready, it * 2 + n + 1)
                        act.sem_inc(bank_free[i % RING_BANKS], 1)

            with act.Fori(0, NE) as e:
                expert(e)
            with act.If(most > P):
                with act.Fori(0, NE) as e:
                    expert(e + NE)
            h_sums()

        @block.vector
        def _(dve):
            V = nc.vector
            steps = Signal(dve_step)
            cnt = {}

            def link(ins):
                dve.wait_ge(dve_step, steps.by(ins))

            def note(sema, k):
                cnt[id(sema)] = cnt.get(id(sema), 0) + k
                dve.wait_ge(sema, cnt[id(sema)])

            def result(i):
                dve.wait_ge(mm_done, i + 1)
                return bank(i)

            def free_bank(i):
                V.sem_inc(bank_free[i % RING_BANKS], 1)

            def evac(n, ins, sema=None, k=1):
                if sema is None:
                    link(ins)
                else:
                    ins.then_inc(sema, k)
                    note(sema, k)
                free_bank(n)

            def normalise(src, dst, r, rsem, ready):
                for t in range(TT):
                    note(rsem, 1)
                    V.tensor_scalar(dst[:, t, :], src[:, t, :], r[:, t:t + 1], None, ALU.mult).then_inc(ready, 1)

            def xT_from(kind, l, row):
                for i in (1, 3):
                    n = AT[(kind, l, i)]
                    o = result(n)
                    gain = cols[:, l, row + 2 * i:row + 2 * i + 2].unsqueeze(2).to_broadcast([P, 2, T])
                    evac(n, V.tensor_tensor(xT[:, 2 * i:2 * i + 2, :], o.rearrange("p (j n) -> p j n", j=2), gain,
                                            ALU.mult), xT_dve)

            link(V.memset(prow[:, :, :, :], 0.0))
            V.sem_inc(rows_cleared, 1)
            V.memset(half_pi[:, :], math.pi / 2)
            dve.wait_ge(rows_loaded, 16 * 12 * L)
            for l in range(L):
                ins = V.tensor_copy(prow[ROW_DT:ROW_DT + ST, l, 0, :].rearrange("p (q n) -> p q n", q=2),
                                    dtq[ROW_DT:ROW_DT + ST, l, :].unsqueeze(2).to_broadcast([ST, 2, NS]))
                link(ins)
            V.sem_inc(rows_ready, 1)
            normalise(h, hn, rstd, rstd_ready, hn_ready)
            dve.wait_ge(par_done, 1)
            o = ps[:, 6, :]
            V.tensor_copy(cols[:, :, 0:ROWS], o.rearrange("p (m n) -> p m n", m=4)[:, 0:2, 0:ROWS]).then_inc(cols_ready, 1)
            V.tensor_scalar(taps[:, :, :], o.rearrange("p (m n) -> p m n", m=4)[:, 2:4, 0:TAPS * CT_], 0.5, None,
                            ALU.mult).then_inc(cols_ready, 1)
            dve.wait_ge(cols_ready, 2)

            S = {name: sm[:, i, :] for i, name in enumerate(SMALL)}
            for name, row in (("ldt", ROW_DT), ("lr", ROW_LR), ("li", ROW_LI)):
                link(V.tensor_copy(S[name].rearrange("p (l j) -> p l j", l=L), cols[:, :, row:row + ST]))
            V.sem_inc(cols_ready, 1)
            xT_from("hT", 0, ROW_MIX)
            note(ssm_act, 1)
            tt = lambda o_, x, y, op: link(V.tensor_tensor(S[o_], S[x], S[y], op))
            tt("lrdt", "lr", "dt", ALU.mult)
            V.sem_inc(ssm_arg, 1)
            tt("lidt", "li", "dt", ALU.mult)
            link(V.tensor_scalar(S["rnd"], S["lidt"], 1 / (2 * math.pi), MAGIC, ALU.mult, ALU.add))
            link(V.tensor_scalar(S["rnd"], S["rnd"], MAGIC, None, ALU.subtract))
            link(V.scalar_tensor_tensor(S["ang"], S["rnd"], -TWO_PI_A, S["lidt"], ALU.mult, ALU.add))
            link(V.scalar_tensor_tensor(S["ang"], S["rnd"], -TWO_PI_B, S["ang"], ALU.mult, ALU.add))
            link(V.scalar_tensor_tensor(S["ang"], S["rnd"], -TWO_PI_C, S["ang"], ALU.mult, ALU.add))
            link(V.tensor_scalar(S["ang"], S["ang"], PI_BELOW, -PI_BELOW, ALU.min, ALU.max))
            V.sem_inc(ssm_arg, 1)
            tt("den", "lr", "lr", ALU.mult)
            tt("t1", "li", "li", ALU.mult)
            tt("den", "den", "t1", ALU.add)
            link(V.reciprocal(S["rden"], S["den"]))
            note(ssm_act, 4)
            V.sem_inc(trig_seed, 1)
            tt("ar", "mag", "c1", ALU.mult)
            tt("ai", "mag", "s1", ALU.mult)
            link(V.tensor_scalar(S["xr"], S["ar"], 1.0, None, ALU.subtract))
            tt("t1", "xr", "lr", ALU.mult)
            tt("t2", "ai", "li", ALU.mult)
            tt("t1", "t1", "t2", ALU.add)
            tt("kr", "t1", "rden", ALU.mult)
            tt("t1", "ai", "lr", ALU.mult)
            tt("t2", "xr", "li", ALU.mult)
            tt("t1", "t1", "t2", ALU.subtract)
            tt("ki", "t1", "rden", ALU.mult)

            def conv_tap(l, i):
                if i >= TAPS * CT_:
                    return
                k, c = divmod(i, CT_)
                base = l * TAPS * CT_
                w = taps[:, l, k * CT_ + c:k * CT_ + c + 1]
                src = upad[:, c, k:k + T]
                if k == 0:
                    ins = V.tensor_scalar(conv[:, c, :], src, w, cols[:, l, ROW_CB + c:ROW_CB + c + 1], ALU.mult, ALU.add)
                else:
                    dve.wait_ge(conv_step, base + i - 3)
                    ins = V.scalar_tensor_tensor(conv[:, c, :], src, w, conv[:, c, :], ALU.mult, ALU.add)
                ins.then_inc(conv_step, 1)

            for l in range(L):
                if l > 0:
                    normalise(h, hn, rstd, rstd_ready, hn_ready)
                    xT_from("hT", l, ROW_MIX)
                note(bc_loaded, 64)
                kr = S["kr"].rearrange("p (l j) -> p l j", l=L)[:, l, :].unsqueeze(2).to_broadcast([P, ST, GH])
                ki = S["ki"].rearrange("p (l j) -> p l j", l=L)[:, l, :].unsqueeze(2).to_broadcast([P, ST, GH])
                link(V.memset(arena[:, 0:1024], 0.0))
                for r in range(2):
                    V.tensor_tensor(bt[:, 0, :, :], braw[:, r, :, :], kr, ALU.mult).then_inc(dve_step, 1)
                    steps.n += 1
                    link(V.tensor_tensor(bt[:, 1, :, :], braw[:, 1 - r, :, :], ki, ALU.mult))
                    for q in range(2):
                        rows = slice(64 * q, 64 * q + 64)
                        ins = V.tensor_tensor(bd[rows, r, :, q, :], bt[rows, 0, :, :], bt[rows, 1, :, :],
                                              ALU.subtract if r == 0 else ALU.add)
                        link(ins)
                V.sem_inc(bd_ready, 1)
                if l == 0:
                    note(consts_ready, 1)
                    link(V.tensor_reduce(evod[:, :], blkm[:, :].rearrange("p (b q) -> p q b", q=2), AX_X, ALU.add))
                for q in range(2):
                    link(V.tensor_scalar(xc[:, :, q, :], craw[:, :, :, :].rearrange("p r i n -> p (r i) n"),
                                         evod[:, q:q + 1], None, ALU.mult))
                V.sem_inc(bd_ready, 1)
                V.sem_inc(bc_used, 1)
                link(V.memset(upad[:, :, 0:PAD], 0.0))
                for i in range(2):
                    n = AT[("ca", l, i)]
                    o = result(n)
                    note(tanh_ready, 1)
                    evac(n, V.scalar_tensor_tensor(upad[:, 2 * i:2 * i + 2, PAD:PAD + T],
                                                   tg[:, i, :].rearrange("p (c n) -> p c n", c=2), 1.0,
                                                   o.rearrange("p (c n) -> p c n", c=2), ALU.add, ALU.mult))
                if l == 0:
                    normalise(mem, mem, mrstd, mrstd_ready, mn_ready)
                for r in range(2):
                    n = AT[("bd", l, r)]
                    o = result(n)
                    evac(n, V.tensor_copy(bdT[:, r, :, :].rearrange("p i n -> p (i n)"), o), bdT_ready)
                if l == 0:
                    for i in (1, 3):
                        n = AT[("memT", i)]
                        o = result(n)
                        gain = cols[:, 0, ROW_MEM + 2 * i:ROW_MEM + 2 * i + 2].unsqueeze(2).to_broadcast([P, 2, T])
                        evac(n, V.tensor_tensor(memT[:, 2 * i:2 * i + 2, :], o.rearrange("p (j n) -> p j n", j=2), gain,
                                                ALU.mult), memT_dve)
                    for i in range(2):
                        trig(nc.vector, link, l, i, tp, w2, 0)
                tap = [0]

                def conv_taps(k):
                    for _ in range(k):
                        conv_tap(l, tap[0])
                        tap[0] += 1

                for p in range(PAIRS):
                    cp = cosT[:, 2 * p:2 * p + 2, :].rearrange("p j n -> p (j n)")
                    sp_ = sinT[:, 2 * p:2 * p + 2, :].rearrange("p j n -> p (j n)")
                    if l == 0 and p in (4, 6):
                        note(trig_pool, 1)
                    if l == 1 and p % 2 == 0:
                        note(trig_pool, 1)
                    if l * PAIRS + p > 0:
                        dve.wait_ge(hst_ready, 2 * (l * PAIRS + p))
                    n0, n1 = AT[("bu", l, p, 0)], AT[("bu", l, p, 1)]
                    result(n1)
                    b0, b1 = n0 % RING_BANKS, n1 % RING_BANKS
                    runs = [(0, 2, b0)] if b1 == b0 + 1 else [(0, 1, b0), (1, 1, b1)]
                    for k, (tab, r) in enumerate(((cp, 0), (sp_, 1), (cp, 1), (sp_, 0))):
                        for s0, n, b in runs:
                            ins = V.tensor_tensor(tp[:, k, s0 * T:(s0 + n) * T].rearrange("p (s n) -> p s n", s=n),
                                                  tab[:, s0 * T:(s0 + n) * T].rearrange("p (s n) -> p s n", s=n),
                                                  ps[:, b:b + n, r * T:(r + 1) * T], ALU.mult)
                            if s0 + n == 2:
                                ins.then_inc(rot_in, 1)
                            else:
                                link(ins)
                    note(rot_in, 4)
                    free_bank(n0)
                    free_bank(n1)
                    conv_taps(8)
                    for r in range(2):
                        note(rin_ready, 1)
                        for s in range(2):
                            j = l * ST + 2 * p + s
                            link(V.tensor_tensor_scan(gsc[:, r, s * T:(s + 1) * T],
                                                      S["mag"][:, j:j + 1].to_broadcast([P, T]),
                                                      rin[:, r, s * T:(s + 1) * T], 0.0, ALU.mult, ALU.add))
                    V.tensor_tensor(tp[:, 0, :], cp, gsc[:, 0, :], ALU.mult).then_inc(rot_out, 1)
                    V.tensor_tensor(tp[:, 1, :], sp_, gsc[:, 1, :], ALU.mult).then_inc(rot_out, 1)
                    V.tensor_tensor(tp[:, 2, :], sp_, gsc[:, 0, :], ALU.mult).then_inc(rot_out, 1)
                    V.tensor_tensor(tp[:, 3, :], cp, gsc[:, 1, :], ALU.mult).then_inc(rot_out, 1)
                    conv_taps(8)
                    note(rot_out, 4)
                    if p % 2 == 1 and p >= 3:
                        y_skip(dve, link, note, l, (p - 3) // 2)
                dve.wait_ge(conv_step, (l + 1) * TAPS * CT_)
                V.sem_inc(conv_ready, 1)
                y_skip(dve, link, note, l, CT_ - 1)
                n = AT[("mean", l)]
                o = result(n)
                evac(n, V.scalar_tensor_tensor(conv[:, :, :], o[:, 0:T].unsqueeze(1).to_broadcast([P, CT_, T]), -1.0 / CW,
                                               conv[:, :, :], ALU.mult, ALU.add))
                V.sem_inc(xc_ready, 1)

                def glu(n_):
                    for t in range(TT):
                        n = AT[("za", l, n_, t)]
                        note(tanh_ready, 1)
                        o = result(n)
                        g = gates[:, t, D + n_ * BLK:D + (n_ + 1) * BLK]
                        dst = merged[:, t, n_ * BLK:(n_ + 1) * BLK]
                        evac(n, V.scalar_tensor_tensor(dst, g, 1.0, o, ALU.add, ALU.mult))
                        link(V.scalar_tensor_tensor(dst, tg[:, t, :], 1.0, dst, ALU.add, ALU.mult))
                        V.sem_inc(tanh_used, 1)

                note(gates_ready, 8)
                n = AT[("var", l)]
                glu(0)
                o = result(n)
                lnv = tp[:, 2, 0:T]
                evac(n, V.tensor_scalar(lnv, o[:, 0:T], 1.0 / CW, LN_EPS, ALU.mult, ALU.add))
                V.sem_inc(var_ready, 1)
                note(lnr_ready, 1)
                link(V.tensor_tensor(conv[:, :, :], conv[:, :, :], tp[:, 2, T:2 * T].unsqueeze(1).to_broadcast([P, CT_, T]),
                                     ALU.mult))
                for c in range(CT_):
                    V.tensor_scalar(conv[:, c, :], conv[:, c, :], cols[:, l, ROW_LG + c:ROW_LG + c + 1],
                                    cols[:, l, ROW_LB + c:ROW_LB + c + 1], ALU.mult, ALU.add).then_inc(dve_step, 1)
                    steps.n += 1
                dve.wait_ge(dve_step, steps.n)
                V.sem_inc(lnz_ready, 1)
                note(lnt_ready, 1)
                link(V.scalar_tensor_tensor(conv[:, :, :].rearrange("p c n -> p (c n)"),
                                            tp[:, 0:2, :].rearrange("p i n -> p (i n)"), 1.0,
                                            conv[:, :, :].rearrange("p c n -> p (c n)"), ALU.add, ALU.mult))
                V.sem_inc(uact_ready, 1)
                glu(1)
                for n_ in range(2):
                    for t in range(TT):
                        n = AT[("ya", l, n_, t)]
                        o = result(n)
                        dst = merged[:, t, n_ * BLK:(n_ + 1) * BLK]
                        evac(n, V.scalar_tensor_tensor(tp[:, 2 + t, :], gates[:, t, n_ * BLK:(n_ + 1) * BLK], 1.0, o,
                                                       ALU.add, ALU.mult))
                        link(V.tensor_tensor(dst, dst, tp[:, 2 + t, :], ALU.add))
                        if n_ == 1:
                            V.sem_inc(merged_ready, 1)
                for i in (1, 3):
                    n = AT[("mT", l, i)]
                    o = result(n)
                    evac(n, V.tensor_scalar(xT[:, 2 * i:2 * i + 2, :].rearrange("p c n -> p (c n)"), o, 0.25, None,
                                            ALU.mult), xT_dve)
                residual("out", l, dve, note, result, link, free_bank)
                normalise(h, hn, rstd, rstd_ready, hn_ready)
                xT_from("hT2", l, ROW_X)
                for hh in range(H + 1):
                    if hh < H:
                        o = result(AT[("sc", l, hh)])
                        link(V.tensor_reduce(smx[:, hh, :], o.rearrange("p (t n) -> p t n", t=TT), AX_X, ALU.max))
                        link(V.tensor_scalar(snb[:, hh, :], smx[:, hh, :], -1.0 / math.sqrt(HD), None, ALU.mult))
                        V.sem_inc(nb_ready, 1)
                        note(exp_ready, TT)
                        link(V.reciprocal(srec[:, hh, :], ssum[:, hh, :]))
                        for t in range(TT):
                            V.tensor_scalar(prob[:, hh, t, :], prob[:, hh, t, :], srec[:, hh, t:t + 1], None,
                                            ALU.mult).then_inc(prob_ready, 1)
                    if hh >= 1:
                        g = hh - 1
                        n = AT[("pT", l, g)]
                        o = result(n)
                        evac(n, V.tensor_copy(pT[:, g, :, :].rearrange("p m n -> p (m n)"), o), pT_ready)
                residual("o", l, dve, note, result, link, free_bank)
                normalise(h, hn, rstd, rstd_ready, hn_ready)
                xT_from("hT3", l, ROW_FFN)
                if l == 0:
                    for b in range(FBLK):
                        for t in range(TT):
                            u = 2 * b + t
                            n = AT[("fgu", b, t)]
                            note(sil_ready, 1)
                            if b >= 2:
                                dve.wait_ge(mm_done, AT[("fT", b - 2)] + 1)
                            evac(n, V.tensor_tensor(h1[:, u % 4, :], sil[:, u % 4, :], bank(n)[:, 256:512], ALU.mult),
                                 h1_ready)
                    for t in range(TT):
                        for n_ in range(2):
                            n = AT[("fdn", t, n_)]
                            o = result(n)
                            dst = h[:, t, n_ * BLK:(n_ + 1) * BLK]
                            evac(n, V.tensor_tensor(dst, dst, o, ALU.add))
                        V.sem_inc(h_ready, 1)

            note(late_loaded, 48)
            n = AT[("rt",)]
            o = result(n)
            for t in range(TT):
                ins = V.tensor_tensor(lg[:, t, :], o[:, t * NE:(t + 1) * NE], rb, ALU.add)
                link(ins)
            free_bank(n)
            link(V.memset(mask[:, :, :], 0.0))
            link(V.memset(gate[:, :, :], 0.0))
            link(V.memset(slot[:, :, :], -1.0))
            for t in range(TT):
                link(V.max(top[:, t, :], lg[:, t, :]))
                link(V.max_index(topu[:, t, :], top[:, t, :], lg[:, t, :]))
                link(V.tensor_copy(topi[:, t, :], topu[:, t, :]))
                link(V.tensor_tensor(tw[:, 0, t:t + 1], top[:, t, 1:2], top[:, t, 0:1], ALU.subtract))
            V.sem_inc(topd_ready, 1)
            for t in range(TT):
                for i in range(2):
                    link(V.tensor_scalar(oneh[:, i, t, :], iota[:, 0:NE], topi[:, t, i:i + 1], None, ALU.is_equal))
                link(V.tensor_tensor(mask[:, t, 0:NE], oneh[:, 0, t, :], oneh[:, 1, t, :], ALU.add))
                link(V.tensor_copy(mask[:, t, NE:2 * NE], mask[:, t, 0:NE]))
            V.sem_inc(mask_ready, 1)
            note(tope_ready, 1)
            link(V.tensor_scalar(tw[:, 2, :], tw[:, 1, :], 1.0, None, ALU.add))
            link(V.reciprocal(tw[:, 2, :], tw[:, 2, :]))
            link(V.tensor_tensor(tw[:, 3, :], tw[:, 1, :], tw[:, 2, :], ALU.mult))
            for t in range(TT):
                link(V.tensor_scalar(gate[:, t, 0:NE], oneh[:, 0, t, :], tw[:, 2, t:t + 1], None, ALU.mult))
                link(V.scalar_tensor_tensor(gate[:, t, 0:NE], oneh[:, 1, t, :], tw[:, 3, t:t + 1], gate[:, t, 0:NE],
                                            ALU.mult, ALU.add))
                link(V.tensor_copy(gate[:, t, NE:2 * NE], gate[:, t, 0:NE]))
            n = AT[("pos",)]
            o = result(n)
            for t in range(TT):
                link(V.tensor_copy(slot[:, t, 0:NE], o[:, t * NE:(t + 1) * NE]))
                link(V.tensor_scalar(slot[:, t, NE:2 * NE], o[:, t * NE:(t + 1) * NE], float(P), None, ALU.subtract))
            link(V.tensor_reduce(tot[:, 0:1], o[:, 2 * NE:3 * NE], AX_X, ALU.max))
            free_bank(n)
            link(V.tensor_copy(over[:, :], tot[:, 0:1]))
            V.sem_inc(over_ready, 1)

            def choose(dst, scale, e, sema):
                for t in range(TT):
                    ins = V.tensor_scalar(dst[:, t, :], iota[:, :], slot[:, t, e], scale[:, t, e],
                                          ALU.is_equal, ALU.mult)
                    ins.then_inc(sema, 1)

            def one(e):
                return bass.ds(e, 1)

            for t in range(TT):
                link(V.tensor_scalar(pick[:, t, :], iota[:, :], slot[:, t, 0:1], mask[:, t, 0:1], ALU.is_equal, ALU.mult))
            V.sem_inc(pick_ready, 1)

            def gathered(i, n, o):
                gain = cols[:, 1, ROW_FFN + 4 * i:ROW_FFN + 4 * i + 4].unsqueeze(2).to_broadcast([P, 4, P])
                return V.tensor_tensor(xgT[:, 4 * i:4 * i + 4, :], o.rearrange("p (j n) -> p j n", j=4), gain, ALU.mult)

            for i in range(2):
                n = AT[("ga0", i)]
                evac(n, gathered(i, n, result(n)), xg_ready)
            most = dve.value_load(over[0:1, 0:1], min_val=0, max_val=T)
            base = steps.n
            sil_0, h1_0 = 2 * FBLK, 2 * FBLK

            def expert(it):
                k = [0]

                def llink(ins):
                    ins.then_inc(dve_step, 1)
                    k[0] += 1
                    dve.wait_ge(dve_step, it * DVE_STEPS + (base + k[0]))

                def lresult(name):
                    i = LAT[name]
                    dve.wait_ge(mm_done, it * PER + i + 1)
                    return bank(i)

                def lfree(name):
                    V.sem_inc(bank_free[LAT[name] % RING_BANKS], 1)

                for t in range(TT):
                    llink(V.tensor_scalar(pickg[:, t, :], iota[:, :], slot[:, t, one(it)], gate[:, t, one(it)],
                                          ALU.is_equal, ALU.mult))
                V.sem_inc(pickg_ready, 1)
                for t in range(TT):
                    llink(V.tensor_scalar(pick[:, t, :], iota[:, :], slot[:, t, one(it + 1)], mask[:, t, one(it + 1)],
                                          ALU.is_equal, ALU.mult))
                V.sem_inc(pick_ready, 1)
                for name in LOOP:
                    if name[0] == "gu":
                        b = name[1]
                        dve.wait_ge(sil_ready, it * EBLK + (sil_0 + b + 1))
                        o = bank(LAT[name])
                        V.tensor_tensor(h1[:, b % 4, :], sil[:, b % 4, :], o[:, 256:512], ALU.mult).then_inc(h1_ready, 1)
                        dve.wait_ge(h1_ready, it * EBLK + (h1_0 + b + 1))
                        lfree(name)
                    elif name[0] == "ga":
                        i = name[1]
                        o = lresult(name)
                        gathered(i, None, o).then_inc(xg_ready, 1)
                        dve.wait_ge(xg_ready, it * 2 + (i + 3))
                        lfree(name)
                    elif name[0] == "gT":
                        o = lresult(name)
                        llink(V.tensor_copy(gT[:, :, :].rearrange("p t n -> p (t n)"), o[:, 0:TT * P]))
                        V.sem_inc(gT_ready, 1)
                        lfree(name)
                    elif name[0] == "add":
                        _, t, n_ = name
                        o = lresult(name)
                        dst = h[:, t, n_ * BLK:(n_ + 1) * BLK]
                        llink(V.tensor_tensor(dst, dst, o, ALU.add))
                        lfree(name)
                assert k[0] == DVE_STEPS, k[0]

            DVE_STEPS = 2 * TT + 1 + 2 * TT
            with dve.Fori(0, NE) as e:
                expert(e)
            with dve.If(most > P):
                with dve.Fori(0, NE) as e:
                    expert(e + NE)
            for t in range(TT):
                V.sem_inc(h_ready, 1)
            for t in range(TT):
                note(rstd_ready, 1)
                V.tensor_scalar(hn[:, t, :], h[:, t, :], rstd[:, t:t + 1], None, ALU.mult).then_inc(hn_ready, 1)
                dve.wait_ge(hn_ready, (3 * L + 1) * TT - TT + t + 1)
                V.tensor_tensor(hn[:, t, :], hn[:, t, :], fg, ALU.mult).then_inc(out_ready, 1)

        @block.gpsimd
        def _(pool):
            GP = nc.gpsimd
            steps = Signal(pool_step)
            cnt = {}

            def link(ins):
                pool.wait_ge(pool_step, steps.by(ins))

            def note(sema, k):
                cnt[id(sema)] = cnt.get(id(sema), 0) + k
                pool.wait_ge(sema, cnt[id(sema)])

            def load_bc(l):
                for r, name in enumerate(("ssm_b_re", "ssm_b_im")):
                    src = a[name][l].rearrange("(j q) s h -> (q s) j h", q=2)
                    pool.dma_start(braw[:, r, :, :], src).then_inc(bc_loaded, 16)
                for r, name in enumerate(("ssm_c_re", "ssm_c_im")):
                    src = a[name][l].rearrange("(i g) h s -> (g h) i s", i=CT_)
                    pool.dma_start(craw[:, r, :, :], src).then_inc(bc_loaded, 16)

            load_bc(0)
            link(GP.memset(ident[:, :], 0.0))
            link(GP.affine_select(out=ident[:, :], in_=ident[:, :], compare_op=ALU.not_equal, fill=1.0, base=0,
                                  pattern=[[-1, P]], channel_multiplier=1))
            link(GP.memset(ones[:, :], 1.0))
            link(GP.affine_select(out=tri[:, :], in_=ones[:, :], compare_op=ALU.is_gt, fill=0.0, base=0,
                                  pattern=[[1, P]], channel_multiplier=-1))
            link(GP.iota(iota_i, pattern=[[1, P]], base=0, channel_multiplier=0))
            link(GP.tensor_copy(iota[:, :], iota_i))
            link(GP.memset(blkm[:, :], 1.0))
            link(GP.affine_select(out=blkm[:, :], in_=blkm[:, :], compare_op=ALU.is_ge, fill=0.0, base=0,
                                  pattern=[[-GH, 8]], channel_multiplier=1))
            link(GP.affine_select(out=blkm[:, :], in_=blkm[:, :], compare_op=ALU.is_ge, fill=0.0, base=GH - 1,
                                  pattern=[[GH, 8]], channel_multiplier=-1))
            link(GP.memset(neg_half[:, :], -0.5))
            GP.sem_inc(consts_ready, 1)

            def rms(src, dst, ready, done):
                for t in range(TT):
                    note(ready, 1)
                    link(GP.tensor_scalar(dst[:, t:t + 1], src[:, t:t + 1], 1.0 / D, RMS_EPS, ALU.mult, ALU.add))
                    GP.tensor_tensor(dst[:, t:t + 1], dst[:, t:t + 1], neg_half[:, 0:1], ALU.pow).then_inc(done, 1)

            def h_rms():
                rms(ssq, rstd, ssq_ready, rstd_ready)

            h_rms()
            rms(mssq, mrstd, mssq_ready, mrstd_ready)
            note(trig_seed, 1)
            for i in (2, 3):
                trig(GP, link, 0, i, ptmp, w2, 1)
                GP.sem_inc(trig_pool, 1)
            for l in range(L):
                if l > 0:
                    h_rms()
                for p in range(PAIRS):
                    note(rot_in, 4)
                    GP.tensor_tensor(rin[:, 0, :], tp[:, 0, :], tp[:, 1, :], ALU.add).then_inc(rin_ready, 1)
                    GP.tensor_tensor(rin[:, 1, :], tp[:, 2, :], tp[:, 3, :], ALU.subtract).then_inc(rin_ready, 1)
                    note(rot_out, 4)
                    q = l * PAIRS + p
                    if q >= 2:
                        pool.wait_ge(y_done, q - 1)
                    GP.tensor_tensor(hst[:, p % 2, 0, :], tp[:, 0, :], tp[:, 1, :], ALU.subtract).then_inc(hst_ready, 1)
                    GP.tensor_tensor(hst[:, p % 2, 1, :], tp[:, 2, :], tp[:, 3, :], ALU.add).then_inc(hst_ready, 1)
                note(var_ready, 1)
                GP.tensor_tensor(tp[:, 2, T:2 * T], tp[:, 2, 0:T], neg_half[:, :], ALU.pow).then_inc(lnr_ready, 1)
                if l == 0:
                    note(bc_used, 1)
                    load_bc(1)
                h_rms()
                h_rms()
                if l == 0:
                    for i in range(4):
                        trig(GP, link, 1, i, ptmp, w2, 1)
                        GP.sem_inc(trig_pool, 1)
            pool.dma_start(rw, a["router_w"][0].rearrange("(k p) n -> p k n", p=P)).then_inc(late_loaded, 16)
            pool.dma_start(rb, a["router_b"][0:1, :].to_broadcast([P, NE])).then_inc(late_loaded, 16)
            pool.dma_start(fg, a["final_norm_g"].unsqueeze(0).to_broadcast([P, D])).then_inc(late_loaded, 16)
            h_rms()


_INS = ["x", "mem", "mem_norm_g", "norm_mix_g", "w_in", "conv_w", "conv_b", "conv_ln_g", "conv_ln_b", "w_conv_pw",
        "ssm_lambda_re", "ssm_lambda_im", "ssm_log_dt", "ssm_b_re", "ssm_b_im", "ssm_c_re", "ssm_c_im", "ssm_d",
        "w_ssm_glu", "w_out", "norm_xattn_g", "w_q", "w_kv", "w_o", "norm_ffn_g", "ffn_w_gate_up", "ffn_w_down",
        "router_w", "router_b", "moe_w_gate_up", "moe_w_down", "final_norm_g"]


def kernel(**inputs):
    import numpy as np
    import concourse.bacc as bacc
    from concourse.bass_utils import run_bass_kernel_spmd

    nc = bacc.Bacc("TRN2", target_bir_lowering=False, num_devices=1)
    arrays, aps = {}, {}
    for name in _INS:
        x = np.ascontiguousarray(inputs[name])
        arrays[f"in_{name}"] = x
        aps[name] = nc.dram_tensor(f"in_{name}", x.shape, mybir.dt.from_np(x.dtype), kind="ExternalInput").ap()
    out = nc.dram_tensor("out_dram", (1, T, D), F32, kind="ExternalOutput").ap()
    trunk_kernel(nc, aps, out)
    r = run_bass_kernel_spmd(nc, [arrays], core_ids=[0])
    return r.results[0]["out_dram"]
```

```python
import math
from contextlib import ExitStack

import concourse.bass as bass
from concourse import mybir

F32 = mybir.dt.float32
F32R = mybir.dt.float32r
I32 = mybir.dt.int32
U32 = mybir.dt.uint32
ALU = mybir.AluOpType
ACT = mybir.ActivationFunctionType
AX_X = mybir.AxisListType.X

P = 128
T = 256
TT = T // P
D = 1024
KD = D // P
L = 2
CW = 512
CT_ = CW // P
TAPS = 31
PAD = TAPS - 1
G = 32
GH = 16
NS = 64
ST = G * NS // P
PAIRS = ST // 2
H = 4
HD = D // H
FF = 2816
FE = 3584
NE = 8
BLK = 512
CHUNK = 2048
HALF = CHUNK // 2
RAW = 3
RAW_E = 6
SPLITS = 3
AHEAD = 2
RING_BANKS = 6
C0 = 2 * CW
C1 = C0 + G * GH
RMS_EPS = 1e-6
LN_EPS = 1e-5
FBLK = FF // 256
EBLK = FE // 256
FT = FF // P
ET = FE // P
MAGIC = 12582912.0
TWO_PI_A = 6.28125
TWO_PI_B = 0.0019350051879882812
TWO_PI_C = 2 * math.pi - TWO_PI_A - TWO_PI_B
PI_BELOW = 3.1415925

ROW_MIX, ROW_X, ROW_FFN, ROW_CB, ROW_LG, ROW_LB, ROW_D, ROW_MEM = 0, 8, 16, 24, 28, 32, 36, 40
ROW_LR, ROW_LI, ROW_DT = 48, 64, 96
ROWS = 112


SMALL = ["ldt", "lr", "li", "dt", "lrdt", "lidt", "mag", "ang", "aabs", "s1", "c1", "ar", "ai", "xr", "den",
         "rden", "kr", "ki", "t1", "t2", "rnd", "c128", "s128"]


class Plan:

    def __init__(self, first=0, first_part=0):
        self.first, self.part = first, first_part
        self.names, self.chunks, self.bound = [], [], {}

    def add(self, names, chunks=()):
        self.names += names
        for i, (src, split, low) in enumerate(chunks):
            if i < len(chunks) - 1:
                self.part += 1
                done = ("part", self.part)
            else:
                done = ("mm", self.first + len(self.names))
            self.chunks.append((src, split, low, done))
        for name in names:
            self.bound[name] = len(self.chunks)


def tok(kind, l, n, names, w, n0, ktiles, low, split=True):
    return [(kind, l, n, t) for t in range(TT)], [(("a", w, l, n0, c), split, low[c % len(low)])
                                                  for c in range(ktiles // 4)]


def make_plan():
    plan = Plan()
    add = plan.add
    third = ("dve", "pool")
    for l in range(L):
        for i in range(4):
            add([("hT", l, i)])
        for kind, n0 in (("cg", CW), ("ca", 0), ("us", C0)):
            for i in range(2):
                add([(kind, l, i)], [(("c", "w_in", l, n0 + 256 * i), True, "dve")])
        for kind in ("bd", "ct"):
            for r in range(2):
                add([(kind, l, r)])
        if l == 0:
            for i in range(4):
                add([("memT", i)])
        for p in range(PAIRS):
            for s in range(2):
                add([("bu", l, p, s)])
            kind, n = FILLERS[p]
            if kind == "k":
                for i in range(2):
                    add([("k", l, n, i)], [(("c", "w_kv", l, BLK * n + 256 * i), False, None)])
            elif kind == "v":
                add([("v", l, n, t) for t in range(TT)], [(("a", "w_kv", l, D + BLK * n, c), False, None) for c in range(2)])
            else:
                add([("gt", l, n, t) for t in range(TT)],
                    [(("a", "w_in", l, C1 + BLK * n, c), True, "pool") for c in range(2)])
        add([("mean", l)])
        for n in range(2):
            for kind, n0, low in (("zg", D, "dve"), ("za", 0, "pool")):
                if n == 0 and kind == "za":
                    add([("var", l)])
                add([(kind, l, n, t) for t in range(TT)], [(("a", "w_ssm_glu", l, n0 + BLK * n, 0), True, low)])
            if n == 0:
                add([("rs", l)])
        for n in range(2):
            add([("ya", l, n, t) for t in range(TT)], [(("a", "w_conv_pw", l, BLK * n, 0), True, "pool")])
        for i in range(4):
            add([("mT", l, i)])
        for n in range(2):
            add([("out", l, n, t) for t in range(TT)],
                [(("a", "w_out", l, BLK * n, c), True, third[c]) for c in range(2)])
        for i in range(4):
            add([("hT2", l, i)])
        for n in range(2):
            for i in range(2):
                add([("q", l, n, i)], [(("c", "w_q", l, BLK * n + 256 * i), True, third[i])])
        for h in range(H + 1):
            if h < H:
                add([("sc", l, h)])
            if h >= 1:
                add([("pT", l, h - 1)])
                add([("oT", l, h - 1)])
        for n in range(2):
            add([("o", l, n, t) for t in range(TT)], [(("a", "w_o", l, BLK * n, c), True, third[c]) for c in range(2)])
        for i in range(4):
            add([("hT3", l, i)])
        if l == 0:
            for b in range(FBLK + 1):
                if b < FBLK:
                    add([("fgu", b, t) for t in range(TT)], [(("fgu", b, c), True, "dve") for c in range(2)])
                if b >= 1:
                    add([("fT", b - 1)])
                if b in FPIECE_END:
                    k = FPIECE_END.index(b)
                    lo = FPIECE_END[k - 1] if k else 0
                    add([("fdn", k, t, n) for t in range(TT) for n in range(2)],
                        [(("fdn", c), True, "dve") for c in range(lo, b)])
    add([("rt",)])
    add([("pos",)])
    loop = Plan(len(plan.names), plan.part)
    add = loop.add

    def gu(b):
        add([("gu", b)], [(("egu", b, c), True, None) for c in range(2) for _ in range(2)])

    def down(k):
        lo, hi = EPIECES[k]
        add([("edn", k, n) for n in range(2)], [(("edn", c), True, None) for c in range(lo, hi) for _ in range(2)])

    gu(0)
    for b in range(1, EBLK):
        gu(b)
        if b % 2 == 0:
            add([("eT", b // 2 - 1)])
            if 2 * (b // 2) == EPIECES[0][1]:
                down(0)
    add([("eT", EBLK // 2 - 1)])
    add([("gT",)])
    down(1)
    for t in range(TT):
        for n in range(2):
            add([("add", t, n)])
    return plan, loop


FILLERS = [("v", 0), ("v", 1), ("gt", 0), ("gt", 1), ("k", 0), ("k", 1), ("gt", 2), ("gt", 3)]
FPIECE_END = (4, 8, 11)
EPIECES = ((0, 8), (8, 14))
TRUNK, EXPERT = make_plan()
PLAN, LOOP = TRUNK.names, EXPERT.names
AT = {name: i for i, name in enumerate(PLAN)}
LAT = {name: len(PLAN) + j for j, name in enumerate(LOOP)}
PER = len(LOOP)
PPER = EXPERT.part - TRUNK.part
assert PER % RING_BANKS == 0
CHUNKS, ECHUNKS = TRUNK.chunks, EXPERT.chunks
EH = len(ECHUNKS)
EC = EH // 2
HSLOTS = 2 * SPLITS
AHEAD_H = 4
assert EC % RAW_E == 0 and EH % HSLOTS == 0
ELOW = ["pool" if u // 2 % 4 == 3 else "dve" for u in range(EH)]
SPLIT_AT = [n for n, ch in enumerate(CHUNKS) if ch[1]]
LOW_COUNT = {}
for _who in ("dve", "pool"):
    for _k, _n in enumerate([n for n in SPLIT_AT if CHUNKS[n][2] == _who]):
        LOW_COUNT[_n] = _k + 1
LOW_TOTAL = {who: sum(1 for n in SPLIT_AT if CHUNKS[n][2] == who) for who in ("dve", "pool")}
ELOW_PER = {who: ELOW.count(who) for who in ("dve", "pool")}
ELOW_COUNT = [ELOW[:u + 1].count(ELOW[u]) for u in range(EH)]


def splits_before(n):
    return sum(1 for k in SPLIT_AT if k < n)


class Signal:

    def __init__(self, sem):
        self.sem, self.n = sem, 0

    def by(self, ins, k=1):
        ins.then_inc(self.sem, k)
        self.n += k
        return self.n


def trunk_kernel(nc, a, out):
    with ExitStack() as ctx:
        def sb(name, shape, dt=F32):
            return ctx.enter_context(nc.sbuf_tensor(name, shape, dt))

        def sem(name):
            return ctx.enter_context(nc.semaphore(name))

        ring = sb("ring", [P, RAW, CHUNK])
        w_hi = sb("w_hi", [P, SPLITS, CHUNK], F32R)
        w_lo = sb("w_lo", [P, SPLITS, CHUNK], F32R)
        x_hi = sb("x_hi", [P, KD, T], F32R)
        x_lo = sb("x_lo", [P, KD, T], F32R)
        a_hi = sb("a_hi", [P, KD, T], F32R)
        a_lo = sb("a_lo", [P, KD, T], F32R)
        h = sb("h", [P, TT, D])
        hn = sb("hn", [P, TT, D])
        memT = sb("memT", [P, KD, T])
        v = sb("v", [P, TT, D])
        trigT = sb("trigT", [P, 2, 2, ST // 2, P])
        kT = trigT[:, 0, :, :, :].rearrange("p a j n -> p (a j n)").rearrange("p (k n) -> p k n", k=KD)
        ident = sb("ident", [P, P])
        ones = sb("ones", [P, P])
        neg_half = sb("neg_half", [P, 1])
        half_pi = sb("half_pi", [P, 1])
        cols = sb("cols", [P, L, P])
        taps = sb("taps", [P, L, TAPS * CT_])
        ptmp = sb("ptmp", [P, 2, 4, P // 2])
        bnd = sb("bnd", [P, 6, 2])
        sm = sb("sm", [P, len(SMALL), L * ST])
        w2 = sb("w2", [P, 2, 4, 4])
        blkm = sb("blkm", [P, 8])
        evod = sb("evod", [P, 2])
        ssq = sb("ssq", [P, TT])
        rstd = sb("rstd", [P, TT])
        mssq = sb("mssq", [P, TT])
        mrstd = sb("mrstd", [P, TT])
        smx = sb("smx", [P, H, TT])
        snb = sb("snb", [P, H, TT])
        ssum = sb("ssum", [P, H, TT])
        srec = sb("srec", [P, H, TT])
        dtq = sb("dtq", [P, L, 2])
        ARENA = 11400
        arena = sb("arena", [P, ARENA])

        class Area:

            def __init__(self):
                self.at = 0

            def cut(self, n):
                self.at += n
                assert self.at <= ARENA, self.at
                return arena[:, self.at - n:self.at]

        mx = Area()
        gates = mx.cut(TT * 2 * D).rearrange("p (t n) -> p t n", t=TT)
        upad = mx.cut(CT_ * (PAD + T)).rearrange("p (c n) -> p c n", c=CT_)
        conv = mx.cut(CT_ * T).rearrange("p (c n) -> p c n", c=CT_)
        tp = mx.cut(4 * 512).rearrange("p (i n) -> p i n", i=4)
        bdT = mx.cut(2 * CT_ * P).rearrange("p (r i n) -> p r i n", r=2, i=CT_)
        bc = mx.cut(2 * CT_ * P)
        cT = bc.rearrange("p (r i n) -> p r i n", r=2, i=CT_)
        hst = mx.cut(2 * 512).rearrange("p (i n) -> p i n", i=2)
        us = hn[:, 0, :].rearrange("p (c n) -> p c n", c=CT_)
        yT = hn[:, 1, :].rearrange("p (c n) -> p c n", c=CT_)
        braw = bc[:, 0:512].rearrange("p (r j h) -> p r j h", r=2, j=ST)
        craw = bc[:, 512:1024].rearrange("p (r i n) -> p r i n", r=2, i=CT_)
        tg = hst
        y_hi, y_lo = a_hi[:, 0:CT_, :], a_lo[:, 0:CT_, :]
        u_hi, u_lo = a_hi[:, CT_:KD, :], a_lo[:, CT_:KD, :]
        bd = gates[:, 0, 0:1024].rearrange("p (r j q h) -> p r j q h", r=2, j=ST, q=2)
        xc = gates[:, 0, 1024:2048].rearrange("p (m q n) -> p m q n", m=8, q=2)
        bt = gates[:, 1, 0:512].rearrange("p (i j h) -> p i j h", i=2, j=ST)
        merged = hn

        xa = Area()
        qT = xa.cut(KD * T).rearrange("p (k n) -> p k n", k=KD)
        prob = xa.cut(H * TT * T).rearrange("p (h t n) -> p h t n", h=H, t=TT)
        pT = xa.cut(H * TT * T).rearrange("p (h m n) -> p h m n", h=H, m=TT)

        fa = Area()
        sil = fa.cut(4 * 256).rearrange("p (b n) -> p b n", b=4)
        h1 = fa.cut(4 * 256).rearrange("p (b n) -> p b n", b=4)
        tri = fa.cut(P)
        iota = fa.cut(P)
        iota_i = fa.cut(P).bitcast(I32)
        xTf = fa.cut(KD * T).rearrange("p (k n) -> p k n", k=KD)
        fgain = fa.cut(D)
        xg_hi = x_hi[:, 0:KD // 2, :].rearrange("p k (a n) -> p (k a) n", a=2)
        xg_lo = x_lo[:, 0:KD // 2, :].rearrange("p k (a n) -> p (k a) n", a=2)
        e_hi = a_hi[:, :, :].rearrange("p k (a n) -> p (k a) n", a=2)
        e_lo = a_lo[:, :, :].rearrange("p k (a n) -> p (k a) n", a=2)
        pick = fa.cut(TT * P).rearrange("p (t n) -> p t n", t=TT)
        pickg = fa.cut(TT * P).rearrange("p (t n) -> p t n", t=TT)
        gT = fa.cut(TT * P).rearrange("p (t n) -> p t n", t=TT)
        ye = fa.cut(D)
        rw = fa.cut(KD * NE).rearrange("p (k n) -> p k n", k=KD)
        rb = fa.cut(NE)
        lg = fa.cut(TT * NE).rearrange("p (t n) -> p t n", t=TT)
        top = fa.cut(TT * 8).rearrange("p (t n) -> p t n", t=TT)
        topi = fa.cut(TT * 8).rearrange("p (t n) -> p t n", t=TT)
        oneh = fa.cut(2 * TT * NE).rearrange("p (i t n) -> p i t n", i=2, t=TT)
        tw = fa.cut(4 * TT).rearrange("p (i t) -> p i t", i=4)
        mask = fa.cut(TT * 17).rearrange("p (t n) -> p t n", t=TT)
        gate = fa.cut(TT * 17).rearrange("p (t n) -> p t n", t=TT)
        slot = fa.cut(TT * 17).rearrange("p (t n) -> p t n", t=TT)
        fg = fa.cut(D)
        tot = fa.cut(2)
        topu = sb("topu", [P, TT, 8], U32)
        over = sb("over", [P, 1], I32)
        prow = arena[:, 0:L * 2 * P].rearrange("p (l m n) -> p l m n", l=L, m=2)
        mem = v[:, :, :]
        raw_e = [ring[:, i, :] for i in range(RAW)] + [memT[:, :, :].rearrange("p k n -> p (k n)"),
                                                       v[:, :, :].rearrange("p t n -> p (t n)"),
                                                       kT.rearrange("p k n -> p (k n)")]

        ps = ctx.enter_context(nc.psum_tensor("ps", [P, 8, 512], F32))

        def bank(i):
            return ps[:, i % RING_BANKS, :]

        raw_loaded = [sem(f"raw_loaded{i}") for i in range(RAW)]
        e_loaded = [sem(f"e_loaded{i}") for i in range(RAW_E)]
        part_done = sem("part_done")
        hi_done = sem("hi_done")
        low_done = {"dve": sem("low_done_dve"), "pool": sem("low_done_pool")}
        mm_done = sem("mm_done")
        bank_free = [sem(f"bank_free{i}") for i in range(RING_BANKS)]
        x_loaded = sem("x_loaded")
        mem_loaded = sem("mem_loaded")
        rows_loaded = sem("rows_loaded")
        bc_loaded = sem("bc_loaded")
        late_loaded = sem("late_loaded")
        rows_cleared = sem("rows_cleared")
        consts_ready = sem("consts_ready")
        rows_ready = sem("rows_ready")
        par_done = sem("par_done")
        cols_ready = sem("cols_ready")
        ssm_act = sem("ssm_act")
        ssm_arg = sem("ssm_arg")
        trig_seed = sem("trig_seed")
        trig_pool = sem("trig_pool")
        trig_dve = sem("trig_dve")
        bc_used = sem("bc_used")
        bd_ready = sem("bd_ready")
        bdT_ready = sem("bdT_ready")
        cT_ready = sem("cT_ready")
        h_ready = sem("h_ready")
        ssq_ready = sem("ssq_ready")
        rstd_ready = sem("rstd_ready")
        hn_ready = sem("hn_ready")
        mssq_ready = sem("mssq_ready")
        mrstd_ready = sem("mrstd_ready")
        mn_ready = sem("mn_ready")
        x_hi_ready = sem("x_hi_ready")
        x_lo_ready = sem("x_lo_ready")
        memT_act = sem("memT_act")
        memT_dve = sem("memT_dve")
        tanh_ready = sem("tanh_ready")
        tanh_used = sem("tanh_used")
        us_ready = sem("us_ready")
        gates_ready = sem("gates_ready")
        kv_ready = sem("kv_ready")
        rot_in = sem("rot_in")
        rin_ready = sem("rin_ready")
        gelu_ready = sem("gelu_ready")
        y_hi_ready = sem("y_hi_ready")
        y_lo_ready = sem("y_lo_ready")
        u32_ready = sem("u32_ready")
        u_hi_ready = sem("u_hi_ready")
        u_lo_ready = sem("u_lo_ready")
        xTf_ready = sem("xTf_ready")
        late_consts = sem("late_consts")
        ga_done = sem("ga_done")
        ga_read = sem("ga_read")
        xg_hi_ready = sem("xg_hi_ready")
        xg_lo_ready = sem("xg_lo_ready")
        a_hi_ready = sem("a_hi_ready")
        a_lo_ready = sem("a_lo_ready")
        rot_out = sem("rot_out")
        hst_ready = sem("hst_ready")
        y_done = sem("y_done")
        y_read = sem("y_read")
        ypre_ready = sem("ypre_ready")
        conv_step = sem("conv_step")
        conv_ready = sem("conv_ready")
        xc_ready = sem("xc_ready")
        sq_ready = sem("sq_ready")
        var_ready = sem("var_ready")
        pow_ready = sem("pow_ready")
        lnr_ready = sem("lnr_ready")
        lnz_ready = sem("lnz_ready")
        lnt_ready = sem("lnt_ready")
        merged_ready = sem("merged_ready")
        q_ready = sem("q_ready")
        nb_ready = sem("nb_ready")
        exp_ready = sem("exp_ready")
        prob_ready = sem("prob_ready")
        pT_ready = sem("pT_ready")
        sil_ready = sem("sil_ready")
        h1_ready = sem("h1_ready")
        topd_ready = sem("topd_ready")
        tope_ready = sem("tope_ready")
        mask_ready = sem("mask_ready")
        over_ready = sem("over_ready")
        pick_ready = sem("pick_ready")
        pickg_ready = sem("pickg_ready")
        gT_ready = sem("gT_ready")
        ye_ready = sem("ye_ready")
        out_ready = sem("out_ready")
        out_stored = sem("out_stored")
        dve_step = sem("dve_step")
        pool_step = sem("pool_step")
        act_step = sem("act_step")

        block = ctx.enter_context(nc.Block())

        def wait_bank(eng, i):
            if i >= RING_BANKS:
                eng.wait_ge(bank_free[i % RING_BANKS], i // RING_BANKS)

        def freed(ins, i):
            ins.then_inc(bank_free[i % RING_BANKS], 1)

        def y_skip(dve, link, note, l, i):
            V = nc.vector
            u = l * CT_ + i
            dve.wait_ge(y_done, l * PAIRS + 2 * i + 2)
            link(V.scalar_tensor_tensor(yT[:, i, :], us[:, i, :], cols[:, l, ROW_D + i:ROW_D + i + 1],
                                        ps[:, 6 + u % 2, 0:T], ALU.mult, ALU.add))
            V.sem_inc(y_read, 1)
            V.sem_inc(ypre_ready, 1)

        def residual(kind, l, dve, note, result, link, free_bank):
            V = nc.vector
            for n_ in range(2):
                for t in range(TT):
                    n = (kind, l, n_, t)
                    o = result(n)
                    dst = h[:, t, n_ * BLK:(n_ + 1) * BLK]
                    link(V.tensor_tensor(dst, dst, o, ALU.add))
                    free_bank(n)
                    if n_ == 1:
                        V.sem_inc(h_ready, 1)

        def trig(E, link, l, i, tmp, mul, m):
            S = {name: sm[:, k, :] for k, name in enumerate(SMALL)}
            jj = slice(4 * (i % 2), 4 * (i % 2) + 4)
            c, s = trigT[:, i // 2, 0, jj, :], trigT[:, i // 2, 1, jj, :]
            js = slice(l * ST + 4 * i, l * ST + 4 * i + 4)
            c1, s1, c128, s128 = (S[n][:, js].unsqueeze(2) for n in ("c1", "s1", "c128", "s128"))
            A, B = tmp
            link(E.memset(c[:, :, 0:1], 1.0))
            link(E.memset(s[:, :, 0:1], 0.0))
            link(E.tensor_copy(c[:, :, 1:2], c1))
            link(E.tensor_copy(s[:, :, 1:2], s1))
            n = 2
            while n <= P:
                ch, sh = c[:, :, n // 2:n // 2 + 1], s[:, :, n // 2:n // 2 + 1]
                wc, ws, x, y = (mul[:, m, k, :].unsqueeze(2) for k in range(4))
                if n == P:
                    wc, ws = c128, s128
                link(E.tensor_tensor(x, ch, ch, ALU.mult))
                link(E.tensor_tensor(y, sh, sh, ALU.mult))
                link(E.tensor_tensor(wc, x, y, ALU.subtract))
                link(E.tensor_tensor(x, ch, sh, ALU.mult))
                link(E.tensor_tensor(ws, x, x, ALU.add))
                if n < P:
                    a_ = A[:, 0:4 * n].rearrange("p (j n) -> p j n", j=4)
                    b_ = B[:, 0:4 * n].rearrange("p (j n) -> p j n", j=4)
                    wcb, wsb = wc.to_broadcast([P, 4, n]), ws.to_broadcast([P, 4, n])
                    link(E.tensor_tensor(a_, c[:, :, 0:n], wcb, ALU.mult))
                    link(E.tensor_tensor(b_, s[:, :, 0:n], wsb, ALU.mult))
                    link(E.tensor_tensor(c[:, :, n:2 * n], a_, b_, ALU.subtract))
                    link(E.tensor_tensor(a_, c[:, :, 0:n], wsb, ALU.mult))
                    link(E.tensor_tensor(b_, s[:, :, 0:n], wcb, ALU.mult))
                    link(E.tensor_tensor(s[:, :, n:2 * n], a_, b_, ALU.add))
                n *= 2

        def source(src, e=None):
            def tiles(w):
                return w.rearrange("(k p) n -> p k n", p=P)

            kind = src[0]
            if kind == "a":
                _, name, l, n0, c = src
                return 4, [(0, tiles(a[name][l])[:, 4 * c:4 * c + 4, n0:n0 + BLK])]
            if kind == "c":
                _, name, l, n0 = src
                return 8, [(0, tiles(a[name][l])[:, :, n0:n0 + 256])]
            if kind in ("fgu", "egu"):
                _, b, c = src
                w, f = (a["ffn_w_gate_up"][0], FF) if kind == "fgu" else (a["moe_w_gate_up"][0, e], FE)
                return 4, [(256 * g, tiles(w)[:, 4 * c:4 * c + 4, g * f + 256 * b:g * f + 256 * b + 256])
                           for g in range(2)]
            c = src[1]
            w = a["ffn_w_down"][0] if kind == "fdn" else a["moe_w_down"][0, e]
            return 2, [(0, tiles(w)[:, 2 * c:2 * c + 2, :])]

        half_hi = w_hi[:, :, :].rearrange("p s (a n) -> p (s a) n", a=2)
        half_lo = w_lo[:, :, :].rearrange("p s (a n) -> p (s a) n", a=2)

        def load(eng, slot, sema, k, parts):
            view = slot.rearrange("p (k n) -> p k n", k=k)
            for c0, src in parts:
                eng.dma_start(view[:, :, c0:c0 + src.shape[2]], src).then_inc(sema, 32 // len(parts))

        def done_wait(eng, done):
            eng.wait_ge(part_done if done[0] == "part" else mm_done, done[1])

        def e_done_wait(eng, it, u):
            kind, n = ECHUNKS[u % EH][3]
            per = PPER if kind == "part" else PER
            eng.wait_ge(part_done if kind == "part" else mm_done, it * per + (n - (per if u < 0 else 0)))

        def low_wait(eng, n):
            eng.wait_ge(low_done[CHUNKS[n][2]], LOW_COUNT[n])

        def e_low_wait(eng, it, u):
            who = ELOW[u % EH]
            n = LOW_TOTAL[who] + ELOW_COUNT[u % EH] - (ELOW_PER[who] if u < 0 else 0)
            eng.wait_ge(low_done[who], it * ELOW_PER[who] + n)

        class Splitter:

            def __init__(self, eng, who):
                self.eng, self.who, self.m = eng, who, 0

            def to(self, m_end):
                while self.m < min(m_end, len(SPLIT_AT)):
                    m, n = self.m, SPLIT_AT[self.m]
                    self.m += 1
                    if self.who == "hi":
                        if m >= SPLITS:
                            done_wait(self.eng, CHUNKS[SPLIT_AT[m - SPLITS]][3])
                        self.eng.wait_ge(raw_loaded[n % RAW], 32 * (n // RAW + 1))
                        self.eng.activation(w_hi[:, m % SPLITS, :], ring[:, n % RAW, :], ACT.Copy).then_inc(hi_done, 1)
                    elif CHUNKS[n][2] == self.who:
                        self.eng.wait_ge(hi_done, m + 1)
                        self.eng.tensor_tensor(w_lo[:, m % SPLITS, :], ring[:, n % RAW, :],
                                               w_hi[:, m % SPLITS, :].bitcast(F32),
                                               ALU.subtract).then_inc(low_done[self.who], 1)

            def upto(self, name):
                self.to(splits_before(TRUNK.bound[name] + AHEAD))

            def expert(self, it, u):
                i2, u = it + (1 if u >= EH else 0), u % EH
                c, k = divmod(u, 2)
                src = raw_e[c % RAW_E][:, k * HALF:(k + 1) * HALF]
                hi, lo = half_hi[:, u % HSLOTS, :], half_lo[:, u % HSLOTS, :]
                if self.who == "hi":
                    e_done_wait(self.eng, i2, u - HSLOTS)
                    if k == 0:
                        self.eng.wait_ge(e_loaded[c % RAW_E], i2 * (32 * EC // RAW_E) + 32 * (c // RAW_E + 1))
                    self.eng.activation(hi, src, ACT.Copy).then_inc(hi_done, 1)
                elif ELOW[u] == self.who:
                    self.eng.wait_ge(hi_done, i2 * EH + (len(SPLIT_AT) + u + 1))
                    self.eng.tensor_tensor(lo, src, hi.bitcast(F32), ALU.subtract).then_inc(low_done[self.who], 1)

            def first_experts(self):
                for u in range(HSLOTS):
                    c, k = divmod(u, 2)
                    if self.who == "hi":
                        if k == 0:
                            done_wait(self.eng, CHUNKS[SPLIT_AT[len(SPLIT_AT) - SPLITS + c]][3])
                            self.eng.wait_ge(e_loaded[c], 32)
                        self.eng.activation(half_hi[:, u, :], raw_e[c][:, k * HALF:(k + 1) * HALF],
                                            ACT.Copy).then_inc(hi_done, 1)
                    else:
                        self.expert(0, u)

        @block.sync
        def _(sp):
            for n, (src, split, _, _) in enumerate(CHUNKS):
                if n >= RAW:
                    before = CHUNKS[n - RAW]
                    if before[1]:
                        low_wait(sp, n - RAW)
                    else:
                        done_wait(sp, before[3])
                load(sp, ring[:, n % RAW, :], raw_loaded[n % RAW], *source(src))

            def expert_chunk(e, it, c):
                e_low_wait(sp, it, 2 * (c - RAW_E) + 1)
                load(sp, raw_e[c % RAW_E], e_loaded[c % RAW_E], *source(ECHUNKS[2 * c][0], e))

            def all_experts(it0):
                with sp.Fori(0, NE - 1) as e:
                    for c in range(SPLITS, EC):
                        expert_chunk(e, e + it0, c)
                    for c in range(SPLITS):
                        expert_chunk(e + 1, e + (it0 + 1), c)
                for c in range(SPLITS, EC):
                    expert_chunk(NE - 1, NE - 1 + it0, c)
                for c in range(SPLITS):
                    expert_chunk(0, NE + it0, c)

            for n in range(len(CHUNKS) - RAW, len(CHUNKS)):
                low_wait(sp, n)
            sp.wait_ge(mm_done, AT[("oT", L - 1, H - 1)] + 1)
            for c in range(SPLITS):
                expert_chunk(0, 0, c)
            all_experts(0)
            sp.wait_ge(over_ready, 1)
            most = sp.value_load(over[0:1, 0:1], min_val=0, max_val=T)
            with sp.If(most > P):
                all_experts(NE)
            for t in range(TT):
                sp.wait_ge(out_ready, t + 1)
                sp.dma_start(out[0, t * P:(t + 1) * P, :], hn[:, t, :]).then_inc(out_stored, 16)
            sp.wait_ge(out_stored, 16 * TT)

        @block.tensor
        def _(pe):
            task = [0]
            chunk = [0]
            sig = {}

            def need(sema, k):
                sig[id(sema)] = sig.get(id(sema), 0) + k
                pe.wait_ge(sema, sig[id(sema)])

            def begin(name):
                assert PLAN[task[0]] == name, (PLAN[task[0]], name)
                wait_bank(pe, task[0])
                task[0] += 1
                return bank(task[0] - 1)

            def end(ins):
                ins.then_inc(mm_done, 1)

            def three(o, hi, lo, w_h, w_l, start, stop, weights_move=True):
                if weights_move:
                    pe.matmul(o, hi, w_h, start=start, stop=False)
                    pe.matmul(o, hi, w_l, start=False, stop=False)
                    return pe.matmul(o, lo, w_h, start=False, stop=stop)
                pe.matmul(o, w_h, hi, start=start, stop=False)
                pe.matmul(o, w_h, lo, start=False, stop=False)
                return pe.matmul(o, w_l, hi, start=False, stop=stop)

            def next_chunk():
                n = chunk[0]
                chunk[0] += 1
                _, split, _, done = CHUNKS[n]
                if split:
                    low_wait(pe, n)
                    m = splits_before(n)
                    return w_hi[:, m % SPLITS, :], w_lo[:, m % SPLITS, :], done
                pe.wait_ge(raw_loaded[n % RAW], 32 * (n // RAW + 1))
                return ring[:, n % RAW, :], None, done

            def token_major(names, hi, lo, ktiles):
                os = [begin(name) for name in names]
                for c in range(ktiles // 4):
                    w_h, w_l, done = next_chunk()
                    for k in range(4):
                        kk = 4 * c + k
                        cols_ = slice(k * BLK, (k + 1) * BLK)
                        for t in range(TT):
                            tok_ = slice(t * P, (t + 1) * P)
                            start, stop = kk == 0, kk == ktiles - 1
                            if lo is None:
                                ins = pe.matmul(os[t], hi[:, kk, tok_], w_h[:, cols_], start=start, stop=stop)
                            else:
                                ins = three(os[t], hi[:, kk, tok_], lo[:, kk, tok_], w_h[:, cols_], w_l[:, cols_],
                                            start, stop)
                            if stop:
                                end(ins)
                    if done[0] == "part":
                        ins.then_inc(part_done, 1)

            def channel_major(names, hi, lo):
                for name in names:
                    o = begin(name)
                    w_h, w_l, done = next_chunk()
                    for j in range(2):
                        for k in range(KD):
                            w = slice(k * 256 + j * P, k * 256 + (j + 1) * P)
                            oo = o[:, j * T:(j + 1) * T]
                            if lo is None:
                                ins = pe.matmul(oo, w_h[:, w], hi[:, k, :], start=(k == 0), stop=(k == KD - 1))
                            else:
                                ins = three(oo, hi[:, k, :], lo[:, k, :], w_h[:, w], w_l[:, w], k == 0, k == KD - 1,
                                            weights_move=False)
                    end(ins)

            def transposes(names, src, ready):
                for i, name in enumerate(names):
                    o = begin(name)
                    for t in range(TT):
                        if i == 0:
                            need(ready, 1)
                        for j in range(2):
                            ins = pe.transpose(o[:, j * T + t * P:j * T + (t + 1) * P],
                                               src[:, t, (2 * i + j) * P:(2 * i + j + 1) * P], ident[:, :])
                    end(ins)

            pe.wait_ge(consts_ready, 1)
            pe.wait_ge(rows_ready, 1)
            o = ps[:, 6, :]
            for l in range(L):
                pe.transpose(o[:, l * P:l * P + ROWS], prow[0:ROWS, l, 0, :], ident[0:ROWS, 0:ROWS])
                ins = pe.transpose(o[:, (2 + l) * P:(2 + l) * P + TAPS * CT_], prow[0:TAPS * CT_, l, 1, :],
                                   ident[0:TAPS * CT_, 0:TAPS * CT_])
            ins.then_inc(par_done, 1)

            for l in range(L):
                transposes([("hT", l, i) for i in range(4)], hn, hn_ready)
                need(x_lo_ready, 4)
                for kind in ("cg", "ca", "us"):
                    channel_major([(kind, l, i) for i in range(2)], x_hi, x_lo)
                need(bd_ready, 2)
                for r in range(2):
                    o = begin(("bd", l, r))
                    for i in range(CT_):
                        ins = pe.transpose(o[:, i * P:(i + 1) * P],
                                           bd[:, r, 4 * i:4 * i + 4, :, :].rearrange("p j q h -> p (j q h)"), ident[:, :])
                    end(ins)
                for r in range(2):
                    o = begin(("ct", l, r))
                    for i in range(CT_):
                        ins = pe.transpose(o[:, i * P:(i + 1) * P],
                                           xc[:, 4 * r + i, :, :].rearrange("p q n -> p (q n)"), ident[:, :])
                    end(ins)
                if l == 0:
                    transposes([("memT", i) for i in range(4)], mem, mn_ready)

                def y_pair(p):
                    i = p // 2
                    u = l * CT_ + i
                    if p % 2 == 0 and u >= 2:
                        pe.wait_ge(y_read, u - 1)
                    if p == 0:
                        need(cT_ready, 2)
                    need(hst_ready, 2)
                    for s in range(2):
                        jj = (2 * p + s) % 4
                        for r in range(2):
                            ins = pe.matmul(ps[32 * jj:32 * jj + 32, 6 + u % 2, 0:T], cT[:, r, i, 32 * jj:32 * jj + 32],
                                            hst[:, r, s * T:(s + 1) * T], start=(r == 0), stop=(r == 1),
                                            tile_position=(0, 32 * jj))
                    ins.then_inc(y_done, 1)

                need(us_ready, 2)
                need(bdT_ready, 2)
                for p in range(PAIRS):
                    for s in range(2):
                        o = begin(("bu", l, p, s))
                        j = 2 * p + s
                        q0 = 32 * (j % 4)
                        for r in range(2):
                            ins = pe.matmul(o[:, r * T:(r + 1) * T], bdT[q0:q0 + 32, r, j // 4, :],
                                            us[q0:q0 + 32, j // 4, :], start=True, stop=True,
                                            tile_position=(q0, 0))
                        end(ins)
                    kind, n = FILLERS[p]
                    if kind != "gt" and l == 0 and p == 0:
                        need(memT_act, 4)
                        need(memT_dve, 2)
                    if kind == "gt":
                        token_major([("gt", l, n, t) for t in range(TT)], x_hi, x_lo, KD)
                    elif kind == "k":
                        channel_major([("k", l, n, i) for i in range(2)], memT, None)
                    else:
                        token_major([("v", l, n, t) for t in range(TT)], memT, None, KD)
                    if p >= 1:
                        y_pair(p - 1)
                y_pair(PAIRS - 1)

                o = begin(("mean", l))
                need(conv_ready, 1)
                for c in range(CT_):
                    ins = pe.matmul(o[:, 0:T], ones[:, :], conv[:, c, :], start=(c == 0), stop=(c == CT_ - 1))
                end(ins)
                need(y_lo_ready, CT_)
                for n in range(2):
                    token_major([("zg", l, n, t) for t in range(TT)], y_hi, y_lo, CT_)
                    if n == 0:
                        o = begin(("var", l))
                        need(sq_ready, 1)
                        sq = tp[:, 0:2, :].rearrange("p i n -> p (i n)").rearrange("p (c n) -> p c n", c=CT_)
                        for t in range(TT):
                            for c in range(CT_):
                                ins = pe.matmul(o[:, t:t + 1], sq[:, c, t * P:(t + 1) * P], ones[:, 0:1],
                                                start=(c == 0), stop=(c == CT_ - 1))
                        end(ins)
                    token_major([("za", l, n, t) for t in range(TT)], y_hi, y_lo, CT_)
                    if n == 0:
                        o = begin(("rs", l))
                        need(lnr_ready, 1)
                        for t in range(TT):
                            ins = pe.matmul(o[:, t * P:(t + 1) * P], ones[:, :], tp[:, 3, t * P:(t + 1) * P],
                                            start=True, stop=True)
                        end(ins)
                need(u_lo_ready, 1)
                for n in range(2):
                    token_major([("ya", l, n, t) for t in range(TT)], u_hi, u_lo, CT_)
                transposes([("mT", l, i) for i in range(4)], merged, merged_ready)
                need(x_lo_ready, 4)
                for n in range(2):
                    token_major([("out", l, n, t) for t in range(TT)], x_hi, x_lo, KD)

                transposes([("hT2", l, i) for i in range(4)], hn, hn_ready)
                need(x_lo_ready, 4)
                for n in range(2):
                    channel_major([("q", l, n, i) for i in range(2)], x_hi, x_lo)
                need(q_ready, 4)
                need(kv_ready, 8)
                for hh in range(H + 1):
                    if hh < H:
                        o = begin(("sc", l, hh))
                        for t in range(TT):
                            for k in range(2):
                                ins = pe.matmul(o[:, t * T:(t + 1) * T], qT[:, 2 * hh + k, t * P:(t + 1) * P],
                                                kT[:, 2 * hh + k, :], start=(k == 0), stop=(k == 1))
                        end(ins)
                    if hh >= 1:
                        g = hh - 1
                        o = begin(("pT", l, g))
                        need(prob_ready, TT)
                        for t in range(TT):
                            for m in range(TT):
                                ins = pe.transpose(o[:, m * T + t * P:m * T + (t + 1) * P],
                                                   prob[:, g, t, m * P:(m + 1) * P], ident[:, :])
                        end(ins)
                        o = begin(("oT", l, g))
                        need(pT_ready, 1)
                        for dtile in range(2):
                            for m in range(TT):
                                c0 = g * HD + dtile * P
                                ins = pe.matmul(o[:, dtile * T:(dtile + 1) * T], v[:, m, c0:c0 + P], pT[:, g, m, :],
                                                start=(m == 0), stop=(m == TT - 1))
                        end(ins)
                need(a_lo_ready, H)
                for n in range(2):
                    token_major([("o", l, n, t) for t in range(TT)], a_hi, a_lo, KD)
                transposes([("hT3", l, i) for i in range(4)], hn, hn_ready)
                if l == 0:
                    need(x_lo_ready, 4)
                    for b in range(FBLK + 1):
                        if b < FBLK:
                            token_major([("fgu", b, t) for t in range(TT)], x_hi, x_lo, KD)
                        if b >= 1:
                            o = begin(("fT", b - 1))
                            need(h1_ready, TT)
                            for t in range(TT):
                                for f in range(2):
                                    ins = pe.transpose(o[:, f * T + t * P:f * T + (t + 1) * P],
                                                       h1[:, (2 * (b - 1) + t) % 4, f * P:(f + 1) * P], ident[:, :])
                            end(ins)
                        if b in FPIECE_END:
                            piece = FPIECE_END.index(b)
                            b0 = FPIECE_END[piece - 1] if piece else 0
                            need(a_lo_ready, b - b0)
                            os = [[begin(("fdn", piece, t, n)) for n in range(2)] for t in range(TT)]
                            for c in range(b0, b):
                                w_h, w_l, done = next_chunk()
                                for k in range(2):
                                    f = 2 * (c - b0) + k
                                    start, stop = f == 0, f == 2 * (b - b0) - 1
                                    for t in range(TT):
                                        for n in range(2):
                                            w = slice(k * D + n * BLK, k * D + (n + 1) * BLK)
                                            ins = three(os[t][n], a_hi[:, f, t * P:(t + 1) * P],
                                                        a_lo[:, f, t * P:(t + 1) * P], w_h[:, w], w_l[:, w], start, stop)
                                            if stop:
                                                end(ins)
                                if done[0] == "part":
                                    ins.then_inc(part_done, 1)

            o = begin(("rt",))
            pe.wait_ge(xTf_ready, 4)
            pe.wait_ge(late_loaded, 16 * 4)
            for t in range(TT):
                for k in range(KD):
                    ins = pe.matmul(o[:, t * NE:(t + 1) * NE], xTf[:, k, t * P:(t + 1) * P], rw[:, k, :],
                                    start=(k == 0), stop=(k == KD - 1))
            end(ins)
            o = begin(("pos",))
            pe.wait_ge(mask_ready, 1)
            pe.matmul(o[:, 0:NE], tri, mask[:, 0, 0:NE], start=True, stop=True)
            for base, w in ((NE, tri), (2 * NE, ones[:, :])):
                pe.matmul(o[:, base:base + NE], ones[:, :], mask[:, 0, 0:NE], start=True, stop=False)
                ins = pe.matmul(o[:, base:base + NE], w, mask[:, 1, 0:NE], start=False, stop=True)
            end(ins)

            def gather(i):
                for j in range(4):
                    k = 4 * i + j
                    for t in range(TT):
                        ins = pe.matmul(ps[:, 6 + i, j * P:(j + 1) * P], hn[:, t, k * P:(k + 1) * P], pick[:, t, :],
                                        start=(t == 0), stop=(t == TT - 1))
                ins.then_inc(ga_done, 1)

            pe.wait_ge(pick_ready, 1)
            for i in range(2):
                gather(i)
            assert task[0] == len(PLAN) and chunk[0] == len(CHUNKS)
            h1_0, a_0 = sig[id(h1_ready)], sig[id(a_lo_ready)]

            pe.wait_ge(over_ready, 1)
            most = pe.value_load(over[0:1, 0:1], min_val=0, max_val=T)

            def expert(it):
                at = [0]

                def lbegin(name):
                    i = LAT[name]
                    pe.wait_ge(bank_free[i % RING_BANKS], it * (PER // RING_BANKS) + i // RING_BANKS)
                    return bank(i)

                def loaded():
                    u = at[0]
                    at[0] += 1
                    e_low_wait(pe, it, u)
                    return half_hi[:, u % HSLOTS, :], half_lo[:, u % HSLOTS, :], ECHUNKS[u][3]

                for name in LOOP:
                    if name[0] == "gu":
                        b = name[1]
                        if b == 0:
                            pe.wait_ge(xg_lo_ready, it * 2 + 2)
                        o = lbegin(name)
                        for c in range(4):
                            w_h, w_l, done = loaded()
                            for k in range(2):
                                kk = 2 * c + k
                                w = slice(k * BLK, (k + 1) * BLK)
                                ins = three(o, xg_hi[:, kk, :], xg_lo[:, kk, :], w_h[:, w], w_l[:, w], kk == 0,
                                            kk == KD - 1)
                            ins.then_inc(part_done if done[0] == "part" else mm_done, 1)
                        if b == EBLK - 1:
                            pe.wait_ge(pick_ready, it + 2)
                            pe.wait_ge(ga_read, it * 2 + 2)
                            for i in range(2):
                                gather(i)
                    elif name[0] == "eT":
                        i = name[1]
                        o = lbegin(name)
                        pe.wait_ge(h1_ready, it * EBLK + (h1_0 + 2 * i + 2))
                        for b in range(2):
                            for f in range(2):
                                ins = pe.transpose(o[:, (2 * b + f) * P:(2 * b + f + 1) * P],
                                                   h1[:, (2 * i + b) % 4, f * P:(f + 1) * P], ident[:, :])
                        ins.then_inc(mm_done, 1)
                    elif name[0] == "gT":
                        o = lbegin(name)
                        pe.wait_ge(pickg_ready, it + 1)
                        for t in range(TT):
                            ins = pe.transpose(o[:, t * P:(t + 1) * P], pickg[:, t, :], ident[:, :])
                        ins.then_inc(mm_done, 1)
                    elif name[0] == "edn" and name[2] == 0:
                        piece = name[1]
                        lo, hi = EPIECES[piece]
                        os = [lbegin(("edn", piece, n)) for n in range(2)]
                        pe.wait_ge(a_lo_ready, it * (EBLK // 2) + (a_0 + hi // 2))
                        for f in range(2 * (hi - lo)):
                            w_h, w_l, done = loaded()
                            stop = f == 2 * (hi - lo) - 1
                            for n in range(2):
                                w = slice(n * BLK, (n + 1) * BLK)
                                ins = three(os[n], e_hi[:, f, :], e_lo[:, f, :], w_h[:, w], w_l[:, w], f == 0, stop)
                                if stop:
                                    ins.then_inc(mm_done, 1)
                            if done[0] == "part":
                                ins.then_inc(part_done, 1)
                    elif name[0] == "add":
                        _, t, n = name
                        o = lbegin(name)
                        if t == 0 and n == 0:
                            pe.wait_ge(gT_ready, it + 1)
                            pe.wait_ge(ye_ready, it * 4 + 4)
                        pe.matmul(o, gT[:, t, :], ye[:, n * BLK:(n + 1) * BLK], start=True, stop=True).then_inc(mm_done, 1)

            with pe.Fori(0, NE) as e:
                expert(e)
            with pe.If(most > P):
                with pe.Fori(0, NE) as e:
                    expert(e + NE)

        @block.scalar
        def _(act):
            act.wait_ge(rows_cleared, 1)
            act.dma_start(h[:, :, :], a["x"][0].rearrange("(t p) n -> p t n", p=P)).then_inc(x_loaded, 16)
            for l in range(L):
                for row, name in ((ROW_MIX, "norm_mix_g"), (ROW_X, "norm_xattn_g"), (ROW_FFN, "norm_ffn_g"),
                                  (ROW_CB, "conv_b"), (ROW_LG, "conv_ln_g"), (ROW_LB, "conv_ln_b")):
                    src = a[name][l].rearrange("(r n) -> r n", n=P)
                    act.dma_start(prow[row:row + src.shape[0], l, 0, :], src).then_inc(rows_loaded, 16)
                act.dma_start(prow[ROW_D:ROW_D + 4, l, 0, :],
                              a["ssm_d"][l].rearrange("(r g) n -> r (g n)", r=4)).then_inc(rows_loaded, 16)
                act.dma_start(prow[ROW_MEM:ROW_MEM + 8, l, 0, :],
                              a["mem_norm_g"].rearrange("(r n) -> r n", n=P)).then_inc(rows_loaded, 16)
                for row, name in ((ROW_LR, "ssm_lambda_re"), (ROW_LI, "ssm_lambda_im")):
                    act.dma_start(prow[row:row + ST, l, 0, :],
                                  a[name][l].rearrange("(j q) n -> j (q n)", q=2)).then_inc(rows_loaded, 16)
                act.dma_start(dtq[ROW_DT:ROW_DT + ST, l, :],
                              a["ssm_log_dt"][l].rearrange("(j q) -> j q", q=2)).then_inc(rows_loaded, 16)
                act.dma_start(prow[0:TAPS * CT_, l, 1, :],
                              a["conv_w"][l].rearrange("k (c n) -> (k c) n", n=P)).then_inc(rows_loaded, 16)
            act.dma_start(mem, a["mem"][0].rearrange("(t p) n -> p t n", p=P)).then_inc(mem_loaded, 16)

            done = {}
            split = Splitter(nc.scalar, "hi")

            def result(name):
                split.upto(name)
                act.wait_ge(mm_done, AT[name] + 1)
                return bank(AT[name])

            def note(sema, k):
                done[id(sema)] = done.get(id(sema), 0) + k
                act.wait_ge(sema, done[id(sema)])

            def free_bank(name):
                act.sem_inc(bank_free[AT[name] % RING_BANKS], 1)

            def h_sums(first=False):
                for t in range(TT):
                    if not first:
                        note(h_ready, 1)
                    elif t == 0:
                        act.wait_ge(x_loaded, 16)
                    nc.scalar.activation(hn[:, t, :], h[:, t, :], ACT.Square,
                                         accum_out=ssq[:, t:t + 1]).then_inc(ssq_ready, 1)

            def x_high(kind, l, row):
                for i in range(4):
                    o = result((kind, l, i))
                    for j in range(2):
                        k = 2 * i + j
                        nc.scalar.activation(x_hi[:, k, :], o[:, j * T:(j + 1) * T], ACT.Copy,
                                             scale=cols[:, l, row + k:row + k + 1]).then_inc(x_hi_ready, 1)

            def copy_out(name, dst, sema, func=ACT.Copy, scale=1.0):
                o = result(name)
                nc.scalar.activation(dst, o[:, 0:512], func, scale=scale).then_inc(sema, 1)
                note(sema, 1)
                free_bank(name)

            h_sums(first=True)
            act.wait_ge(mem_loaded, 16)
            for t in range(TT):
                nc.scalar.activation(tp[:, 2 * t:2 * t + 2, :].rearrange("p i n -> p (i n)"), mem[:, t, :], ACT.Square,
                                     accum_out=mssq[:, t:t + 1]).then_inc(mssq_ready, 1)
            split.to(SPLITS)
            act.wait_ge(cols_ready, 3)
            x_high("hT", 0, ROW_MIX)

            S = {n: sm[:, i, :] for i, n in enumerate(SMALL)}
            nc.scalar.activation(S["dt"], S["ldt"], ACT.Exp).then_inc(ssm_act, 1)
            act.wait_ge(ssm_arg, 1)
            nc.scalar.activation(S["mag"], S["lrdt"], ACT.Exp).then_inc(ssm_act, 1)
            act.wait_ge(ssm_arg, 2)
            nc.scalar.activation(S["s1"], S["ang"], ACT.Sin).then_inc(ssm_act, 1)
            nc.scalar.activation(S["aabs"], S["ang"], ACT.Abs).then_inc(ssm_act, 1)
            act.wait_ge(ssm_act, 4)
            nc.scalar.activation(S["c1"], S["aabs"], ACT.Sin, scale=-1.0, bias=half_pi[:, 0:1]).then_inc(ssm_act, 1)

            for l in range(L):
                if l > 0:
                    h_sums()
                    x_high("hT", l, ROW_MIX)
                for i in range(2):
                    copy_out(("cg", l, i), tg[:, i, :], tanh_ready, ACT.Tanh, 0.5)
                for i in range(2):
                    copy_out(("us", l, i), us[:, 2 * i:2 * i + 2, :].rearrange("p c n -> p (c n)"), us_ready)
                for r in range(2):
                    copy_out(("ct", l, r), cT[:, r, :, :].rearrange("p i n -> p (i n)"), cT_ready, scale=(1.0, -1.0)[r])
                if l == 0:
                    for i in (0, 2):
                        o = result(("memT", i))
                        for j in range(2):
                            k = 2 * i + j
                            nc.scalar.activation(memT[:, k, :], o[:, j * T:(j + 1) * T], ACT.Copy,
                                                 scale=cols[:, 0, ROW_MEM + k:ROW_MEM + k + 1]).then_inc(memT_act, 1)
                        note(memT_act, 2)
                        free_bank(("memT", i))
                for p in range(PAIRS):
                    kind, n = FILLERS[p]
                    if kind == "k" and n == 0:
                        act.wait_ge(rot_out, 4 * (l * PAIRS + PAIRS // 2))
                    for i in range(2):
                        if kind == "gt":
                            copy_out((kind, l, n, i), gates[:, i, n * BLK:(n + 1) * BLK], gates_ready, ACT.Tanh, 0.5)
                        elif kind == "k":
                            c = 4 * n + 2 * i
                            copy_out((kind, l, n, i), kT[:, c:c + 2, :].rearrange("p c n -> p (c n)"), kv_ready)
                        else:
                            copy_out((kind, l, n, i), v[:, i, n * BLK:(n + 1) * BLK], kv_ready)
                for i in range(CT_):
                    note(ypre_ready, 1)
                    nc.scalar.activation(yT[:, i, :], yT[:, i, :], ACT.Gelu_apprx_tanh).then_inc(gelu_ready, 1)
                    note(gelu_ready, 1)
                    nc.scalar.activation(y_hi[:, i, :], yT[:, i, :], ACT.Copy).then_inc(y_hi_ready, 1)
                note(xc_ready, 1)
                nc.scalar.activation(tp[:, 0:2, :].rearrange("p i n -> p (i n)"),
                                     conv[:, :, :].rearrange("p c n -> p (c n)"), ACT.Square).then_inc(sq_ready, 1)
                for n in range(2):
                    for t in range(TT):
                        u = (l * 2 + n) * TT + t
                        if u >= 2:
                            act.wait_ge(tanh_used, u - 1)
                        copy_out(("zg", l, n, t), tg[:, t, :], tanh_ready, ACT.Tanh, 0.5)
                    if n == 0:
                        split.upto(("rs", l))
                        note(lnz_ready, 1)
                        nc.scalar.activation(tp[:, 0:2, :].rearrange("p i n -> p (i n)"),
                                             conv[:, :, :].rearrange("p c n -> p (c n)"), ACT.Tanh,
                                             scale=0.5).then_inc(lnt_ready, 1)
                        note(u32_ready, 1)
                        nc.scalar.activation(u_hi[:, :, :].rearrange("p c n -> p (c n)"),
                                             conv[:, :, :].rearrange("p c n -> p (c n)"), ACT.Copy).then_inc(u_hi_ready, 1)
                for i in range(4):
                    o = result(("mT", l, i))
                    nc.scalar.activation(x_hi[:, 2 * i:2 * i + 2, :].rearrange("p c n -> p (c n)"), o[:, 0:512], ACT.Copy,
                                         scale=0.25).then_inc(x_hi_ready, 2)
                split.upto(("out", l, 1, 1))
                h_sums()
                x_high("hT2", l, ROW_X)
                for n in range(2):
                    for i in range(2):
                        c = 4 * n + 2 * i
                        copy_out(("q", l, n, i), qT[:, c:c + 2, :].rearrange("p c n -> p (c n)"), q_ready)
                for hh in range(H + 1):
                    if hh < H:
                        n = ("sc", l, hh)
                        note(nb_ready, 1)
                        for t in range(TT):
                            nc.scalar.activation(prob[:, hh, t, :], bank(AT[n])[:, t * T:(t + 1) * T], ACT.Exp,
                                                 scale=1.0 / math.sqrt(HD), bias=snb[:, hh, t:t + 1],
                                                 accum_out=ssum[:, hh, t:t + 1]).then_inc(exp_ready, 1)
                        note(exp_ready, TT)
                        free_bank(n)
                    if hh >= 1:
                        g = hh - 1
                        o = result(("oT", l, g))
                        nc.scalar.activation(a_hi[:, 2 * g:2 * g + 2, :].rearrange("p c n -> p (c n)"), o[:, 0:512],
                                             ACT.Copy).then_inc(a_hi_ready, 1)
                split.upto(("o", l, 1, 1))
                h_sums()
                if l == 0:
                    x_high("hT3", l, ROW_FFN)
                    for b in range(FBLK + 1):
                        for t in range(TT):
                            if b < FBLK:
                                u = 2 * b + t
                                if u >= 4:
                                    act.wait_ge(h1_ready, u - 3)
                                o = result(("fgu", b, t))
                                nc.scalar.activation(sil[:, u % 4, :], o[:, 0:256], ACT.Silu).then_inc(sil_ready, 1)
                        if b >= 1:
                            piece = [b <= x for x in FPIECE_END].index(True)
                            f = 2 * (b - 1 - (FPIECE_END[piece - 1] if piece else 0))
                            o = result(("fT", b - 1))
                            nc.scalar.activation(a_hi[:, f:f + 2, :].rearrange("p f n -> p (f n)"), o[:, 0:512],
                                                 ACT.Copy).then_inc(a_hi_ready, 1)
                    split.upto(("fdn", len(FPIECE_END) - 1, 1, 1))
                else:
                    split.to(len(SPLIT_AT))
                    split.first_experts()

            act.wait_ge(topd_ready, 1)
            nc.scalar.activation(tw[:, 1, :], tw[:, 0, :], ACT.Exp).then_inc(tope_ready, 1)
            def xg_high(i):
                nc.scalar.activation(xg_hi[:, 4 * i:4 * i + 4, :].rearrange("p k n -> p (k n)"), ps[:, 6 + i, :],
                                     ACT.Copy).then_inc(xg_hi_ready, 1)

            act.wait_ge(ga_done, 2)
            for i in range(2):
                xg_high(i)
            act.wait_ge(over_ready, 1)
            most = act.value_load(over[0:1, 0:1], min_val=0, max_val=T)
            h1_0, a_0 = 2 * FBLK, FBLK + L * H

            def expert(it):
                nxt = [HSLOTS]

                def ahead(name):
                    while nxt[0] < min(EXPERT.bound[name] + AHEAD_H, EH + HSLOTS):
                        split.expert(it, nxt[0])
                        nxt[0] += 1

                def lresult(name):
                    ahead(name)
                    act.wait_ge(mm_done, it * PER + LAT[name] + 1)
                    return bank(LAT[name])

                for name in LOOP:
                    i = LAT[name]
                    if name[0] == "gu":
                        b = name[1]
                        act.wait_ge(h1_ready, it * EBLK + (h1_0 + b - 3))
                        o = lresult(name)
                        nc.scalar.activation(sil[:, b % 4, :], o[:, 0:256], ACT.Silu).then_inc(sil_ready, 1)
                        if b == EBLK - 1:
                            act.wait_ge(ga_done, it * 2 + 4)
                            for k in range(2):
                                xg_high(k)
                    elif name[0] == "eT":
                        o = lresult(name)
                        j = name[1]
                        f = 4 * j if 2 * j < EPIECES[0][1] else 4 * j - 2 * EPIECES[1][0]
                        nc.scalar.activation(e_hi[:, f:f + 4, :].rearrange("p f n -> p (f n)"), o[:, 0:512],
                                             ACT.Copy).then_inc(a_hi_ready, 1)
                    elif name[0] == "edn" and name[1] == 0:
                        o = lresult(name)
                        n = name[2]
                        nc.scalar.activation(ye[:, n * BLK:(n + 1) * BLK], o[:, 0:512], ACT.Copy).then_inc(ye_ready, 1)
                        act.wait_ge(ye_ready, it * 4 + n + 1)
                        act.sem_inc(bank_free[i % RING_BANKS], 1)
                while nxt[0] < EH + HSLOTS:
                    split.expert(it, nxt[0])
                    nxt[0] += 1

            with act.Fori(0, NE) as e:
                expert(e)
            with act.If(most > P):
                with act.Fori(0, NE) as e:
                    expert(e + NE)
            h_sums()

        @block.vector
        def _(dve):
            V = nc.vector
            steps = Signal(dve_step)
            cnt = {}

            def link(ins):
                dve.wait_ge(dve_step, steps.by(ins))

            def note(sema, k):
                cnt[id(sema)] = cnt.get(id(sema), 0) + k
                dve.wait_ge(sema, cnt[id(sema)])

            split = Splitter(V, "dve")

            def result(name):
                split.upto(name)
                dve.wait_ge(mm_done, AT[name] + 1)
                return bank(AT[name])

            def free_bank(name):
                V.sem_inc(bank_free[AT[name] % RING_BANKS], 1)

            def evac(n, ins, sema=None, k=1):
                if sema is None:
                    link(ins)
                else:
                    ins.then_inc(sema, k)
                    note(sema, k)
                free_bank(n)

            def normalise(src, dst, r, rsem, ready):
                for t in range(TT):
                    note(rsem, 1)
                    V.tensor_scalar(dst[:, t, :], src[:, t, :], r[:, t:t + 1], None, ALU.mult).then_inc(ready, 1)

            def x_low(kind, l, row):
                for i in range(4):
                    o = result((kind, l, i))
                    note(x_hi_ready, 2)
                    for j in range(2):
                        k = 2 * i + j
                        ins = V.scalar_tensor_tensor(x_lo[:, k, :], o[:, j * T:(j + 1) * T], cols[:, l, row + k:row + k + 1],
                                                     x_hi[:, k, :].bitcast(F32), ALU.mult, ALU.subtract)
                        if j == 0:
                            link(ins)
                    evac((kind, l, i), ins, x_lo_ready)

            def a_low(name, k):
                o = result(name)
                note(a_hi_ready, 1)
                evac(name, V.tensor_tensor(a_lo[:, k:k + 2, :].rearrange("p c n -> p (c n)"), o,
                                           a_hi[:, k:k + 2, :].rearrange("p c n -> p (c n)").bitcast(F32), ALU.subtract),
                     a_lo_ready)

            link(V.memset(prow[:, :, :, :], 0.0))
            V.sem_inc(rows_cleared, 1)
            V.memset(half_pi[:, :], math.pi / 2)
            dve.wait_ge(rows_loaded, 16 * 12 * L)
            for l in range(L):
                ins = V.tensor_copy(prow[ROW_DT:ROW_DT + ST, l, 0, :].rearrange("p (q n) -> p q n", q=2),
                                    dtq[ROW_DT:ROW_DT + ST, l, :].unsqueeze(2).to_broadcast([ST, 2, NS]))
                link(ins)
            V.sem_inc(rows_ready, 1)
            normalise(h, hn, rstd, rstd_ready, hn_ready)
            dve.wait_ge(par_done, 1)
            o = ps[:, 6, :]
            V.tensor_copy(cols[:, :, 0:ROWS], o.rearrange("p (m n) -> p m n", m=4)[:, 0:2, 0:ROWS]).then_inc(cols_ready, 1)
            V.tensor_scalar(taps[:, :, :], o.rearrange("p (m n) -> p m n", m=4)[:, 2:4, 0:TAPS * CT_], 0.5, None,
                            ALU.mult).then_inc(cols_ready, 1)
            dve.wait_ge(cols_ready, 2)

            S = {name: sm[:, i, :] for i, name in enumerate(SMALL)}
            for name, row in (("ldt", ROW_DT), ("lr", ROW_LR), ("li", ROW_LI)):
                link(V.tensor_copy(S[name].rearrange("p (l j) -> p l j", l=L), cols[:, :, row:row + ST]))
            V.sem_inc(cols_ready, 1)
            x_low("hT", 0, ROW_MIX)
            note(ssm_act, 1)
            tt = lambda o_, x, y, op: link(V.tensor_tensor(S[o_], S[x], S[y], op))
            tt("lrdt", "lr", "dt", ALU.mult)
            V.sem_inc(ssm_arg, 1)
            tt("lidt", "li", "dt", ALU.mult)
            link(V.tensor_scalar(S["rnd"], S["lidt"], 1 / (2 * math.pi), MAGIC, ALU.mult, ALU.add))
            link(V.tensor_scalar(S["rnd"], S["rnd"], MAGIC, None, ALU.subtract))
            link(V.scalar_tensor_tensor(S["ang"], S["rnd"], -TWO_PI_A, S["lidt"], ALU.mult, ALU.add))
            link(V.scalar_tensor_tensor(S["ang"], S["rnd"], -TWO_PI_B, S["ang"], ALU.mult, ALU.add))
            link(V.scalar_tensor_tensor(S["ang"], S["rnd"], -TWO_PI_C, S["ang"], ALU.mult, ALU.add))
            link(V.tensor_scalar(S["ang"], S["ang"], PI_BELOW, -PI_BELOW, ALU.min, ALU.max))
            V.sem_inc(ssm_arg, 1)
            tt("den", "lr", "lr", ALU.mult)
            tt("t1", "li", "li", ALU.mult)
            tt("den", "den", "t1", ALU.add)
            link(V.reciprocal(S["rden"], S["den"]))
            note(ssm_act, 4)
            V.sem_inc(trig_seed, 1)
            tt("ar", "mag", "c1", ALU.mult)
            tt("ai", "mag", "s1", ALU.mult)
            link(V.tensor_scalar(S["xr"], S["ar"], 1.0, None, ALU.subtract))
            tt("t1", "xr", "lr", ALU.mult)
            tt("t2", "ai", "li", ALU.mult)
            tt("t1", "t1", "t2", ALU.add)
            tt("kr", "t1", "rden", ALU.mult)
            tt("t1", "ai", "lr", ALU.mult)
            tt("t2", "xr", "li", ALU.mult)
            tt("t1", "t1", "t2", ALU.subtract)
            tt("ki", "t1", "rden", ALU.mult)

            def conv_tap(l, i):
                if i >= TAPS * CT_:
                    return
                k, c = divmod(i, CT_)
                base = l * TAPS * CT_
                w = taps[:, l, k * CT_ + c:k * CT_ + c + 1]
                src = upad[:, c, k:k + T]
                if k == 0:
                    ins = V.tensor_scalar(conv[:, c, :], src, w, cols[:, l, ROW_CB + c:ROW_CB + c + 1], ALU.mult, ALU.add)
                else:
                    dve.wait_ge(conv_step, base + i - 3)
                    ins = V.scalar_tensor_tensor(conv[:, c, :], src, w, conv[:, c, :], ALU.mult, ALU.add)
                ins.then_inc(conv_step, 1)

            for l in range(L):
                if l > 0:
                    normalise(h, hn, rstd, rstd_ready, hn_ready)
                    x_low("hT", l, ROW_MIX)
                note(bc_loaded, 64)
                kr = S["kr"].rearrange("p (l j) -> p l j", l=L)[:, l, :].unsqueeze(2).to_broadcast([P, ST, GH])
                ki = S["ki"].rearrange("p (l j) -> p l j", l=L)[:, l, :].unsqueeze(2).to_broadcast([P, ST, GH])
                link(V.memset(arena[:, 0:1024], 0.0))
                for r in range(2):
                    V.tensor_tensor(bt[:, 0, :, :], braw[:, r, :, :], kr, ALU.mult).then_inc(dve_step, 1)
                    steps.n += 1
                    link(V.tensor_tensor(bt[:, 1, :, :], braw[:, 1 - r, :, :], ki, ALU.mult))
                    for q in range(2):
                        rows = slice(64 * q, 64 * q + 64)
                        ins = V.tensor_tensor(bd[rows, r, :, q, :], bt[rows, 0, :, :], bt[rows, 1, :, :],
                                              ALU.subtract if r == 0 else ALU.add)
                        link(ins)
                V.sem_inc(bd_ready, 1)
                if l == 0:
                    note(consts_ready, 1)
                    link(V.tensor_reduce(evod[:, :], blkm[:, :].rearrange("p (b q) -> p q b", q=2), AX_X, ALU.add))
                for q in range(2):
                    link(V.tensor_scalar(xc[:, :, q, :], craw[:, :, :, :].rearrange("p r i n -> p (r i) n"),
                                         evod[:, q:q + 1], None, ALU.mult))
                V.sem_inc(bd_ready, 1)
                V.sem_inc(bc_used, 1)
                link(V.memset(upad[:, :, 0:PAD], 0.0))
                for i in range(2):
                    n = ("ca", l, i)
                    o = result(n)
                    note(tanh_ready, 1)
                    evac(n, V.scalar_tensor_tensor(upad[:, 2 * i:2 * i + 2, PAD:PAD + T],
                                                   tg[:, i, :].rearrange("p (c n) -> p c n", c=2), 1.0,
                                                   o.rearrange("p (c n) -> p c n", c=2), ALU.add, ALU.mult))
                if l == 0:
                    normalise(mem, mem, mrstd, mrstd_ready, mn_ready)
                for r in range(2):
                    n = ("bd", l, r)
                    o = result(n)
                    evac(n, V.tensor_copy(bdT[:, r, :, :].rearrange("p i n -> p (i n)"), o), bdT_ready)
                if l == 0:
                    for i in (1, 3):
                        n = ("memT", i)
                        o = result(n)
                        gain = cols[:, 0, ROW_MEM + 2 * i:ROW_MEM + 2 * i + 2].unsqueeze(2).to_broadcast([P, 2, T])
                        evac(n, V.tensor_tensor(memT[:, 2 * i:2 * i + 2, :], o.rearrange("p (j n) -> p j n", j=2), gain,
                                                ALU.mult), memT_dve)
                    for i in range(2):
                        trig(nc.vector, link, l, i, (tp[:, 0, :], tp[:, 1, :]), w2, 0)
                tap = [0]

                def conv_taps(k):
                    for _ in range(k):
                        conv_tap(l, tap[0])
                        tap[0] += 1

                def halves(x, n=2):
                    return x.rearrange("p (s a n) -> p s a n", s=n, a=2)

                for p in range(PAIRS):
                    q = l * PAIRS + p
                    jt = slice(2 * p % (ST // 2), 2 * p % (ST // 2) + 2)
                    cp, sn = (trigT[:, p // 4, k, jt, :].unsqueeze(2).to_broadcast([P, 2, 2, P]) for k in range(2))
                    if l == 0 and p in (4, 6):
                        note(trig_pool, 1)
                    if l == 1 and p % 2 == 0:
                        note(trig_pool, 1)
                    n0, n1 = ("bu", l, p, 0), ("bu", l, p, 1)
                    result(n0)
                    result(n1)
                    if q > 0:
                        dve.wait_ge(hst_ready, 2 * q)
                    b0, b1 = AT[n0] % RING_BANKS, AT[n1] % RING_BANKS
                    runs = [(0, 2, b0)] if b1 == b0 + 1 else [(0, 1, b0), (1, 1, b1)]
                    for k, (tab, r) in enumerate(((cp, 0), (sn, 1), (cp, 1), (sn, 0))):
                        for s0, n, b in runs:
                            ins = V.tensor_tensor(halves(tp[:, k, s0 * T:(s0 + n) * T], n), tab[:, s0:s0 + n],
                                                  ps[:, b:b + n, r * T:(r + 1) * T].rearrange("p s (a n) -> p s a n", a=2),
                                                  ALU.mult)
                            if s0 + n == 2:
                                ins.then_inc(rot_in, 1)
                            else:
                                link(ins)
                    note(rot_in, 4)
                    free_bank(n0)
                    free_bank(n1)
                    conv_taps(8)
                    def recur(a_):
                        for r in range(2):
                            if a_ == 0:
                                note(rin_ready, 1)
                            for s in range(2):
                                j = l * ST + 2 * p + s
                                x = tp[:, 2 * r, s * T + a_ * P:s * T + (a_ + 1) * P]
                                V.tensor_tensor_scan(x, S["mag"][:, j:j + 1].to_broadcast([P, P]), x,
                                                     bnd[:, 4 + r, s:s + 1] if a_ else 0.0,
                                                     ALU.mult, ALU.add).then_inc(dve_step, 1)
                                steps.n += 1
                    recur(0)
                    conv_taps(2)
                    dve.wait_ge(dve_step, steps.n)
                    c128, s128 = (S[x][:, l * ST + 2 * p:l * ST + 2 * p + 2] for x in ("c128", "s128"))
                    g_re, g_im = (halves(tp[:, r, :])[:, :, 0, P - 1:P].rearrange("p s n -> p (s n)") for r in (0, 2))
                    for k, (x, y) in enumerate(((c128, g_re), (s128, g_im), (s128, g_re), (c128, g_im))):
                        V.tensor_tensor(bnd[:, k, :], x, y, ALU.mult).then_inc(dve_step, 1)
                        steps.n += 1
                    conv_taps(1)
                    dve.wait_ge(dve_step, steps.n)
                    V.tensor_tensor(bnd[:, 4, :], bnd[:, 0, :], bnd[:, 1, :], ALU.subtract).then_inc(dve_step, 1)
                    V.tensor_tensor(bnd[:, 5, :], bnd[:, 2, :], bnd[:, 3, :], ALU.add).then_inc(dve_step, 1)
                    steps.n += 2
                    conv_taps(1)
                    dve.wait_ge(dve_step, steps.n)
                    recur(1)
                    conv_taps(1)
                    dve.wait_ge(dve_step, steps.n)
                    V.tensor_tensor(halves(tp[:, 1, :]), sn, halves(tp[:, 2, :]), ALU.mult).then_inc(rot_out, 1)
                    V.tensor_tensor(halves(tp[:, 3, :]), sn, halves(tp[:, 0, :]), ALU.mult).then_inc(rot_out, 1)
                    V.tensor_tensor(halves(tp[:, 0, :]), cp, halves(tp[:, 0, :]), ALU.mult).then_inc(rot_out, 1)
                    V.tensor_tensor(halves(tp[:, 2, :]), cp, halves(tp[:, 2, :]), ALU.mult).then_inc(rot_out, 1)
                    conv_taps(3)
                    note(rot_out, 4)
                    if p % 2 == 1 and p >= 3:
                        y_skip(dve, link, note, l, (p - 3) // 2)
                def y_low(i):
                    note(y_hi_ready, 1)
                    V.tensor_tensor(y_lo[:, i, :], yT[:, i, :], y_hi[:, i, :].bitcast(F32), ALU.subtract).then_inc(y_lo_ready, 1)

                conv_taps(TAPS * CT_)
                dve.wait_ge(conv_step, (l + 1) * TAPS * CT_)
                V.sem_inc(conv_ready, 1)
                y_skip(dve, link, note, l, CT_ - 1)
                n = ("mean", l)
                o = result(n)
                evac(n, V.scalar_tensor_tensor(conv[:, :, :], o[:, 0:T].unsqueeze(1).to_broadcast([P, CT_, T]), -1.0 / CW,
                                               conv[:, :, :], ALU.mult, ALU.add))
                V.sem_inc(xc_ready, 1)
                for i in range(CT_):
                    y_low(i)

                def glu(n_):
                    for t in range(TT):
                        n = ("za", l, n_, t)
                        o = result(n)
                        note(tanh_ready, 1)
                        g = gates[:, t, D + n_ * BLK:D + (n_ + 1) * BLK]
                        dst = merged[:, t, n_ * BLK:(n_ + 1) * BLK]
                        evac(n, V.scalar_tensor_tensor(dst, g, 1.0, o, ALU.add, ALU.mult))
                        link(V.scalar_tensor_tensor(dst, tg[:, t, :], 1.0, dst, ALU.add, ALU.mult))
                        V.sem_inc(tanh_used, 1)

                n = ("var", l)
                o = result(n)
                evac(n, V.tensor_scalar(tp[:, 2, 0:TT], o[:, 0:TT], 1.0 / CW, LN_EPS, ALU.mult, ALU.add))
                V.sem_inc(var_ready, 1)
                note(pow_ready, 1)
                for t in range(TT):
                    link(V.tensor_scalar(tp[:, 3, t * P:(t + 1) * P], ident[:, :], tp[:, 2, TT + t:TT + t + 1], None,
                                         ALU.mult))
                V.sem_inc(lnr_ready, 1)
                note(gates_ready, 8)
                dve.wait_ge(y_lo_ready, (l + 1) * CT_)
                glu(0)
                n = ("rs", l)
                o = result(n)
                evac(n, V.tensor_tensor(conv[:, :, :], conv[:, :, :], o[:, 0:T].unsqueeze(1).to_broadcast([P, CT_, T]),
                                        ALU.mult))
                for c in range(CT_):
                    V.tensor_scalar(conv[:, c, :], conv[:, c, :], cols[:, l, ROW_LG + c:ROW_LG + c + 1],
                                    cols[:, l, ROW_LB + c:ROW_LB + c + 1], ALU.mult, ALU.add).then_inc(dve_step, 1)
                    steps.n += 1
                dve.wait_ge(dve_step, steps.n)
                V.sem_inc(lnz_ready, 1)
                note(lnt_ready, 1)
                link(V.scalar_tensor_tensor(conv[:, :, :].rearrange("p c n -> p (c n)"),
                                            tp[:, 0:2, :].rearrange("p i n -> p (i n)"), 1.0,
                                            conv[:, :, :].rearrange("p c n -> p (c n)"), ALU.add, ALU.mult))
                V.sem_inc(u32_ready, 1)
                note(u_hi_ready, 1)
                V.tensor_tensor(u_lo[:, :, :].rearrange("p c n -> p (c n)"), conv[:, :, :].rearrange("p c n -> p (c n)"),
                                u_hi[:, :, :].rearrange("p c n -> p (c n)").bitcast(F32), ALU.subtract).then_inc(u_lo_ready, 1)
                glu(1)
                for n_ in range(2):
                    for t in range(TT):
                        n = ("ya", l, n_, t)
                        o = result(n)
                        dst = merged[:, t, n_ * BLK:(n_ + 1) * BLK]
                        evac(n, V.scalar_tensor_tensor(tp[:, 2 + t, :], gates[:, t, n_ * BLK:(n_ + 1) * BLK], 1.0, o,
                                                       ALU.add, ALU.mult))
                        link(V.tensor_tensor(dst, dst, tp[:, 2 + t, :], ALU.add))
                        if n_ == 1:
                            V.sem_inc(merged_ready, 1)
                for i in range(4):
                    n = ("mT", l, i)
                    o = result(n)
                    note(x_hi_ready, 2)
                    evac(n, V.scalar_tensor_tensor(x_lo[:, 2 * i:2 * i + 2, :].rearrange("p c n -> p (c n)"), o, 0.25,
                                                   x_hi[:, 2 * i:2 * i + 2, :].rearrange("p c n -> p (c n)").bitcast(F32),
                                                   ALU.mult, ALU.subtract), x_lo_ready)
                residual("out", l, dve, note, result, link, free_bank)
                normalise(h, hn, rstd, rstd_ready, hn_ready)
                x_low("hT2", l, ROW_X)
                for hh in range(H + 1):
                    if hh < H:
                        o = result(("sc", l, hh))
                        link(V.tensor_reduce(smx[:, hh, :], o.rearrange("p (t n) -> p t n", t=TT), AX_X, ALU.max))
                        link(V.tensor_scalar(snb[:, hh, :], smx[:, hh, :], -1.0 / math.sqrt(HD), None, ALU.mult))
                        V.sem_inc(nb_ready, 1)
                        note(exp_ready, TT)
                        link(V.reciprocal(srec[:, hh, :], ssum[:, hh, :]))
                        for t in range(TT):
                            V.tensor_scalar(prob[:, hh, t, :], prob[:, hh, t, :], srec[:, hh, t:t + 1], None,
                                            ALU.mult).then_inc(prob_ready, 1)
                    if hh >= 1:
                        g = hh - 1
                        n = ("pT", l, g)
                        o = result(n)
                        evac(n, V.tensor_copy(pT[:, g, :, :].rearrange("p m n -> p (m n)"), o), pT_ready)
                        a_low(("oT", l, g), 2 * g)
                residual("o", l, dve, note, result, link, free_bank)
                normalise(h, hn, rstd, rstd_ready, hn_ready)
                if l == 0:
                    x_low("hT3", l, ROW_FFN)
                    for b in range(FBLK + 1):
                        for t in range(TT):
                            if b < FBLK:
                                u = 2 * b + t
                                n = ("fgu", b, t)
                                result(n)
                                note(sil_ready, 1)
                                evac(n, V.tensor_tensor(h1[:, u % 4, :], sil[:, u % 4, :], bank(AT[n])[:, 256:512],
                                                        ALU.mult), h1_ready)
                        if b >= 1:
                            piece = [b <= x for x in FPIECE_END].index(True)
                            a_low(("fT", b - 1), 2 * (b - 1 - (FPIECE_END[piece - 1] if piece else 0)))
                        if b in FPIECE_END:
                            piece = FPIECE_END.index(b)
                            for t in range(TT):
                                for n_ in range(2):
                                    n = ("fdn", piece, t, n_)
                                    o = result(n)
                                    dst = h[:, t, n_ * BLK:(n_ + 1) * BLK]
                                    evac(n, V.tensor_tensor(dst, dst, o, ALU.add))
                                if piece == len(FPIECE_END) - 1:
                                    V.sem_inc(h_ready, 1)

            for i in range(4):
                n = ("hT3", L - 1, i)
                o = result(n)
                gain = cols[:, L - 1, ROW_FFN + 2 * i:ROW_FFN + 2 * i + 2].unsqueeze(2).to_broadcast([P, 2, T])
                evac(n, V.tensor_tensor(xTf[:, 2 * i:2 * i + 2, :], o.rearrange("p (j n) -> p j n", j=2), gain, ALU.mult),
                     xTf_ready)
            note(late_loaded, 64)
            note(late_consts, 1)
            for t in range(TT):
                link(V.tensor_tensor(hn[:, t, :], hn[:, t, :], fgain, ALU.mult))
            split.first_experts()

            n = ("rt",)
            o = result(n)
            for t in range(TT):
                ins = V.tensor_tensor(lg[:, t, :], o[:, t * NE:(t + 1) * NE], rb, ALU.add)
                link(ins)
            free_bank(n)
            link(V.memset(mask[:, :, :], 0.0))
            link(V.memset(gate[:, :, :], 0.0))
            link(V.memset(slot[:, :, :], -1.0))
            for t in range(TT):
                link(V.max(top[:, t, :], lg[:, t, :]))
                link(V.max_index(topu[:, t, :], top[:, t, :], lg[:, t, :]))
                link(V.tensor_copy(topi[:, t, :], topu[:, t, :]))
                link(V.tensor_tensor(tw[:, 0, t:t + 1], top[:, t, 1:2], top[:, t, 0:1], ALU.subtract))
            V.sem_inc(topd_ready, 1)
            for t in range(TT):
                for i in range(2):
                    link(V.tensor_scalar(oneh[:, i, t, :], iota[:, 0:NE], topi[:, t, i:i + 1], None, ALU.is_equal))
                link(V.tensor_tensor(mask[:, t, 0:NE], oneh[:, 0, t, :], oneh[:, 1, t, :], ALU.add))
                link(V.tensor_copy(mask[:, t, NE:2 * NE], mask[:, t, 0:NE]))
            V.sem_inc(mask_ready, 1)
            note(tope_ready, 1)
            link(V.tensor_scalar(tw[:, 2, :], tw[:, 1, :], 1.0, None, ALU.add))
            link(V.reciprocal(tw[:, 2, :], tw[:, 2, :]))
            link(V.tensor_tensor(tw[:, 3, :], tw[:, 1, :], tw[:, 2, :], ALU.mult))
            for t in range(TT):
                link(V.tensor_scalar(gate[:, t, 0:NE], oneh[:, 0, t, :], tw[:, 2, t:t + 1], None, ALU.mult))
                link(V.scalar_tensor_tensor(gate[:, t, 0:NE], oneh[:, 1, t, :], tw[:, 3, t:t + 1], gate[:, t, 0:NE],
                                            ALU.mult, ALU.add))
                link(V.tensor_copy(gate[:, t, NE:2 * NE], gate[:, t, 0:NE]))
            n = ("pos",)
            o = result(n)
            for t in range(TT):
                link(V.tensor_copy(slot[:, t, 0:NE], o[:, t * NE:(t + 1) * NE]))
                link(V.tensor_scalar(slot[:, t, NE:2 * NE], o[:, t * NE:(t + 1) * NE], float(P), None, ALU.subtract))
            link(V.tensor_reduce(tot[:, 0:1], o[:, 2 * NE:3 * NE], AX_X, ALU.max))
            free_bank(n)
            link(V.tensor_copy(over[:, :], tot[:, 0:1]))
            V.sem_inc(over_ready, 1)

            def one(e):
                return bass.ds(e, 1)

            for t in range(TT):
                link(V.tensor_scalar(pick[:, t, :], iota, slot[:, t, 0:1], mask[:, t, 0:1], ALU.is_equal, ALU.mult))
            V.sem_inc(pick_ready, 1)

            def xg_low(i, done):
                dve.wait_ge(xg_hi_ready, done)
                V.tensor_tensor(xg_lo[:, 4 * i:4 * i + 4, :].rearrange("p k n -> p (k n)"), ps[:, 6 + i, :],
                                xg_hi[:, 4 * i:4 * i + 4, :].rearrange("p k n -> p (k n)").bitcast(F32),
                                ALU.subtract).then_inc(xg_lo_ready, 1)
                dve.wait_ge(xg_lo_ready, done)
                V.sem_inc(ga_read, 1)

            for i in range(2):
                xg_low(i, i + 1)
            most = dve.value_load(over[0:1, 0:1], min_val=0, max_val=T)
            base = steps.n
            sil_0, h1_0, a_0 = 2 * FBLK, 2 * FBLK, FBLK + L * H

            def expert(it):
                k = [0]
                nxt = [HSLOTS]

                def ahead(name):
                    while nxt[0] < min(EXPERT.bound[name] + AHEAD_H, EH + HSLOTS):
                        split.expert(it, nxt[0])
                        nxt[0] += 1

                def llink(ins):
                    ins.then_inc(dve_step, 1)
                    k[0] += 1
                    dve.wait_ge(dve_step, it * DVE_STEPS + (base + k[0]))

                def lresult(name):
                    ahead(name)
                    dve.wait_ge(mm_done, it * PER + LAT[name] + 1)
                    return bank(LAT[name])

                def lfree(name):
                    V.sem_inc(bank_free[LAT[name] % RING_BANKS], 1)

                for t in range(TT):
                    llink(V.tensor_scalar(pickg[:, t, :], iota, slot[:, t, one(it)], gate[:, t, one(it)],
                                          ALU.is_equal, ALU.mult))
                V.sem_inc(pickg_ready, 1)
                for t in range(TT):
                    llink(V.tensor_scalar(pick[:, t, :], iota, slot[:, t, one(it + 1)], mask[:, t, one(it + 1)],
                                          ALU.is_equal, ALU.mult))
                V.sem_inc(pick_ready, 1)
                for name in LOOP:
                    if name[0] == "gu":
                        b = name[1]
                        ahead(name)
                        dve.wait_ge(sil_ready, it * EBLK + (sil_0 + b + 1))
                        o = bank(LAT[name])
                        V.tensor_tensor(h1[:, b % 4, :], sil[:, b % 4, :], o[:, 256:512], ALU.mult).then_inc(h1_ready, 1)
                        dve.wait_ge(h1_ready, it * EBLK + (h1_0 + b + 1))
                        lfree(name)
                        if b == EBLK - 1:
                            for i in range(2):
                                xg_low(i, it * 2 + (i + 3))
                    elif name[0] == "eT":
                        j = name[1]
                        f = 4 * j if 2 * j < EPIECES[0][1] else 4 * j - 2 * EPIECES[1][0]
                        o = lresult(name)
                        dve.wait_ge(a_hi_ready, it * (EBLK // 2) + (a_0 + j + 1))
                        V.tensor_tensor(e_lo[:, f:f + 4, :].rearrange("p f n -> p (f n)"), o,
                                        e_hi[:, f:f + 4, :].rearrange("p f n -> p (f n)").bitcast(F32),
                                        ALU.subtract).then_inc(a_lo_ready, 1)
                        dve.wait_ge(a_lo_ready, it * (EBLK // 2) + (a_0 + j + 1))
                        lfree(name)
                    elif name[0] == "edn" and name[1] == 1:
                        n_ = name[2]
                        o = lresult(name)
                        dve.wait_ge(ye_ready, it * 4 + (2 + n_))
                        dst = ye[:, n_ * BLK:(n_ + 1) * BLK]
                        V.tensor_tensor(dst, dst, o, ALU.add).then_inc(ye_ready, 1)
                        dve.wait_ge(ye_ready, it * 4 + (3 + n_))
                        lfree(name)
                    elif name[0] == "gT":
                        o = lresult(name)
                        llink(V.tensor_copy(gT[:, :, :].rearrange("p t n -> p (t n)"), o[:, 0:TT * P]))
                        V.sem_inc(gT_ready, 1)
                        lfree(name)
                    elif name[0] == "add":
                        _, t, n_ = name
                        o = lresult(name)
                        dst = h[:, t, n_ * BLK:(n_ + 1) * BLK]
                        llink(V.tensor_tensor(dst, dst, o, ALU.add))
                        lfree(name)
                while nxt[0] < EH + HSLOTS:
                    split.expert(it, nxt[0])
                    nxt[0] += 1
                assert k[0] == DVE_STEPS, k[0]

            DVE_STEPS = 2 * TT + 1 + 2 * TT
            with dve.Fori(0, NE) as e:
                expert(e)
            with dve.If(most > P):
                with dve.Fori(0, NE) as e:
                    expert(e + NE)
            for t in range(TT):
                V.sem_inc(h_ready, 1)
            for t in range(TT):
                note(rstd_ready, 1)
                V.tensor_scalar(hn[:, t, :], h[:, t, :], rstd[:, t:t + 1], None, ALU.mult).then_inc(hn_ready, 1)
                dve.wait_ge(hn_ready, (3 * L + 1) * TT - TT + t + 1)
                V.tensor_tensor(hn[:, t, :], hn[:, t, :], fg, ALU.mult).then_inc(out_ready, 1)

        @block.gpsimd
        def _(pool):
            GP = nc.gpsimd
            steps = Signal(pool_step)
            cnt = {}

            def link(ins):
                pool.wait_ge(pool_step, steps.by(ins))

            def note(sema, k):
                cnt[id(sema)] = cnt.get(id(sema), 0) + k
                pool.wait_ge(sema, cnt[id(sema)])

            def load_bc(l):
                for r, name in enumerate(("ssm_b_re", "ssm_b_im")):
                    src = a[name][l].rearrange("(j q) s h -> (q s) j h", q=2)
                    pool.dma_start(braw[:, r, :, :], src).then_inc(bc_loaded, 16)
                for r, name in enumerate(("ssm_c_re", "ssm_c_im")):
                    src = a[name][l].rearrange("(i g) h s -> (g h) i s", i=CT_)
                    pool.dma_start(craw[:, r, :, :], src).then_inc(bc_loaded, 16)

            load_bc(0)
            link(GP.memset(ident[:, :], 0.0))
            link(GP.affine_select(out=ident[:, :], in_=ident[:, :], compare_op=ALU.not_equal, fill=1.0, base=0,
                                  pattern=[[-1, P]], channel_multiplier=1))
            link(GP.memset(ones[:, :], 1.0))
            link(GP.memset(blkm[:, :], 1.0))
            link(GP.affine_select(out=blkm[:, :], in_=blkm[:, :], compare_op=ALU.is_ge, fill=0.0, base=0,
                                  pattern=[[-GH, 8]], channel_multiplier=1))
            link(GP.affine_select(out=blkm[:, :], in_=blkm[:, :], compare_op=ALU.is_ge, fill=0.0, base=GH - 1,
                                  pattern=[[GH, 8]], channel_multiplier=-1))
            link(GP.memset(neg_half[:, :], -0.5))
            split = Splitter(GP, "pool")
            GP.sem_inc(consts_ready, 1)

            def rms(src, dst, ready, done):
                for t in range(TT):
                    note(ready, 1)
                    link(GP.tensor_scalar(dst[:, t:t + 1], src[:, t:t + 1], 1.0 / D, RMS_EPS, ALU.mult, ALU.add))
                    GP.tensor_tensor(dst[:, t:t + 1], dst[:, t:t + 1], neg_half[:, 0:1], ALU.pow).then_inc(done, 1)

            def h_rms():
                rms(ssq, rstd, ssq_ready, rstd_ready)

            h_rms()
            rms(mssq, mrstd, mssq_ready, mrstd_ready)
            note(trig_seed, 1)
            for i in (2, 3):
                trig(GP, link, 0, i, [ptmp[:, k, :, :].rearrange("p j n -> p (j n)") for k in range(2)], w2, 1)
                GP.sem_inc(trig_pool, 1)
            for l in range(L):
                if l > 0:
                    h_rms()
                for p in range(PAIRS):
                    kind, n = FILLERS[p]
                    m_to = splits_before(TRUNK.bound[(kind, l, n, 1)] + AHEAD)
                    note(rot_in, 4)
                    GP.tensor_tensor(tp[:, 0, :], tp[:, 0, :], tp[:, 1, :], ALU.add).then_inc(rin_ready, 1)
                    GP.tensor_tensor(tp[:, 2, :], tp[:, 2, :], tp[:, 3, :], ALU.subtract).then_inc(rin_ready, 1)
                    split.to(max(split.m, m_to - 1))
                    note(rot_out, 4)
                    q = l * PAIRS + p
                    if q >= 1:
                        pool.wait_ge(y_done, q)
                    GP.tensor_tensor(hst[:, 0, :], tp[:, 0, :], tp[:, 1, :], ALU.subtract).then_inc(hst_ready, 1)
                    GP.tensor_tensor(hst[:, 1, :], tp[:, 3, :], tp[:, 2, :], ALU.add).then_inc(hst_ready, 1)
                    split.to(m_to)
                split.upto(("zg", l, 0, 1))
                note(var_ready, 1)
                GP.tensor_tensor(tp[:, 2, TT:2 * TT], tp[:, 2, 0:TT], neg_half[:, 0:1].to_broadcast([P, TT]),
                                 ALU.pow).then_inc(pow_ready, 1)
                if l == 0:
                    pool.wait_ge(y_done, PAIRS)
                    load_bc(1)
                split.upto(("out", l, 1, 1))
                h_rms()
                split.upto(("o", l, 1, 1))
                h_rms()
                if l == 0:
                    for i in range(4):
                        trig(GP, link, 1, i, [ptmp[:, k, :, :].rearrange("p j n -> p (j n)") for k in range(2)], w2, 1)
                        GP.sem_inc(trig_pool, 1)
                    split.upto(("fdn", len(FPIECE_END) - 1, 1, 1))
            split.to(len(SPLIT_AT))
            link(GP.affine_select(out=tri, in_=ones[:, :], compare_op=ALU.is_gt, fill=0.0, base=0,
                                  pattern=[[1, P]], channel_multiplier=-1))
            link(GP.iota(iota_i, pattern=[[1, P]], base=0, channel_multiplier=0))
            link(GP.tensor_copy(iota, iota_i))
            GP.sem_inc(late_consts, 1)
            pool.dma_start(fgain, a["norm_ffn_g"][L - 1:L, :].to_broadcast([P, D])).then_inc(late_loaded, 16)
            pool.dma_start(rw, a["router_w"][0].rearrange("(k p) n -> p k n", p=P)).then_inc(late_loaded, 16)
            pool.dma_start(rb, a["router_b"][0:1, :].to_broadcast([P, NE])).then_inc(late_loaded, 16)
            pool.dma_start(fg, a["final_norm_g"].unsqueeze(0).to_broadcast([P, D])).then_inc(late_loaded, 16)

            def expert(it):
                for u in range(HSLOTS, EH + HSLOTS):
                    split.expert(it, u)

            split.first_experts()
            pool.wait_ge(over_ready, 1)
            most = pool.value_load(over[0:1, 0:1], min_val=0, max_val=T)
            with pool.Fori(0, NE) as e:
                expert(e)
            with pool.If(most > P):
                with pool.Fori(0, NE) as e:
                    expert(e + NE)
            h_rms()


_INS = ["x", "mem", "mem_norm_g", "norm_mix_g", "w_in", "conv_w", "conv_b", "conv_ln_g", "conv_ln_b", "w_conv_pw",
        "ssm_lambda_re", "ssm_lambda_im", "ssm_log_dt", "ssm_b_re", "ssm_b_im", "ssm_c_re", "ssm_c_im", "ssm_d",
        "w_ssm_glu", "w_out", "norm_xattn_g", "w_q", "w_kv", "w_o", "norm_ffn_g", "ffn_w_gate_up", "ffn_w_down",
        "router_w", "router_b", "moe_w_gate_up", "moe_w_down", "final_norm_g"]


def kernel(**inputs):
    import numpy as np
    import concourse.bacc as bacc
    from concourse.bass_utils import run_bass_kernel_spmd

    nc = bacc.Bacc("TRN2", target_bir_lowering=False, num_devices=1)
    arrays, aps = {}, {}
    for name in _INS:
        x = np.ascontiguousarray(inputs[name])
        arrays[f"in_{name}"] = x
        aps[name] = nc.dram_tensor(f"in_{name}", x.shape, mybir.dt.from_np(x.dtype), kind="ExternalInput").ap()
    out = nc.dram_tensor("out_dram", (1, T, D), F32, kind="ExternalOutput").ap()
    trunk_kernel(nc, aps, out)
    r = run_bass_kernel_spmd(nc, [arrays], core_ids=[0])
    return r.results[0]["out_dram"]
```

```python
import math
from contextlib import ExitStack

import concourse.bass as bass
from concourse import mybir

F32 = mybir.dt.float32
F32R = mybir.dt.float32r
I32 = mybir.dt.int32
U32 = mybir.dt.uint32
ALU = mybir.AluOpType
ACT = mybir.ActivationFunctionType
AX_X = mybir.AxisListType.X

P = 128
T = 256
TT = T // P
D = 1024
KD = D // P
L = 2
CW = 512
CT_ = CW // P
TAPS = 31
PAD = TAPS - 1
G = 32
GH = 16
NS = 64
ST = G * NS // P
PAIRS = ST // 2
H = 4
HD = D // H
FF = 2816
FE = 3584
NE = 8
BLK = 512
CHUNK = 2048
HALF = CHUNK // 2
RAW = 3
RAW_E = 7
SPLITS = 3
AHEAD = 2
RING_BANKS = 6
CONV_DVE = CT_ - 1
TAPS_FIRST = 12
C0 = 2 * CW
C1 = C0 + G * GH
RMS_EPS = 1e-6
LN_EPS = 1e-5
FBLK = FF // 256
EBLK = FE // 256
MAGIC = 12582912.0
TWO_PI_A = 6.28125
TWO_PI_B = 0.0019350051879882812
TWO_PI_C = 2 * math.pi - TWO_PI_A - TWO_PI_B
PI_BELOW = 3.1415925

ROW_MIX, ROW_X, ROW_FFN, ROW_CB, ROW_LG, ROW_LB, ROW_D, ROW_MEM = 0, 8, 16, 24, 28, 32, 36, 40
ROW_LR, ROW_LI, ROW_DT = 48, 64, 96
ROWS = 112


SMALL = ["ldt", "lr", "li", "dt", "lrdt", "lidt", "mag", "ang", "aabs", "s1", "c1", "ar", "ai", "xr", "den",
         "rden", "kr", "ki", "t1", "t2", "rnd", "c128", "s128"]


class Plan:

    def __init__(self, first=0, first_part=0):
        self.first, self.part = first, first_part
        self.names, self.chunks, self.bound = [], [], {}

    def add(self, names, chunks=()):
        self.names += names
        for i, (src, split, low) in enumerate(chunks):
            if i < len(chunks) - 1:
                self.part += 1
                done = ("part", self.part)
            else:
                done = ("mm", self.first + len(self.names))
            self.chunks.append((src, split, low, done))
        for name in names:
            self.bound[name] = len(self.chunks)


def make_plan():
    plan = Plan()
    add = plan.add
    shared = ("dve", "pool")
    for l in range(L):
        for i in range(4):
            add([("hT", l, i)])
        for kind, n0 in (("cg", CW), ("ca", 0), ("us", C0)):
            for i in range(2):
                add([(kind, l, i)], [(("c", "w_in", l, n0 + 256 * i), True, "dve")])
        for kind in ("bd", "ct"):
            for r in range(2):
                add([(kind, l, r)])
        if l == 0:
            for i in range(4):
                add([("memT", i)])
        for p in range(PAIRS):
            for s in range(2):
                add([("bu", l, p, s)])
            kind, n = FILLERS[p]
            if kind == "k":
                for i in range(2):
                    add([("k", l, n, i)], [(("c", "w_kv", l, BLK * n + 256 * i), False, None)])
            elif kind == "v":
                add([("v", l, n, t) for t in range(TT)], [(("a", "w_kv", l, D + BLK * n, c), False, None) for c in range(2)])
            else:
                add([("gt", l, n, t) for t in range(TT)],
                    [(("a", "w_in", l, C1 + BLK * n, c), True, ("pool", "dve")[c]) for c in range(2)])
        add([("mean", l)])
        for n in range(2):
            for kind, n0, low in (("zg", D, "dve"), ("za", 0, "pool")):
                if n == 0 and kind == "za":
                    add([("var", l)])
                add([(kind, l, n, t) for t in range(TT)], [(("a", "w_ssm_glu", l, n0 + BLK * n, 0), True, low)])
            if n == 0:
                add([("rs", l)])
        for n in range(2):
            add([("ya", l, n, t) for t in range(TT)], [(("a", "w_conv_pw", l, BLK * n, 0), True, "pool")])
        for i in range(4):
            add([("mT", l, i)])
        for n in range(2):
            add([("out", l, n, t) for t in range(TT)],
                [(("a", "w_out", l, BLK * n, c), True, shared[c]) for c in range(2)])
        for i in range(4):
            add([("hT2", l, i)])
        for kind, h in ATTENTION:
            add([(kind, l, h)], [(("c", "w_q", l, HD * h), True, shared[h % 2])] if kind == "q" else ())
        for n in range(2):
            add([("o", l, n, t) for t in range(TT)], [(("a", "w_o", l, BLK * n, c), True, shared[c]) for c in range(2)])
        for i in range(4):
            add([("hT3", l, i)])
        if l == 0:
            for b in range(FBLK + 1):
                if b < FBLK:
                    add([("fgu", b, t) for t in range(TT)], [(("fgu", b, c), True, "dve") for c in range(2)])
                if b >= 1:
                    add([("fT", b - 1)])
                if b in FPIECE_END:
                    k = FPIECE_END.index(b)
                    lo = FPIECE_END[k - 1] if k else 0
                    add([("fdn", k, t, n) for t in range(TT) for n in range(2)],
                        [(("fdn", c), True, "dve") for c in range(lo, b)])
    add([("rt",)])
    add([("pos",)])
    loop = Plan(len(plan.names), plan.part)
    add = loop.add

    def gu(b):
        add([("gu", b)], [(("egu", b, c), True, None) for c in range(2) for _ in range(2)])

    def down(k):
        lo, hi = EPIECES[k]
        add([("edn", k, n) for n in range(2)], [(("edn", c), True, None) for c in range(lo, hi) for _ in range(2)])

    gu(0)
    for b in range(1, EBLK):
        gu(b)
        if b % 2 == 0:
            add([("eT", b // 2 - 1)])
        if b == EPIECES[0][1] + 1:
            down(0)
    add([("eT", EBLK // 2 - 1)])
    add([("gT",)])
    down(1)
    for t in range(TT):
        for n in range(2):
            add([("add", t, n)])
    return plan, loop


FILLERS = [("v", 0), ("gt", 0), ("v", 1), ("gt", 1), ("k", 0), ("gt", 2), ("k", 1), ("gt", 3)]
ATTENTION = [("q", 0), ("q", 1), ("sc", 0), ("q", 2), ("sc", 1), ("pT", 0), ("q", 3), ("sc", 2), ("sc", 3), ("oT", 0),
             ("pT", 1), ("pT", 2), ("oT", 1), ("pT", 3), ("oT", 2), ("oT", 3)]
FPIECE_END = (4, 8, 11)
EPIECES = ((0, 8), (8, 14))
TRUNK, EXPERT = make_plan()
PLAN, LOOP = TRUNK.names, EXPERT.names
AT = {name: i for i, name in enumerate(PLAN)}
LAT = {name: len(PLAN) + j for j, name in enumerate(LOOP)}
PER = len(LOOP)
PPER = EXPERT.part - TRUNK.part
assert PER % RING_BANKS == 0
CHUNKS, ECHUNKS = TRUNK.chunks, EXPERT.chunks
EH = len(ECHUNKS)
EC = EH // 2
HSLOTS = 2 * SPLITS
AHEAD_H = 4
assert EC % RAW_E == 0 and EH % HSLOTS == 0
ELOW = ["pool" if u // 2 % 4 == 3 else "dve" for u in range(EH)]
SPLIT_AT = [n for n, ch in enumerate(CHUNKS) if ch[1]]
LOW_COUNT = {}
for _who in ("dve", "pool"):
    for _k, _n in enumerate([n for n in SPLIT_AT if CHUNKS[n][2] == _who]):
        LOW_COUNT[_n] = _k + 1
LOW_TOTAL = {who: sum(1 for n in SPLIT_AT if CHUNKS[n][2] == who) for who in ("dve", "pool")}
ELOW_PER = {who: ELOW.count(who) for who in ("dve", "pool")}
ELOW_COUNT = [ELOW[:u + 1].count(ELOW[u]) for u in range(EH)]


def splits_before(n):
    return sum(1 for k in SPLIT_AT if k < n)


class Signal:

    def __init__(self, sem):
        self.sem, self.n = sem, 0

    def by(self, ins, k=1):
        ins.then_inc(self.sem, k)
        self.n += k
        return self.n


def trunk_kernel(nc, a, out):
    with ExitStack() as ctx:
        def sb(name, shape, dt=F32):
            return ctx.enter_context(nc.sbuf_tensor(name, shape, dt))

        def sem(name):
            return ctx.enter_context(nc.semaphore(name))

        ring = sb("ring", [P, RAW, CHUNK])
        w_hi = sb("w_hi", [P, SPLITS, CHUNK], F32R)
        w_lo = sb("w_lo", [P, SPLITS, CHUNK], F32R)
        x_hi = sb("x_hi", [P, KD, T], F32R)
        x_lo = sb("x_lo", [P, KD, T], F32R)
        a_hi = sb("a_hi", [P, KD, T], F32R)
        a_lo = sb("a_lo", [P, KD, T], F32R)
        h = sb("h", [P, TT, D])
        hn = sb("hn", [P, TT, D])
        memT = sb("memT", [P, KD, T])
        v = sb("v", [P, TT, D])
        trigT = sb("trigT", [P, 2, 2, ST // 2, P])
        kT = trigT[:, 0, :, :, :].rearrange("p a j n -> p (a j n)").rearrange("p (k n) -> p k n", k=KD)
        ident = sb("ident", [P, P])
        ones = sb("ones", [P, P])
        neg_half = sb("neg_half", [P, 1])
        half_pi = sb("half_pi", [P, 1])
        cols = sb("cols", [P, L, P])
        gain_row = sb("gain_row", [KD, P])
        gain_col = sb("gain_col", [P, KD])
        taps = sb("taps", [P, L, TAPS * CT_])
        ptmp = sb("ptmp", [P, 4, 4 * P // 2])
        bnd = sb("bnd", [P, 6, 2])
        sm = sb("sm", [P, len(SMALL), L * ST])
        w2 = sb("w2", [P, 2, 5, ST // 2])
        blkm = sb("blkm", [P, 8])
        evod = sb("evod", [P, 2])
        ssq = sb("ssq", [P, TT, 2])
        rstd = sb("rstd", [P, TT])
        mssq = sb("mssq", [P, TT])
        mrstd = sb("mrstd", [P, TT])
        smx = sb("smx", [P, H, TT])
        snb = sb("snb", [P, H, TT])
        ssum = sb("ssum", [P, H, TT])
        srec = sb("srec", [P, H, TT])
        dtq = sb("dtq", [P, L, 2])
        ARENA = 11400
        arena = sb("arena", [P, ARENA])

        class Area:

            def __init__(self):
                self.at = 0

            def cut(self, n):
                self.at += n
                assert self.at <= ARENA, self.at
                return arena[:, self.at - n:self.at]

        mx = Area()
        gates = mx.cut(TT * 2 * D).rearrange("p (t n) -> p t n", t=TT)
        upad = mx.cut(CT_ * (PAD + T)).rearrange("p (c n) -> p c n", c=CT_)
        conv = mx.cut(CT_ * T).rearrange("p (c n) -> p c n", c=CT_)
        tp = mx.cut(4 * 512).rearrange("p (i n) -> p i n", i=4)
        bdT = mx.cut(2 * CT_ * P).rearrange("p (r i n) -> p r i n", r=2, i=CT_)
        bc = mx.cut(2 * CT_ * P)
        cT = bc.rearrange("p (r i n) -> p r i n", r=2, i=CT_)
        hst = mx.cut(2 * 512).rearrange("p (i n) -> p i n", i=2)
        us = hn[:, 0, :].rearrange("p (c n) -> p c n", c=CT_)
        yT = hn[:, 1, :].rearrange("p (c n) -> p c n", c=CT_)
        braw = bc[:, 0:512].rearrange("p (r j h) -> p r j h", r=2, j=ST)
        craw = bc[:, 512:1024].rearrange("p (r i n) -> p r i n", r=2, i=CT_)
        tg = hst
        y_hi, y_lo = a_hi[:, 0:CT_, :], a_lo[:, 0:CT_, :]
        u_hi, u_lo = a_hi[:, CT_:KD, :], a_lo[:, CT_:KD, :]
        bd = gates[:, 0, 0:1024].rearrange("p (r j q h) -> p r j q h", r=2, j=ST, q=2)
        xc = gates[:, 0, 1024:2048].rearrange("p (m q n) -> p m q n", m=8, q=2)
        bt = gates[:, 1, 0:512].rearrange("p (i j h) -> p i j h", i=2, j=ST)
        merged = hn

        xa = Area()
        qT = xa.cut(KD * T).rearrange("p (k n) -> p k n", k=KD)
        prob = xa.cut(H * TT * T).rearrange("p (h t n) -> p h t n", h=H, t=TT)
        pT = xa.cut(H * TT * T).rearrange("p (h m n) -> p h m n", h=H, m=TT)

        fa = Area()
        sil = fa.cut(4 * 256).rearrange("p (b n) -> p b n", b=4)
        h1 = fa.cut(4 * 256).rearrange("p (b n) -> p b n", b=4)
        xTf = fa.cut(KD * T).rearrange("p (k n) -> p k n", k=KD)
        fa.at = max(fa.at, xa.at)
        tri = fa.cut(P)
        iota = fa.cut(P)
        iota_i = fa.cut(P).bitcast(I32)
        fgain = fa.cut(D)
        xg_hi = x_hi[:, 0:KD // 2, :].rearrange("p k (a n) -> p (k a) n", a=2)
        xg_lo = x_lo[:, 0:KD // 2, :].rearrange("p k (a n) -> p (k a) n", a=2)
        e_hi = a_hi[:, :, :].rearrange("p k (a n) -> p (k a) n", a=2)
        e_lo = a_lo[:, :, :].rearrange("p k (a n) -> p (k a) n", a=2)
        pick = fa.cut(TT * P).rearrange("p (t n) -> p t n", t=TT)
        pickg = fa.cut(TT * P).rearrange("p (t n) -> p t n", t=TT)
        gT = fa.cut(TT * P).rearrange("p (t n) -> p t n", t=TT)
        ye = fa.cut(D)
        rw = fa.cut(KD * NE).rearrange("p (k n) -> p k n", k=KD)
        rb = fa.cut(NE)
        lg = fa.cut(TT * NE).rearrange("p (t n) -> p t n", t=TT)
        top = fa.cut(TT * 8).rearrange("p (t n) -> p t n", t=TT)
        topi = fa.cut(TT * 8).rearrange("p (t n) -> p t n", t=TT)
        oneh = fa.cut(2 * TT * NE).rearrange("p (i t n) -> p i t n", i=2, t=TT)
        tw = fa.cut(4 * TT).rearrange("p (i t) -> p i t", i=4)
        mask = fa.cut(TT * 17).rearrange("p (t n) -> p t n", t=TT)
        gate = fa.cut(TT * 17).rearrange("p (t n) -> p t n", t=TT)
        slot = fa.cut(TT * 17).rearrange("p (t n) -> p t n", t=TT)
        fg = fa.cut(D)
        tot = fa.cut(2)
        topu = sb("topu", [P, TT, 8], U32)
        over = sb("over", [P, 1], I32)
        prow = arena[:, 0:L * 2 * P].rearrange("p (l m n) -> p l m n", l=L, m=2)
        mem = v[:, :, :]
        raw_e = [ring[:, i, :] for i in range(RAW)] + [memT[:, :, :].rearrange("p k n -> p (k n)"),
                                                       v[:, :, :].rearrange("p t n -> p (t n)"),
                                                       kT.rearrange("p k n -> p (k n)"),
                                                       trigT[:, 1, :, :, :].rearrange("p a j n -> p (a j n)")]

        ps = ctx.enter_context(nc.psum_tensor("ps", [P, 8, 512], F32))

        def bank(i):
            return ps[:, i % RING_BANKS, :]

        raw_loaded = [sem(f"raw_loaded{i}") for i in range(RAW)]
        e_loaded = [sem(f"e_loaded{i}") for i in range(RAW_E)]
        part_done = sem("part_done")
        hi_done = sem("hi_done")
        low_done = {"dve": sem("low_done_dve"), "pool": sem("low_done_pool")}
        mm_done = sem("mm_done")
        bank_free = [sem(f"bank_free{i}") for i in range(RING_BANKS)]
        x_loaded = sem("x_loaded")
        mem_loaded = sem("mem_loaded")
        rows_loaded = sem("rows_loaded")
        bc_loaded = sem("bc_loaded")
        late_loaded = sem("late_loaded")
        rows_cleared = sem("rows_cleared")
        consts_ready = sem("consts_ready")
        rows_ready = sem("rows_ready")
        gain_loaded = sem("gain_loaded")
        gain_done = sem("gain_done")
        gain_ready = sem("gain_ready")
        par_done = sem("par_done")
        cols_ready = sem("cols_ready")
        ssm_act = sem("ssm_act")
        ssm_arg = sem("ssm_arg")
        trig_seed = sem("trig_seed")
        trig_pool = sem("trig_pool")
        bd_ready = sem("bd_ready")
        bdT_ready = sem("bdT_ready")
        cT_ready = sem("cT_ready")
        h_ready = sem("h_ready")
        ssq_ready = sem("ssq_ready")
        rstd_ready = sem("rstd_ready")
        hn_ready = sem("hn_ready")
        mssq_ready = sem("mssq_ready")
        mrstd_ready = sem("mrstd_ready")
        mn_ready = sem("mn_ready")
        x_hi_ready = sem("x_hi_ready")
        x_lo_ready = sem("x_lo_ready")
        memT_act = sem("memT_act")
        memT_dve = sem("memT_dve")
        tanh_ready = sem("tanh_ready")
        tanh_used = sem("tanh_used")
        us_ready = sem("us_ready")
        gates_ready = sem("gates_ready")
        kv_ready = sem("kv_ready")
        rot_in = sem("rot_in")
        rin_ready = sem("rin_ready")
        gelu_ready = sem("gelu_ready")
        y_hi_ready = sem("y_hi_ready")
        y_lo_ready = sem("y_lo_ready")
        u32_ready = sem("u32_ready")
        u_hi_ready = sem("u_hi_ready")
        u_lo_ready = sem("u_lo_ready")
        xTf_ready = sem("xTf_ready")
        late_consts = sem("late_consts")
        gained_ready = sem("gained_ready")
        ga_done = sem("ga_done")
        ga_read = sem("ga_read")
        xg_hi_ready = sem("xg_hi_ready")
        xg_lo_ready = sem("xg_lo_ready")
        a_hi_ready = sem("a_hi_ready")
        a_lo_ready = sem("a_lo_ready")
        rot_out = sem("rot_out")
        hst_ready = sem("hst_ready")
        y_done = sem("y_done")
        y_read = sem("y_read")
        ypre_ready = sem("ypre_ready")
        conv_step = sem("conv_step")
        upad_ready = sem("upad_ready")
        product_ready = sem("product_ready")
        product_added = sem("product_added")
        conv_ready = sem("conv_ready")
        xc_ready = sem("xc_ready")
        sq_ready = sem("sq_ready")
        var_ready = sem("var_ready")
        pow_ready = sem("pow_ready")
        lnr_ready = sem("lnr_ready")
        lnz_ready = sem("lnz_ready")
        lnt_ready = sem("lnt_ready")
        merged_ready = sem("merged_ready")
        q_ready = sem("q_ready")
        nb_ready = sem("nb_ready")
        exp_ready = sem("exp_ready")
        prob_ready = sem("prob_ready")
        pT_ready = sem("pT_ready")
        sil_ready = sem("sil_ready")
        h1_ready = sem("h1_ready")
        topd_ready = sem("topd_ready")
        tope_ready = sem("tope_ready")
        mask_ready = sem("mask_ready")
        over_ready = sem("over_ready")
        pick_ready = sem("pick_ready")
        pickg_ready = sem("pickg_ready")
        gT_ready = sem("gT_ready")
        ye_ready = sem("ye_ready")
        out_ready = sem("out_ready")
        out_stored = sem("out_stored")
        dve_step = sem("dve_step")
        pool_step = sem("pool_step")

        block = ctx.enter_context(nc.Block())

        def wait_bank(eng, i):
            if i >= RING_BANKS:
                eng.wait_ge(bank_free[i % RING_BANKS], i // RING_BANKS)

        def freed(ins, i):
            ins.then_inc(bank_free[i % RING_BANKS], 1)

        def y_skip(dve, link, note, l, i):
            V = nc.vector
            u = l * CT_ + i
            dve.wait_ge(y_done, l * PAIRS + 2 * i + 2)
            link(V.scalar_tensor_tensor(yT[:, i, :], us[:, i, :], cols[:, l, ROW_D + i:ROW_D + i + 1],
                                        ps[:, 6 + u % 2, 0:T], ALU.mult, ALU.add))
            V.sem_inc(y_read, 1)
            V.sem_inc(ypre_ready, 1)

        def norm_gain(l, row, k):
            return gain_col[:, k:k + 1] if (l, row) == (0, ROW_MIX) else cols[:, l, row + k:row + k + 1]

        def conv_add(E, l, c, k):
            w, src = taps[:, l, k * CT_ + c:k * CT_ + c + 1], upad[:, c, k:k + T]
            if k == 0:
                return E.tensor_scalar(conv[:, c, :], src, w, cols[:, l, ROW_CB + c:ROW_CB + c + 1], ALU.mult, ALU.add)
            return E.scalar_tensor_tensor(conv[:, c, :], src, w, conv[:, c, :], ALU.mult, ALU.add)

        def residual(kind, l, dve, note, result, link, free_bank):
            V = nc.vector
            for n_ in range(2):
                for t in range(TT):
                    n = (kind, l, n_, t)
                    o = result(n)
                    dst = h[:, t, n_ * BLK:(n_ + 1) * BLK]
                    link(V.tensor_tensor(dst, dst, o, ALU.add))
                    free_bank(n)
                    V.sem_inc(h_ready, 1)

        def trig(E, step, settle, l, j0, count, tmp, m, n0=1, n1=P):
            S = {name: sm[:, k, :] for k, name in enumerate(SMALL)}
            jj = slice(j0 % (ST // 2), j0 % (ST // 2) + count)
            c, s = (trigT[:, j0 // (ST // 2), k, jj, :] for k in range(2))
            js = slice(l * ST + j0, l * ST + j0 + count)
            c1, s1, c128, s128 = (S[n][:, js].unsqueeze(2) for n in ("c1", "s1", "c128", "s128"))
            if n0 == 1:
                step(E.memset(c[:, :, 0:1], 1.0))
                step(E.memset(s[:, :, 0:1], 0.0))
                step(E.tensor_copy(c[:, :, 1:2], c1))
                step(E.tensor_copy(s[:, :, 1:2], s1))
                settle()
            n = max(n0, 2)
            while n < n1 or n == n1 == P:
                ch, sh = c[:, :, n // 2:n // 2 + 1], s[:, :, n // 2:n // 2 + 1]
                wc, ws, x, y, z = (w2[:, m, k, 0:count].unsqueeze(2) for k in range(5))
                if n == P:
                    wc, ws = c128, s128
                step(E.tensor_tensor(x, ch, ch, ALU.mult))
                step(E.tensor_tensor(y, sh, sh, ALU.mult))
                step(E.tensor_tensor(z, ch, sh, ALU.mult))
                settle()
                step(E.tensor_tensor(wc, x, y, ALU.subtract))
                step(E.tensor_tensor(ws, z, z, ALU.add))
                settle()
                if n < P:
                    c_wc, s_ws, c_ws, s_wc = (t[:, 0:count * n].rearrange("p (j n) -> p j n", j=count) for t in tmp)
                    wcb, wsb = wc.to_broadcast([P, count, n]), ws.to_broadcast([P, count, n])
                    step(E.tensor_tensor(c_wc, c[:, :, 0:n], wcb, ALU.mult))
                    step(E.tensor_tensor(s_ws, s[:, :, 0:n], wsb, ALU.mult))
                    step(E.tensor_tensor(c_ws, c[:, :, 0:n], wsb, ALU.mult))
                    step(E.tensor_tensor(s_wc, s[:, :, 0:n], wcb, ALU.mult))
                    settle()
                    step(E.tensor_tensor(c[:, :, n:2 * n], c_wc, s_ws, ALU.subtract))
                    step(E.tensor_tensor(s[:, :, n:2 * n], c_ws, s_wc, ALU.add))
                    settle()
                n *= 2

        def source(src, e=None):
            def tiles(w):
                return w.rearrange("(k p) n -> p k n", p=P)

            kind = src[0]
            if kind == "a":
                _, name, l, n0, c = src
                return 4, [(0, tiles(a[name][l])[:, 4 * c:4 * c + 4, n0:n0 + BLK])]
            if kind == "c":
                _, name, l, n0 = src
                return 8, [(0, tiles(a[name][l])[:, :, n0:n0 + 256])]
            if kind in ("fgu", "egu"):
                _, b, c = src
                w, f = (a["ffn_w_gate_up"][0], FF) if kind == "fgu" else (a["moe_w_gate_up"][0, e], FE)
                return 4, [(256 * g, tiles(w)[:, 4 * c:4 * c + 4, g * f + 256 * b:g * f + 256 * b + 256])
                           for g in range(2)]
            c = src[1]
            w = a["ffn_w_down"][0] if kind == "fdn" else a["moe_w_down"][0, e]
            return 2, [(0, tiles(w)[:, 2 * c:2 * c + 2, :])]

        half_hi = w_hi[:, :, :].rearrange("p s (a n) -> p (s a) n", a=2)
        half_lo = w_lo[:, :, :].rearrange("p s (a n) -> p (s a) n", a=2)

        def load(eng, slot, sema, k, parts):
            view = slot.rearrange("p (k n) -> p k n", k=k)
            for c0, src in parts:
                eng.dma_start(view[:, :, c0:c0 + src.shape[2]], src).then_inc(sema, 32 // len(parts))

        def done_wait(eng, done):
            eng.wait_ge(part_done if done[0] == "part" else mm_done, done[1])

        def e_done_wait(eng, it, u):
            kind, n = ECHUNKS[u % EH][3]
            per = PPER if kind == "part" else PER
            eng.wait_ge(part_done if kind == "part" else mm_done, it * per + (n - (per if u < 0 else 0)))

        def low_wait(eng, n):
            eng.wait_ge(low_done[CHUNKS[n][2]], LOW_COUNT[n])

        def e_low_wait(eng, it, u):
            who = ELOW[u % EH]
            n = LOW_TOTAL[who] + ELOW_COUNT[u % EH] - (ELOW_PER[who] if u < 0 else 0)
            eng.wait_ge(low_done[who], it * ELOW_PER[who] + n)

        class Splitter:

            def __init__(self, eng, who):
                self.eng, self.who, self.m = eng, who, 0

            def to(self, m_end):
                while self.m < min(m_end, len(SPLIT_AT)):
                    m, n = self.m, SPLIT_AT[self.m]
                    self.m += 1
                    if self.who == "hi":
                        if m >= SPLITS:
                            done_wait(self.eng, CHUNKS[SPLIT_AT[m - SPLITS]][3])
                        self.eng.wait_ge(raw_loaded[n % RAW], 32 * (n // RAW + 1))
                        self.eng.activation(w_hi[:, m % SPLITS, :], ring[:, n % RAW, :], ACT.Copy).then_inc(hi_done, 1)
                    elif CHUNKS[n][2] == self.who:
                        self.eng.wait_ge(hi_done, m + 1)
                        self.eng.tensor_tensor(w_lo[:, m % SPLITS, :], ring[:, n % RAW, :],
                                               w_hi[:, m % SPLITS, :].bitcast(F32),
                                               ALU.subtract).then_inc(low_done[self.who], 1)

            def upto(self, name):
                self.to(splits_before(TRUNK.bound[name] + AHEAD))

            def expert(self, it, u):
                i2, u = it + (1 if u >= EH else 0), u % EH
                c, k = divmod(u, 2)
                src = raw_e[c % RAW_E][:, k * HALF:(k + 1) * HALF]
                hi, lo = half_hi[:, u % HSLOTS, :], half_lo[:, u % HSLOTS, :]
                if self.who == "hi":
                    e_done_wait(self.eng, i2, u - HSLOTS)
                    if k == 0:
                        self.eng.wait_ge(e_loaded[c % RAW_E], i2 * (32 * EC // RAW_E) + 32 * (c // RAW_E + 1))
                    self.eng.activation(hi, src, ACT.Copy).then_inc(hi_done, 1)
                elif ELOW[u] == self.who:
                    self.eng.wait_ge(hi_done, i2 * EH + (len(SPLIT_AT) + u + 1))
                    self.eng.tensor_tensor(lo, src, hi.bitcast(F32), ALU.subtract).then_inc(low_done[self.who], 1)

            def first_experts(self, u0=0, u1=HSLOTS):
                for u in range(u0, u1):
                    c, k = divmod(u, 2)
                    if self.who == "hi":
                        if k == 0:
                            done_wait(self.eng, CHUNKS[SPLIT_AT[len(SPLIT_AT) - SPLITS + c]][3])
                            self.eng.wait_ge(e_loaded[c], 32)
                        self.eng.activation(half_hi[:, u, :], raw_e[c][:, k * HALF:(k + 1) * HALF],
                                            ACT.Copy).then_inc(hi_done, 1)
                    else:
                        self.expert(0, u)

        @block.sync
        def _(sp):
            sp.dma_start(h[:, :, :], a["x"][0].rearrange("(t p) n -> p t n", p=P)).then_inc(x_loaded, 16)
            for n, (src, split, _, _) in enumerate(CHUNKS):
                if n == 1:
                    sp.wait_ge(rows_loaded, 16 * 12)
                if n >= RAW:
                    before = CHUNKS[n - RAW]
                    if before[1]:
                        low_wait(sp, n - RAW)
                    else:
                        done_wait(sp, before[3])
                load(sp, ring[:, n % RAW, :], raw_loaded[n % RAW], *source(src))

            def expert_chunk(e, it, c):
                e_low_wait(sp, it, 2 * (c - RAW_E) + 1)
                load(sp, raw_e[c % RAW_E], e_loaded[c % RAW_E], *source(ECHUNKS[2 * c][0], e))

            def all_experts(it0):
                with sp.Fori(0, NE - 1) as e:
                    for c in range(SPLITS, EC):
                        expert_chunk(e, e + it0, c)
                    for c in range(SPLITS):
                        expert_chunk(e + 1, e + (it0 + 1), c)
                for c in range(SPLITS, EC):
                    expert_chunk(NE - 1, NE - 1 + it0, c)
                for c in range(SPLITS):
                    expert_chunk(0, NE + it0, c)

            for n in range(len(CHUNKS) - RAW, len(CHUNKS)):
                low_wait(sp, n)
            sp.wait_ge(mm_done, AT[("oT", L - 1, H - 1)] + 1)
            for c in range(SPLITS):
                expert_chunk(0, 0, c)
            all_experts(0)
            sp.wait_ge(over_ready, 1)
            most = sp.value_load(over[0:1, 0:1], min_val=0, max_val=T)
            with sp.If(most > P):
                all_experts(NE)
            for t in range(TT):
                sp.wait_ge(out_ready, t + 1)
                sp.dma_start(out[0, t * P:(t + 1) * P, :], hn[:, t, :]).then_inc(out_stored, 16)
            sp.wait_ge(out_stored, 16 * TT)

        @block.tensor
        def _(pe):
            task = [0]
            chunk = [0]
            sig = {}

            def need(sema, k):
                sig[id(sema)] = sig.get(id(sema), 0) + k
                pe.wait_ge(sema, sig[id(sema)])

            def begin(name):
                assert PLAN[task[0]] == name, (PLAN[task[0]], name)
                wait_bank(pe, task[0])
                task[0] += 1
                return bank(task[0] - 1)

            def end(ins):
                ins.then_inc(mm_done, 1)

            def three(o, hi, lo, w_h, w_l, start, stop, weights_move=True):
                if weights_move:
                    pe.matmul(o, hi, w_h, start=start, stop=False)
                    pe.matmul(o, hi, w_l, start=False, stop=False)
                    return pe.matmul(o, lo, w_h, start=False, stop=stop)
                pe.matmul(o, w_h, hi, start=start, stop=False)
                pe.matmul(o, w_h, lo, start=False, stop=False)
                return pe.matmul(o, w_l, hi, start=False, stop=stop)

            def next_chunk():
                n = chunk[0]
                chunk[0] += 1
                _, split, _, done = CHUNKS[n]
                if split:
                    low_wait(pe, n)
                    m = splits_before(n)
                    return w_hi[:, m % SPLITS, :], w_lo[:, m % SPLITS, :], done
                pe.wait_ge(raw_loaded[n % RAW], 32 * (n // RAW + 1))
                return ring[:, n % RAW, :], None, done

            def token_major(names, hi, lo, ktiles, fresh=None, every=2):
                os = [begin(name) for name in names]
                for c in range(ktiles // 4):
                    w_h, w_l, done = next_chunk()
                    order = [(k, t) for k in range(4) for t in range(TT)]
                    if c == ktiles // 4 - 1 and not fresh:
                        order.sort(key=lambda kt: kt[1])
                    for k, t in order:
                        kk = 4 * c + k
                        if fresh and t == 0 and kk % every == 0:
                            need(fresh, 1)
                        w = slice(k * BLK, (k + 1) * BLK)
                        tok_ = slice(t * P, (t + 1) * P)
                        start, stop = kk == 0, kk == ktiles - 1
                        if lo is None:
                            ins = pe.matmul(os[t], hi[:, kk, tok_], w_h[:, w], start=start, stop=stop)
                        else:
                            ins = three(os[t], hi[:, kk, tok_], lo[:, kk, tok_], w_h[:, w], w_l[:, w], start, stop)
                        if stop:
                            end(ins)
                    if done[0] == "part":
                        ins.then_inc(part_done, 1)

            def channel_major(names, hi, lo, fresh=False):
                for name in names:
                    o = begin(name)
                    w_h, w_l, done = next_chunk()
                    for j in range(2):
                        for k in range(KD):
                            if fresh and name == names[0] and j == 0 and k % 2 == 0:
                                need(x_lo_ready, 1)
                            w = slice(k * 256 + j * P, k * 256 + (j + 1) * P)
                            oo = o[:, j * T:(j + 1) * T]
                            if lo is None:
                                ins = pe.matmul(oo, w_h[:, w], hi[:, k, :], start=(k == 0), stop=(k == KD - 1))
                            else:
                                ins = three(oo, hi[:, k, :], lo[:, k, :], w_h[:, w], w_l[:, w], k == 0, k == KD - 1,
                                            weights_move=False)
                    end(ins)

            def transposes(names, src, ready):
                os = [begin(name) for name in names]
                for t in range(TT):
                    need(ready, 1)
                    for i, o in enumerate(os):
                        for j in range(2):
                            ins = pe.transpose(o[:, j * T + t * P:j * T + (t + 1) * P],
                                               src[:, t, (2 * i + j) * P:(2 * i + j + 1) * P], ident[:, :])
                        if t == TT - 1:
                            end(ins)

            pe.wait_ge(consts_ready, 1)
            pe.wait_ge(gain_loaded, 16)
            pe.transpose(ps[:, 7, 0:KD], gain_row[:, :], ident[0:KD, 0:KD]).then_inc(gain_done, 1)

            def parameters():
                pe.wait_ge(rows_ready, 1)
                o = ps[:, 6, :]
                for l in range(L):
                    pe.transpose(o[:, l * P:l * P + ROWS], prow[0:ROWS, l, 0, :], ident[0:ROWS, 0:ROWS])
                    ins = pe.transpose(o[:, (2 + l) * P:(2 + l) * P + TAPS * CT_], prow[0:TAPS * CT_, l, 1, :],
                                       ident[0:TAPS * CT_, 0:TAPS * CT_])
                ins.then_inc(par_done, 1)

            for l in range(L):
                transposes([("hT", l, i) for i in range(4)], hn, hn_ready)
                for kind in ("cg", "ca", "us"):
                    for i in range(2):
                        channel_major([(kind, l, i)], x_hi, x_lo, fresh=(kind == "cg" and i == 0))
                        if l == 0 and (kind, i) == ("cg", 0):
                            parameters()
                need(bd_ready, 2)
                for r in range(2):
                    o = begin(("bd", l, r))
                    for i in range(CT_):
                        ins = pe.transpose(o[:, i * P:(i + 1) * P],
                                           bd[:, r, 4 * i:4 * i + 4, :, :].rearrange("p j q h -> p (j q h)"), ident[:, :])
                    end(ins)
                for r in range(2):
                    o = begin(("ct", l, r))
                    for i in range(CT_):
                        ins = pe.transpose(o[:, i * P:(i + 1) * P],
                                           xc[:, 4 * r + i, :, :].rearrange("p q n -> p (q n)"), ident[:, :])
                    end(ins)
                if l == 0:
                    transposes([("memT", i) for i in range(4)], mem, mn_ready)

                def y_pair(p):
                    i = p // 2
                    u = l * CT_ + i
                    if p % 2 == 0 and u >= 2:
                        pe.wait_ge(y_read, u - 1)
                    if p == 0:
                        need(cT_ready, 2)
                    need(hst_ready, 2)
                    for s in range(2):
                        jj = (2 * p + s) % 4
                        for r in range(2):
                            ins = pe.matmul(ps[32 * jj:32 * jj + 32, 6 + u % 2, 0:T], cT[:, r, i, 32 * jj:32 * jj + 32],
                                            hst[:, r, s * T:(s + 1) * T], start=(r == 0), stop=(r == 1),
                                            tile_position=(0, 32 * jj))
                    ins.then_inc(y_done, 1)

                need(us_ready, 2)
                need(bdT_ready, 2)
                for p in range(PAIRS):
                    for s in range(2):
                        o = begin(("bu", l, p, s))
                        j = 2 * p + s
                        q0 = 32 * (j % 4)
                        for r in range(2):
                            ins = pe.matmul(o[:, r * T:(r + 1) * T], bdT[q0:q0 + 32, r, j // 4, :],
                                            us[q0:q0 + 32, j // 4, :], start=True, stop=True,
                                            tile_position=(q0, 0))
                        end(ins)
                    kind, n = FILLERS[p]
                    if kind != "gt" and l == 0 and p == 0:
                        need(memT_act, 4)
                        need(memT_dve, 2)
                    if kind == "gt":
                        token_major([("gt", l, n, t) for t in range(TT)], x_hi, x_lo, KD)
                    elif kind == "k":
                        channel_major([("k", l, n, i) for i in range(2)], memT, None)
                    else:
                        token_major([("v", l, n, t) for t in range(TT)], memT, None, KD)
                    if p >= 1:
                        y_pair(p - 1)
                o = begin(("mean", l))
                need(conv_ready, 2)
                for c in range(CT_):
                    ins = pe.matmul(o[:, 0:T], ones[:, :], conv[:, c, :], start=(c == 0), stop=(c == CT_ - 1))
                end(ins)
                y_pair(PAIRS - 1)
                for n in range(2):
                    token_major([("zg", l, n, t) for t in range(TT)], y_hi, y_lo, CT_,
                                fresh=y_lo_ready if n == 0 else None, every=1)
                    if n == 0:
                        o = begin(("var", l))
                        need(sq_ready, 1)
                        sq = tp[:, 0:2, :].rearrange("p i n -> p (i n)").rearrange("p (c n) -> p c n", c=CT_)
                        for t in range(TT):
                            for c in range(CT_):
                                ins = pe.matmul(o[:, t:t + 1], sq[:, c, t * P:(t + 1) * P], ones[:, 0:1],
                                                start=(c == 0), stop=(c == CT_ - 1))
                        end(ins)
                    token_major([("za", l, n, t) for t in range(TT)], y_hi, y_lo, CT_)
                    if n == 0:
                        o = begin(("rs", l))
                        need(lnr_ready, 1)
                        for t in range(TT):
                            ins = pe.matmul(o[:, t * P:(t + 1) * P], ones[:, :], tp[:, 3, t * P:(t + 1) * P],
                                            start=True, stop=True)
                        end(ins)
                need(u_lo_ready, 1)
                for n in range(2):
                    token_major([("ya", l, n, t) for t in range(TT)], u_hi, u_lo, CT_)
                transposes([("mT", l, i) for i in range(4)], merged, merged_ready)
                for n in range(2):
                    token_major([("out", l, n, t) for t in range(TT)], x_hi, x_lo, KD, fresh=x_lo_ready if n == 0 else None)

                transposes([("hT2", l, i) for i in range(4)], hn, hn_ready)
                for kind, hh in ATTENTION:
                    if kind == "q":
                        channel_major([("q", l, hh)], x_hi, x_lo, fresh=(hh == 0))
                    elif kind == "sc":
                        o = begin(("sc", l, hh))
                        need(q_ready, 1)
                        if hh == 0:
                            need(kv_ready, 8)
                        for t in range(TT):
                            for k in range(2):
                                ins = pe.matmul(o[:, t * T:(t + 1) * T], qT[:, 2 * hh + k, t * P:(t + 1) * P],
                                                kT[:, 2 * hh + k, :], start=(k == 0), stop=(k == 1))
                        end(ins)
                    elif kind == "pT":
                        o = begin(("pT", l, hh))
                        need(prob_ready, TT)
                        for t in range(TT):
                            for m in range(TT):
                                ins = pe.transpose(o[:, m * T + t * P:m * T + (t + 1) * P],
                                                   prob[:, hh, t, m * P:(m + 1) * P], ident[:, :])
                        end(ins)
                    else:
                        o = begin(("oT", l, hh))
                        need(pT_ready, 1)
                        for dtile in range(2):
                            for m in range(TT):
                                c0 = hh * HD + dtile * P
                                ins = pe.matmul(o[:, dtile * T:(dtile + 1) * T], v[:, m, c0:c0 + P], pT[:, hh, m, :],
                                                start=(m == 0), stop=(m == TT - 1))
                        end(ins)
                for n in range(2):
                    token_major([("o", l, n, t) for t in range(TT)], a_hi, a_lo, KD, fresh=a_lo_ready if n == 0 else None)
                transposes([("hT3", l, i) for i in range(4)], hn, hn_ready)
                if l == 0:
                    for b in range(FBLK + 1):
                        if b < FBLK:
                            token_major([("fgu", b, t) for t in range(TT)], x_hi, x_lo, KD, fresh=x_lo_ready if b == 0 else None)
                        if b >= 1:
                            o = begin(("fT", b - 1))
                            need(h1_ready, TT)
                            for t in range(TT):
                                for f in range(2):
                                    ins = pe.transpose(o[:, f * T + t * P:f * T + (t + 1) * P],
                                                       h1[:, (2 * (b - 1) + t) % 4, f * P:(f + 1) * P], ident[:, :])
                            end(ins)
                        if b in FPIECE_END:
                            piece = FPIECE_END.index(b)
                            b0 = FPIECE_END[piece - 1] if piece else 0
                            os = [[begin(("fdn", piece, t, n)) for n in range(2)] for t in range(TT)]
                            for c in range(b0, b):
                                w_h, w_l, done = next_chunk()
                                need(a_lo_ready, 1)
                                order = [(k, t) for k in range(2) for t in range(TT)]
                                if c == b - 1:
                                    order.sort(key=lambda kt: kt[1])
                                for k, t in order:
                                    f = 2 * (c - b0) + k
                                    start, stop = f == 0, f == 2 * (b - b0) - 1
                                    for n in range(2):
                                        w = slice(k * D + n * BLK, k * D + (n + 1) * BLK)
                                        ins = three(os[t][n], a_hi[:, f, t * P:(t + 1) * P],
                                                    a_lo[:, f, t * P:(t + 1) * P], w_h[:, w], w_l[:, w], start, stop)
                                        if stop:
                                            end(ins)
                                if done[0] == "part":
                                    ins.then_inc(part_done, 1)

            o = begin(("rt",))
            pe.wait_ge(late_loaded, 16 * 4)
            for t in range(TT):
                for k in range(KD):
                    if t == 0 and k % 2 == 0:
                        pe.wait_ge(xTf_ready, k // 2 + 1)
                    ins = pe.matmul(o[:, t * NE:(t + 1) * NE], xTf[:, k, t * P:(t + 1) * P], rw[:, k, :],
                                    start=(k == 0), stop=(k == KD - 1))
            end(ins)
            o = begin(("pos",))
            pe.wait_ge(mask_ready, 1)
            pe.matmul(o[:, 0:NE], tri, mask[:, 0, 0:NE], start=True, stop=True)
            for base, w in ((NE, tri), (2 * NE, ones[:, :])):
                pe.matmul(o[:, base:base + NE], ones[:, :], mask[:, 0, 0:NE], start=True, stop=False)
                ins = pe.matmul(o[:, base:base + NE], w, mask[:, 1, 0:NE], start=False, stop=True)
            end(ins)

            def gather(i):
                for j in range(4):
                    k = 4 * i + j
                    for t in range(TT):
                        ins = pe.matmul(ps[:, 6 + i, j * P:(j + 1) * P], hn[:, t, k * P:(k + 1) * P], pick[:, t, :],
                                        start=(t == 0), stop=(t == TT - 1))
                ins.then_inc(ga_done, 1)

            pe.wait_ge(pick_ready, 1)
            pe.wait_ge(gained_ready, TT)
            for i in range(2):
                gather(i)
            assert task[0] == len(PLAN) and chunk[0] == len(CHUNKS)
            h1_0, a_0 = sig[id(h1_ready)], sig[id(a_lo_ready)]

            pe.wait_ge(over_ready, 1)
            most = pe.value_load(over[0:1, 0:1], min_val=0, max_val=T)

            def expert(it):
                at = [0]

                def lbegin(name):
                    i = LAT[name]
                    pe.wait_ge(bank_free[i % RING_BANKS], it * (PER // RING_BANKS) + i // RING_BANKS)
                    return bank(i)

                def loaded():
                    u = at[0]
                    at[0] += 1
                    e_low_wait(pe, it, u)
                    return half_hi[:, u % HSLOTS, :], half_lo[:, u % HSLOTS, :], ECHUNKS[u][3]

                for name in LOOP:
                    if name[0] == "gu":
                        b = name[1]
                        if b == 0:
                            pe.wait_ge(xg_lo_ready, it * 2 + 2)
                        o = lbegin(name)
                        for c in range(4):
                            w_h, w_l, done = loaded()
                            for k in range(2):
                                kk = 2 * c + k
                                w = slice(k * BLK, (k + 1) * BLK)
                                ins = three(o, xg_hi[:, kk, :], xg_lo[:, kk, :], w_h[:, w], w_l[:, w], kk == 0,
                                            kk == KD - 1)
                            ins.then_inc(part_done if done[0] == "part" else mm_done, 1)
                        if b == EBLK - 1:
                            pe.wait_ge(pick_ready, it + 2)
                            pe.wait_ge(ga_read, it * 2 + 2)
                            gather(0)
                    elif name[0] == "eT":
                        i = name[1]
                        o = lbegin(name)
                        pe.wait_ge(h1_ready, it * EBLK + (h1_0 + 2 * i + 2))
                        for b in range(2):
                            for f in range(2):
                                ins = pe.transpose(o[:, (2 * b + f) * P:(2 * b + f + 1) * P],
                                                   h1[:, (2 * i + b) % 4, f * P:(f + 1) * P], ident[:, :])
                        ins.then_inc(mm_done, 1)
                    elif name[0] == "gT":
                        o = lbegin(name)
                        pe.wait_ge(pickg_ready, it + 1)
                        for t in range(TT):
                            ins = pe.transpose(o[:, t * P:(t + 1) * P], pickg[:, t, :], ident[:, :])
                        ins.then_inc(mm_done, 1)
                    elif name[0] == "edn" and name[2] == 0:
                        piece = name[1]
                        lo, hi = EPIECES[piece]
                        os = [lbegin(("edn", piece, n)) for n in range(2)]
                        for f in range(2 * (hi - lo)):
                            if f % 4 == 0:
                                pe.wait_ge(a_lo_ready, it * (EBLK // 2) + (a_0 + (lo // 2 + f // 4 + 1)))
                            w_h, w_l, done = loaded()
                            stop = f == 2 * (hi - lo) - 1
                            for n in range(2):
                                w = slice(n * BLK, (n + 1) * BLK)
                                ins = three(os[n], e_hi[:, f, :], e_lo[:, f, :], w_h[:, w], w_l[:, w], f == 0, stop)
                                if stop:
                                    ins.then_inc(mm_done, 1)
                            if done[0] == "part":
                                ins.then_inc(part_done, 1)
                        if piece == 1:
                            gather(1)
                    elif name[0] == "add":
                        _, t, n = name
                        o = lbegin(name)
                        if t == 0 and n == 0:
                            pe.wait_ge(gT_ready, it + 1)
                            pe.wait_ge(ye_ready, it * 4 + 4)
                        pe.matmul(o, gT[:, t, :], ye[:, n * BLK:(n + 1) * BLK], start=True, stop=True).then_inc(mm_done, 1)

            with pe.Fori(0, NE) as e:
                expert(e)
            with pe.If(most > P):
                with pe.Fori(0, NE) as e:
                    expert(e + NE)

        @block.scalar
        def _(act):
            act.dma_start(gain_row[:, :], a["norm_mix_g"][0].rearrange("(r n) -> r n", n=P)).then_inc(gain_loaded, 16)
            act.wait_ge(rows_cleared, 1)
            for row, name in ((ROW_MIX, "norm_mix_g"), (ROW_X, "norm_xattn_g"), (ROW_FFN, "norm_ffn_g"),
                              (ROW_CB, "conv_b"), (ROW_LG, "conv_ln_g"), (ROW_LB, "conv_ln_b")):
                src = a[name].rearrange("l (r n) -> r l n", n=P)
                act.dma_start(prow[row:row + src.shape[0], :, 0, :], src).then_inc(rows_loaded, 16)
            act.dma_start(prow[ROW_D:ROW_D + 4, :, 0, :],
                          a["ssm_d"].rearrange("l (r g) n -> r l (g n)", r=4)).then_inc(rows_loaded, 16)
            act.dma_start(prow[ROW_MEM:ROW_MEM + 8, 0, 0, :],
                          a["mem_norm_g"].rearrange("(r n) -> r n", n=P)).then_inc(rows_loaded, 16)
            for row, name in ((ROW_LR, "ssm_lambda_re"), (ROW_LI, "ssm_lambda_im")):
                act.dma_start(prow[row:row + ST, :, 0, :],
                              a[name].rearrange("l (j q) n -> j l (q n)", q=2)).then_inc(rows_loaded, 16)
            act.dma_start(dtq[ROW_DT:ROW_DT + ST, :, :],
                          a["ssm_log_dt"].rearrange("l (j q) -> j l q", q=2)).then_inc(rows_loaded, 16)
            act.dma_start(prow[0:TAPS * CT_, :, 1, :],
                          a["conv_w"].rearrange("l k (c n) -> (k c) l n", n=P)).then_inc(rows_loaded, 16)
            act.dma_start(mem, a["mem"][0].rearrange("(t p) n -> p t n", p=P)).then_inc(mem_loaded, 16)

            done = {}
            split = Splitter(nc.scalar, "hi")

            def result(name, ahead=True):
                if ahead:
                    split.upto(name)
                act.wait_ge(mm_done, AT[name] + 1)
                return bank(AT[name])

            def note(sema, k):
                done[id(sema)] = done.get(id(sema), 0) + k
                act.wait_ge(sema, done[id(sema)])

            def free_bank(name):
                act.sem_inc(bank_free[AT[name] % RING_BANKS], 1)

            def h_sums(halves=((0, 0), (1, 0), (0, 1), (1, 1))):
                for t, n_ in halves:
                    note(h_ready, 1)
                    w = slice(n_ * BLK, (n_ + 1) * BLK)
                    nc.scalar.activation(hn[:, t, w], h[:, t, w], ACT.Square,
                                         accum_out=ssq[:, t, n_:n_ + 1]).then_inc(ssq_ready, 1)

            def x_high(kind, l, row):
                for i in range(4):
                    o = result((kind, l, i), ahead=(l, row) != (0, ROW_MIX))
                    for j in range(2):
                        k = 2 * i + j
                        nc.scalar.activation(x_hi[:, k, :], o[:, j * T:(j + 1) * T], ACT.Copy,
                                             scale=norm_gain(l, row, k)).then_inc(x_hi_ready, 1)

            def copy_out(name, dst, sema, func=ACT.Copy, scale=1.0):
                o = result(name)
                nc.scalar.activation(dst, o[:, 0:512], func, scale=scale).then_inc(sema, 1)
                note(sema, 1)
                free_bank(name)

            act.wait_ge(x_loaded, 16)
            for t in range(TT):
                for n_ in range(2):
                    w = slice(n_ * BLK, (n_ + 1) * BLK)
                    nc.scalar.activation(hn[:, t, w], h[:, t, w], ACT.Square,
                                         accum_out=ssq[:, t, n_:n_ + 1]).then_inc(ssq_ready, 1)
            split.to(1)
            act.wait_ge(gain_ready, 1)
            x_high("hT", 0, ROW_MIX)
            split.to(3)
            act.wait_ge(mem_loaded, 16)
            for t in range(TT):
                nc.scalar.activation(tp[:, 2 * t:2 * t + 2, :].rearrange("p i n -> p (i n)"), mem[:, t, :], ACT.Square,
                                     accum_out=mssq[:, t:t + 1]).then_inc(mssq_ready, 1)

            S = {n: sm[:, i, :] for i, n in enumerate(SMALL)}
            act.wait_ge(cols_ready, 3)
            nc.scalar.activation(S["dt"], S["ldt"], ACT.Exp).then_inc(ssm_act, 1)
            act.wait_ge(ssm_arg, 1)
            nc.scalar.activation(S["mag"], S["lrdt"], ACT.Exp).then_inc(ssm_act, 1)
            split.to(4)
            act.wait_ge(ssm_arg, 2)
            nc.scalar.activation(S["s1"], S["ang"], ACT.Sin).then_inc(ssm_act, 1)
            nc.scalar.activation(S["aabs"], S["ang"], ACT.Abs).then_inc(ssm_act, 1)
            act.wait_ge(ssm_act, 4)
            nc.scalar.activation(S["c1"], S["aabs"], ACT.Sin, scale=-1.0, bias=half_pi[:, 0:1]).then_inc(ssm_act, 1)

            for l in range(L):
                if l > 0:
                    h_sums(((0, 0), (0, 1), (1, 0), (1, 1)))
                    x_high("hT", l, ROW_MIX)
                for i in range(2):
                    copy_out(("cg", l, i), tg[:, i, :], tanh_ready, ACT.Tanh, 0.5)
                for i in range(2):
                    copy_out(("us", l, i), us[:, 2 * i:2 * i + 2, :].rearrange("p c n -> p (c n)"), us_ready)
                for r in range(2):
                    copy_out(("ct", l, r), cT[:, r, :, :].rearrange("p i n -> p (i n)"), cT_ready, scale=(1.0, -1.0)[r])
                if l == 0:
                    for i in (0, 2):
                        o = result(("memT", i))
                        for j in range(2):
                            k = 2 * i + j
                            nc.scalar.activation(memT[:, k, :], o[:, j * T:(j + 1) * T], ACT.Copy,
                                                 scale=cols[:, 0, ROW_MEM + k:ROW_MEM + k + 1]).then_inc(memT_act, 1)
                        note(memT_act, 2)
                        free_bank(("memT", i))
                tap = [0]

                def products(count):
                    for _ in range(min(count, TAPS - 1 - tap[0])):
                        u, k = l * (TAPS - 1) + tap[0], tap[0] + 1
                        tap[0] += 1
                        if u >= 4:
                            act.wait_ge(product_added, u - 3)
                        w = taps[:, l, k * CT_ + CT_ - 1:k * CT_ + CT_]
                        nc.scalar.activation(ptmp[:, u % 4, :], upad[:, CT_ - 1, k:k + T], ACT.Copy,
                                             scale=w).then_inc(product_ready, 1)

                act.wait_ge(upad_ready, l + 1)
                act.wait_ge(trig_pool, 2 + 4 * l)
                products(4)
                for p in range(PAIRS):
                    kind, n = FILLERS[p]
                    if kind == "k" and n == 0:
                        act.wait_ge(rot_out, 4 * (l * PAIRS + PAIRS // 2))
                    for i in range(2):
                        if kind == "gt":
                            copy_out((kind, l, n, i), gates[:, i, n * BLK:(n + 1) * BLK], gates_ready, ACT.Tanh, 0.5)
                        elif kind == "k":
                            c = 4 * n + 2 * i
                            copy_out((kind, l, n, i), kT[:, c:c + 2, :].rearrange("p c n -> p (c n)"), kv_ready)
                        else:
                            copy_out((kind, l, n, i), v[:, i, n * BLK:(n + 1) * BLK], kv_ready)
                        products(2)
                for i in range(CT_):
                    note(ypre_ready, 1)
                    nc.scalar.activation(yT[:, i, :], yT[:, i, :], ACT.Gelu_apprx_tanh).then_inc(gelu_ready, 1)
                    note(gelu_ready, 1)
                    nc.scalar.activation(y_hi[:, i, :], yT[:, i, :], ACT.Copy).then_inc(y_hi_ready, 1)
                note(xc_ready, 1)
                nc.scalar.activation(tp[:, 0:2, :].rearrange("p i n -> p (i n)"),
                                     conv[:, :, :].rearrange("p c n -> p (c n)"), ACT.Square).then_inc(sq_ready, 1)
                for n in range(2):
                    for t in range(TT):
                        u = (l * 2 + n) * TT + t
                        if u >= 2:
                            act.wait_ge(tanh_used, u - 1)
                        copy_out(("zg", l, n, t), tg[:, t, :], tanh_ready, ACT.Tanh, 0.5)
                    if n == 0:
                        split.upto(("zg", l, 1, 0))
                        note(lnz_ready, 1)
                        nc.scalar.activation(tp[:, 0:2, :].rearrange("p i n -> p (i n)"),
                                             conv[:, :, :].rearrange("p c n -> p (c n)"), ACT.Tanh,
                                             scale=0.5).then_inc(lnt_ready, 1)
                        split.upto(("za", l, 1, 0))
                        note(u32_ready, 1)
                        nc.scalar.activation(u_hi[:, :, :].rearrange("p c n -> p (c n)"),
                                             conv[:, :, :].rearrange("p c n -> p (c n)"), ACT.Copy).then_inc(u_hi_ready, 1)
                for i in range(4):
                    o = result(("mT", l, i))
                    nc.scalar.activation(x_hi[:, 2 * i:2 * i + 2, :].rearrange("p c n -> p (c n)"), o[:, 0:512], ACT.Copy,
                                         scale=0.25).then_inc(x_hi_ready, 2)
                split.upto(("out", l, 1, 1))
                h_sums()
                x_high("hT2", l, ROW_X)
                for kind, hh in ATTENTION:
                    if kind == "q":
                        copy_out(("q", l, hh), qT[:, 2 * hh:2 * hh + 2, :].rearrange("p c n -> p (c n)"), q_ready)
                    elif kind == "sc":
                        n = ("sc", l, hh)
                        split.upto(n)
                        note(nb_ready, 1)
                        for t in range(TT):
                            nc.scalar.activation(prob[:, hh, t, :], bank(AT[n])[:, t * T:(t + 1) * T], ACT.Exp,
                                                 scale=1.0 / math.sqrt(HD), bias=snb[:, hh, t:t + 1],
                                                 accum_out=ssum[:, hh, t:t + 1]).then_inc(exp_ready, 1)
                        note(exp_ready, TT)
                        free_bank(n)
                    elif kind == "oT":
                        o = result(("oT", l, hh))
                        nc.scalar.activation(a_hi[:, 2 * hh:2 * hh + 2, :].rearrange("p c n -> p (c n)"), o[:, 0:512],
                                             ACT.Copy).then_inc(a_hi_ready, 1)
                split.upto(("o", l, 1, 1))
                h_sums()
                if l == 0:
                    x_high("hT3", l, ROW_FFN)
                    for b in range(FBLK + 1):
                        for t in range(TT):
                            if b < FBLK:
                                u = 2 * b + t
                                if u >= 4:
                                    act.wait_ge(h1_ready, u - 3)
                                o = result(("fgu", b, t))
                                nc.scalar.activation(sil[:, u % 4, :], o[:, 0:256], ACT.Silu).then_inc(sil_ready, 1)
                        if b >= 1:
                            piece = [b <= x for x in FPIECE_END].index(True)
                            f = 2 * (b - 1 - (FPIECE_END[piece - 1] if piece else 0))
                            o = result(("fT", b - 1))
                            nc.scalar.activation(a_hi[:, f:f + 2, :].rearrange("p f n -> p (f n)"), o[:, 0:512],
                                                 ACT.Copy).then_inc(a_hi_ready, 1)
                    split.upto(("fdn", len(FPIECE_END) - 1, 1, 1))
                else:
                    split.to(len(SPLIT_AT))
                    split.first_experts()

            act.wait_ge(topd_ready, 1)
            nc.scalar.activation(tw[:, 1, :], tw[:, 0, :], ACT.Exp).then_inc(tope_ready, 1)
            def xg_high(i):
                nc.scalar.activation(xg_hi[:, 4 * i:4 * i + 4, :].rearrange("p k n -> p (k n)"), ps[:, 6 + i, :],
                                     ACT.Copy).then_inc(xg_hi_ready, 1)

            act.wait_ge(ga_done, 2)
            for i in range(2):
                xg_high(i)
            act.wait_ge(over_ready, 1)
            most = act.value_load(over[0:1, 0:1], min_val=0, max_val=T)
            h1_0, a_0 = 2 * FBLK, FBLK + L * H

            def expert(it):
                nxt = [HSLOTS]

                def ahead(name):
                    while nxt[0] < min(EXPERT.bound[name] + AHEAD_H, EH + HSLOTS):
                        split.expert(it, nxt[0])
                        nxt[0] += 1

                def lresult(name):
                    ahead(name)
                    act.wait_ge(mm_done, it * PER + LAT[name] + 1)
                    return bank(LAT[name])

                for name in LOOP:
                    i = LAT[name]
                    if name[0] == "gu":
                        b = name[1]
                        act.wait_ge(h1_ready, it * EBLK + (h1_0 + b - 3))
                        o = lresult(name)
                        nc.scalar.activation(sil[:, b % 4, :], o[:, 0:256], ACT.Silu).then_inc(sil_ready, 1)
                    elif name[0] == "eT":
                        o = lresult(name)
                        j = name[1]
                        f = 4 * j if 2 * j < EPIECES[0][1] else 4 * j - 2 * EPIECES[1][0]
                        nc.scalar.activation(e_hi[:, f:f + 4, :].rearrange("p f n -> p (f n)"), o[:, 0:512],
                                             ACT.Copy).then_inc(a_hi_ready, 1)
                    elif name[0] == "edn" and name[1] == 0:
                        o = lresult(name)
                        n = name[2]
                        nc.scalar.activation(ye[:, n * BLK:(n + 1) * BLK], o[:, 0:512], ACT.Copy).then_inc(ye_ready, 1)
                        act.wait_ge(ye_ready, it * 4 + n + 1)
                        act.sem_inc(bank_free[i % RING_BANKS], 1)
                    elif name[0] == "gT":
                        ahead(name)
                        act.wait_ge(ga_done, it * 2 + 3)
                        xg_high(0)
                    elif name == ("edn", 1, 1):
                        ahead(name)
                        act.wait_ge(ga_done, it * 2 + 4)
                        xg_high(1)
                while nxt[0] < EH + HSLOTS:
                    split.expert(it, nxt[0])
                    nxt[0] += 1

            with act.Fori(0, NE) as e:
                expert(e)
            with act.If(most > P):
                with act.Fori(0, NE) as e:
                    expert(e + NE)
            h_sums()

        @block.vector
        def _(dve):
            V = nc.vector
            steps = Signal(dve_step)
            cnt = {}

            def link(ins):
                dve.wait_ge(dve_step, steps.by(ins))

            def settle():
                dve.wait_ge(dve_step, steps.n)

            def note(sema, k):
                cnt[id(sema)] = cnt.get(id(sema), 0) + k
                dve.wait_ge(sema, cnt[id(sema)])

            split = Splitter(V, "dve")

            def result(name, ahead=True):
                if ahead:
                    split.upto(name)
                dve.wait_ge(mm_done, AT[name] + 1)
                return bank(AT[name])

            def free_bank(name):
                V.sem_inc(bank_free[AT[name] % RING_BANKS], 1)

            def evac(n, ins, sema=None, k=1):
                if sema is None:
                    link(ins)
                else:
                    ins.then_inc(sema, k)
                    note(sema, k)
                free_bank(n)

            def normalise(src, dst, r, rsem, ready):
                for t in range(TT):
                    note(rsem, 1)
                    V.tensor_scalar(dst[:, t, :], src[:, t, :], r[:, t:t + 1], None, ALU.mult).then_inc(ready, 1)

            def x_low(kind, l, row):
                for i in range(4):
                    o = result((kind, l, i), ahead=(l, row) != (0, ROW_MIX))
                    note(x_hi_ready, 2)
                    for j in range(2):
                        k = 2 * i + j
                        ins = V.scalar_tensor_tensor(x_lo[:, k, :], o[:, j * T:(j + 1) * T], norm_gain(l, row, k),
                                                     x_hi[:, k, :].bitcast(F32), ALU.mult, ALU.subtract)
                        if j == 0:
                            link(ins)
                    evac((kind, l, i), ins, x_lo_ready)

            def a_low(name, k):
                o = result(name)
                note(a_hi_ready, 1)
                evac(name, V.tensor_tensor(a_lo[:, k:k + 2, :].rearrange("p c n -> p (c n)"), o,
                                           a_hi[:, k:k + 2, :].rearrange("p c n -> p (c n)").bitcast(F32), ALU.subtract),
                     a_lo_ready)

            link(V.memset(prow[:, :, :, :], 0.0))
            V.sem_inc(rows_cleared, 1)
            V.memset(half_pi[:, :], math.pi / 2)
            normalise(h, hn, rstd, rstd_ready, hn_ready)
            dve.wait_ge(gain_done, 1)
            V.tensor_copy(gain_col[:, :], ps[:, 7, 0:KD]).then_inc(gain_ready, 1)
            dve.wait_ge(gain_ready, 1)
            split.to(1)
            x_low("hT", 0, ROW_MIX)
            dve.wait_ge(rows_loaded, 16 * 12)
            for l in range(L):
                ins = V.tensor_copy(prow[ROW_DT:ROW_DT + ST, l, 0, :].rearrange("p (q n) -> p q n", q=2),
                                    dtq[ROW_DT:ROW_DT + ST, l, :].unsqueeze(2).to_broadcast([ST, 2, NS]))
                link(ins)
            V.sem_inc(rows_ready, 1)
            split.to(3)
            dve.wait_ge(par_done, 1)
            o = ps[:, 6, :]
            V.tensor_copy(cols[:, :, 0:ROWS], o.rearrange("p (m n) -> p m n", m=4)[:, 0:2, 0:ROWS]).then_inc(cols_ready, 1)
            V.tensor_scalar(taps[:, :, :], o.rearrange("p (m n) -> p m n", m=4)[:, 2:4, 0:TAPS * CT_], 0.5, None,
                            ALU.mult).then_inc(cols_ready, 1)
            dve.wait_ge(cols_ready, 2)

            S = {name: sm[:, i, :] for i, name in enumerate(SMALL)}
            for name, row in (("ldt", ROW_DT), ("lr", ROW_LR), ("li", ROW_LI)):
                link(V.tensor_copy(S[name].rearrange("p (l j) -> p l j", l=L), cols[:, :, row:row + ST]))
            V.sem_inc(cols_ready, 1)
            note(ssm_act, 1)
            tt = lambda o_, x, y, op: link(V.tensor_tensor(S[o_], S[x], S[y], op))
            tt("lrdt", "lr", "dt", ALU.mult)
            V.sem_inc(ssm_arg, 1)
            tt("lidt", "li", "dt", ALU.mult)
            link(V.tensor_scalar(S["rnd"], S["lidt"], 1 / (2 * math.pi), MAGIC, ALU.mult, ALU.add))
            link(V.tensor_scalar(S["rnd"], S["rnd"], MAGIC, None, ALU.subtract))
            link(V.scalar_tensor_tensor(S["ang"], S["rnd"], -TWO_PI_A, S["lidt"], ALU.mult, ALU.add))
            link(V.scalar_tensor_tensor(S["ang"], S["rnd"], -TWO_PI_B, S["ang"], ALU.mult, ALU.add))
            link(V.scalar_tensor_tensor(S["ang"], S["rnd"], -TWO_PI_C, S["ang"], ALU.mult, ALU.add))
            link(V.tensor_scalar(S["ang"], S["ang"], PI_BELOW, -PI_BELOW, ALU.min, ALU.max))
            V.sem_inc(ssm_arg, 1)
            tt("den", "lr", "lr", ALU.mult)
            tt("t1", "li", "li", ALU.mult)
            tt("den", "den", "t1", ALU.add)
            link(V.reciprocal(S["rden"], S["den"]))
            split.to(4)
            note(ssm_act, 4)
            V.sem_inc(trig_seed, 1)
            tt("ar", "mag", "c1", ALU.mult)
            tt("ai", "mag", "s1", ALU.mult)
            link(V.tensor_scalar(S["xr"], S["ar"], 1.0, None, ALU.subtract))
            tt("t1", "xr", "lr", ALU.mult)
            tt("t2", "ai", "li", ALU.mult)
            tt("t1", "t1", "t2", ALU.add)
            tt("kr", "t1", "rden", ALU.mult)
            tt("t1", "ai", "lr", ALU.mult)
            tt("t2", "xr", "li", ALU.mult)
            tt("t1", "t1", "t2", ALU.subtract)
            tt("ki", "t1", "rden", ALU.mult)

            def conv_tap(l, i):
                if i >= TAPS * CONV_DVE:
                    return
                k, c = divmod(i, CONV_DVE)
                if k > 0:
                    dve.wait_ge(conv_step, l * TAPS * CONV_DVE + i - CONV_DVE + 1)
                conv_add(V, l, c, k).then_inc(conv_step, 1)

            for l in range(L):
                if l > 0:
                    normalise(h, hn, rstd, rstd_ready, hn_ready)
                    x_low("hT", l, ROW_MIX)
                split.upto(("cg", l, 0))
                note(bc_loaded, 64)
                kr = S["kr"].rearrange("p (l j) -> p l j", l=L)[:, l, :].unsqueeze(2).to_broadcast([P, ST, GH])
                ki = S["ki"].rearrange("p (l j) -> p l j", l=L)[:, l, :].unsqueeze(2).to_broadcast([P, ST, GH])
                link(V.memset(arena[:, 0:1024], 0.0))
                for r in range(2):
                    V.tensor_tensor(bt[:, 0, :, :], braw[:, r, :, :], kr, ALU.mult).then_inc(dve_step, 1)
                    steps.n += 1
                    link(V.tensor_tensor(bt[:, 1, :, :], braw[:, 1 - r, :, :], ki, ALU.mult))
                    for q in range(2):
                        rows = slice(64 * q, 64 * q + 64)
                        ins = V.tensor_tensor(bd[rows, r, :, q, :], bt[rows, 0, :, :], bt[rows, 1, :, :],
                                              ALU.subtract if r == 0 else ALU.add)
                        link(ins)
                V.sem_inc(bd_ready, 1)
                if l == 0:
                    note(consts_ready, 1)
                    link(V.tensor_reduce(evod[:, :], blkm[:, :].rearrange("p (b q) -> p q b", q=2), AX_X, ALU.add))
                for q in range(2):
                    link(V.tensor_scalar(xc[:, :, q, :], craw[:, :, :, :].rearrange("p r i n -> p (r i) n"),
                                         evod[:, q:q + 1], None, ALU.mult))
                V.sem_inc(bd_ready, 1)
                split.upto(("ca", l, 0))
                if l == 0:
                    trig(V, steps.by, settle, 0, 0, ST // 2, [tp[:, k, :] for k in range(4)], 0, 1, 16)
                    split.upto(("ca", l, 1))
                tap = [0]

                def conv_taps(k):
                    for _ in range(k):
                        conv_tap(l, tap[0])
                        tap[0] += 1

                link(V.memset(upad[:, :, 0:PAD], 0.0))
                for i in range(2):
                    n = ("ca", l, i)
                    o = result(n)
                    note(tanh_ready, 1)
                    evac(n, V.scalar_tensor_tensor(upad[:, 2 * i:2 * i + 2, PAD:PAD + T],
                                                   tg[:, i, :].rearrange("p (c n) -> p c n", c=2), 1.0,
                                                   o.rearrange("p (c n) -> p c n", c=2), ALU.add, ALU.mult))
                    if l == 0 and i == 0:
                        trig(V, steps.by, settle, 0, 0, ST // 2, [tp[:, k, :] for k in range(4)], 0, 16, 64)
                link(conv_add(V, l, CT_ - 1, 0))
                V.sem_inc(upad_ready, 1)
                if l == 0:
                    normalise(mem, mem, mrstd, mrstd_ready, mn_ready)
                for r in range(2):
                    n = ("bd", l, r)
                    o = result(n)
                    evac(n, V.tensor_copy(bdT[:, r, :, :].rearrange("p i n -> p (i n)"), o), bdT_ready)
                if l == 0:
                    for i in (1, 3):
                        n = ("memT", i)
                        o = result(n)
                        gain = cols[:, 0, ROW_MEM + 2 * i:ROW_MEM + 2 * i + 2].unsqueeze(2).to_broadcast([P, 2, T])
                        evac(n, V.tensor_tensor(memT[:, 2 * i:2 * i + 2, :], o.rearrange("p (j n) -> p j n", j=2), gain,
                                                ALU.mult), memT_dve)
                if l == 0:
                    trig(V, steps.by, settle, 0, 0, ST // 2, [tp[:, k, :] for k in range(4)], 0, 64)
                conv_taps(TAPS_FIRST)

                def halves(x, n=2):
                    return x.rearrange("p (s a n) -> p s a n", s=n, a=2)

                for p in range(PAIRS):
                    q = l * PAIRS + p
                    jt = slice(2 * p % (ST // 2), 2 * p % (ST // 2) + 2)
                    cp, sn = (trigT[:, p // 4, k, jt, :].unsqueeze(2).to_broadcast([P, 2, 2, P]) for k in range(2))
                    if l == 0 and p in (4, 6):
                        note(trig_pool, 1)
                    if l == 1 and p % 2 == 0:
                        note(trig_pool, 1)
                    n0, n1 = ("bu", l, p, 0), ("bu", l, p, 1)
                    result(n0)
                    result(n1)
                    if q > 0:
                        dve.wait_ge(hst_ready, 2 * q)
                    b0, b1 = AT[n0] % RING_BANKS, AT[n1] % RING_BANKS
                    runs = [(0, 2, b0)] if b1 == b0 + 1 else [(0, 1, b0), (1, 1, b1)]
                    for k, (tab, r) in enumerate(((cp, 0), (sn, 1), (cp, 1), (sn, 0))):
                        for s0, n, b in runs:
                            ins = V.tensor_tensor(halves(tp[:, k, s0 * T:(s0 + n) * T], n), tab[:, s0:s0 + n],
                                                  ps[:, b:b + n, r * T:(r + 1) * T].rearrange("p s (a n) -> p s a n", a=2),
                                                  ALU.mult)
                            if s0 + n == 2:
                                ins.then_inc(rot_in, 1)
                            else:
                                link(ins)
                    note(rot_in, 4)
                    free_bank(n0)
                    free_bank(n1)
                    conv_taps(5)
                    def recur(a_):
                        for r in range(2):
                            if a_ == 0:
                                note(rin_ready, 1)
                            for s in range(2):
                                j = l * ST + 2 * p + s
                                x = tp[:, 2 * r, s * T + a_ * P:s * T + (a_ + 1) * P]
                                V.tensor_tensor_scan(x, S["mag"][:, j:j + 1].to_broadcast([P, P]), x,
                                                     bnd[:, 4 + r, s:s + 1] if a_ else 0.0,
                                                     ALU.mult, ALU.add).then_inc(dve_step, 1)
                                steps.n += 1
                    recur(0)
                    conv_taps(2)
                    dve.wait_ge(dve_step, steps.n)
                    c128, s128 = (S[x][:, l * ST + 2 * p:l * ST + 2 * p + 2] for x in ("c128", "s128"))
                    g_re, g_im = (halves(tp[:, r, :])[:, :, 0, P - 1:P].rearrange("p s n -> p (s n)") for r in (0, 2))
                    for k, (x, y) in enumerate(((c128, g_re), (s128, g_im), (s128, g_re), (c128, g_im))):
                        V.tensor_tensor(bnd[:, k, :], x, y, ALU.mult).then_inc(dve_step, 1)
                        steps.n += 1
                    conv_taps(1)
                    dve.wait_ge(dve_step, steps.n)
                    V.tensor_tensor(bnd[:, 4, :], bnd[:, 0, :], bnd[:, 1, :], ALU.subtract).then_inc(dve_step, 1)
                    V.tensor_tensor(bnd[:, 5, :], bnd[:, 2, :], bnd[:, 3, :], ALU.add).then_inc(dve_step, 1)
                    steps.n += 2
                    conv_taps(1)
                    dve.wait_ge(dve_step, steps.n)
                    recur(1)
                    conv_taps(1)
                    dve.wait_ge(dve_step, steps.n)
                    V.tensor_tensor(halves(tp[:, 1, :]), sn, halves(tp[:, 2, :]), ALU.mult).then_inc(rot_out, 1)
                    V.tensor_tensor(halves(tp[:, 3, :]), sn, halves(tp[:, 0, :]), ALU.mult).then_inc(rot_out, 1)
                    V.tensor_tensor(halves(tp[:, 0, :]), cp, halves(tp[:, 0, :]), ALU.mult).then_inc(rot_out, 1)
                    V.tensor_tensor(halves(tp[:, 2, :]), cp, halves(tp[:, 2, :]), ALU.mult).then_inc(rot_out, 1)
                    conv_taps(2)
                    note(rot_out, 4)
                    if p == PAIRS - 1:
                        split.upto(("mean", l))
                    if p % 2 == 1 and p >= 3:
                        y_skip(dve, link, note, l, (p - 3) // 2)
                    if p == PAIRS - 2:
                        assert tap[0] >= TAPS * CONV_DVE
                        dve.wait_ge(conv_step, (l + 1) * TAPS * CONV_DVE)
                        V.sem_inc(conv_ready, 1)
                def y_low(i):
                    note(y_hi_ready, 1)
                    V.tensor_tensor(y_lo[:, i, :], yT[:, i, :], y_hi[:, i, :].bitcast(F32), ALU.subtract).then_inc(y_lo_ready, 1)

                for i in range(CT_ - 1):
                    y_low(i)
                y_skip(dve, link, note, l, CT_ - 1)
                y_low(CT_ - 1)
                n = ("mean", l)
                o = result(n)
                evac(n, V.scalar_tensor_tensor(conv[:, :, :], o[:, 0:T].unsqueeze(1).to_broadcast([P, CT_, T]), -1.0 / CW,
                                               conv[:, :, :], ALU.mult, ALU.add))
                V.sem_inc(xc_ready, 1)

                def glu(n_):
                    for t in range(TT):
                        n = ("za", l, n_, t)
                        o = result(n)
                        note(tanh_ready, 1)
                        g = gates[:, t, D + n_ * BLK:D + (n_ + 1) * BLK]
                        dst = merged[:, t, n_ * BLK:(n_ + 1) * BLK]
                        evac(n, V.scalar_tensor_tensor(dst, g, 1.0, o, ALU.add, ALU.mult))
                        link(V.scalar_tensor_tensor(dst, tg[:, t, :], 1.0, dst, ALU.add, ALU.mult))
                        V.sem_inc(tanh_used, 1)

                n = ("var", l)
                o = result(n)
                evac(n, V.tensor_scalar(tp[:, 2, 0:TT], o[:, 0:TT], 1.0 / CW, LN_EPS, ALU.mult, ALU.add))
                V.sem_inc(var_ready, 1)
                note(pow_ready, 1)
                for t in range(TT):
                    link(V.tensor_scalar(tp[:, 3, t * P:(t + 1) * P], ident[:, :], tp[:, 2, TT + t:TT + t + 1], None,
                                         ALU.mult))
                V.sem_inc(lnr_ready, 1)
                n = ("rs", l)
                o = result(n)
                evac(n, V.tensor_tensor(conv[:, :, :], conv[:, :, :], o[:, 0:T].unsqueeze(1).to_broadcast([P, CT_, T]),
                                        ALU.mult))
                for c in range(CT_):
                    V.tensor_scalar(conv[:, c, :], conv[:, c, :], cols[:, l, ROW_LG + c:ROW_LG + c + 1],
                                    cols[:, l, ROW_LB + c:ROW_LB + c + 1], ALU.mult, ALU.add).then_inc(dve_step, 1)
                    steps.n += 1
                dve.wait_ge(dve_step, steps.n)
                V.sem_inc(lnz_ready, 1)
                note(gates_ready, 8)
                dve.wait_ge(y_lo_ready, (l + 1) * CT_)
                glu(0)
                note(lnt_ready, 1)
                link(V.scalar_tensor_tensor(conv[:, :, :].rearrange("p c n -> p (c n)"),
                                            tp[:, 0:2, :].rearrange("p i n -> p (i n)"), 1.0,
                                            conv[:, :, :].rearrange("p c n -> p (c n)"), ALU.add, ALU.mult))
                V.sem_inc(u32_ready, 1)
                note(u_hi_ready, 1)
                V.tensor_tensor(u_lo[:, :, :].rearrange("p c n -> p (c n)"), conv[:, :, :].rearrange("p c n -> p (c n)"),
                                u_hi[:, :, :].rearrange("p c n -> p (c n)").bitcast(F32), ALU.subtract).then_inc(u_lo_ready, 1)
                glu(1)
                for n_ in range(2):
                    for t in range(TT):
                        n = ("ya", l, n_, t)
                        o = result(n)
                        dst = merged[:, t, n_ * BLK:(n_ + 1) * BLK]
                        evac(n, V.scalar_tensor_tensor(tp[:, 2 + t, :], gates[:, t, n_ * BLK:(n_ + 1) * BLK], 1.0, o,
                                                       ALU.add, ALU.mult))
                        link(V.tensor_tensor(dst, dst, tp[:, 2 + t, :], ALU.add))
                        if n_ == 1:
                            V.sem_inc(merged_ready, 1)
                for i in range(4):
                    n = ("mT", l, i)
                    o = result(n)
                    note(x_hi_ready, 2)
                    evac(n, V.scalar_tensor_tensor(x_lo[:, 2 * i:2 * i + 2, :].rearrange("p c n -> p (c n)"), o, 0.25,
                                                   x_hi[:, 2 * i:2 * i + 2, :].rearrange("p c n -> p (c n)").bitcast(F32),
                                                   ALU.mult, ALU.subtract), x_lo_ready)
                residual("out", l, dve, note, result, link, free_bank)
                normalise(h, hn, rstd, rstd_ready, hn_ready)
                x_low("hT2", l, ROW_X)

                def maxima(hh):
                    o = result(("sc", l, hh))
                    link(V.tensor_reduce(smx[:, hh, :], o.rearrange("p (t n) -> p t n", t=TT), AX_X, ALU.max))
                    link(V.tensor_scalar(snb[:, hh, :], smx[:, hh, :], -1.0 / math.sqrt(HD), None, ALU.mult))
                    V.sem_inc(nb_ready, 1)

                def probabilities(hh):
                    note(exp_ready, TT)
                    link(V.reciprocal(srec[:, hh, :], ssum[:, hh, :]))
                    for t in range(TT):
                        V.tensor_scalar(prob[:, hh, t, :], prob[:, hh, t, :], srec[:, hh, t:t + 1], None,
                                        ALU.mult).then_inc(prob_ready, 1)

                def copy_pT(hh):
                    n = ("pT", l, hh)
                    o = result(n)
                    evac(n, V.tensor_copy(pT[:, hh, :, :].rearrange("p m n -> p (m n)"), o), pT_ready)

                maxima(0)
                probabilities(0)
                maxima(1)
                copy_pT(0)
                probabilities(1)
                maxima(2)
                maxima(3)
                probabilities(2)
                a_low(("oT", l, 0), 0)
                copy_pT(1)
                probabilities(3)
                copy_pT(2)
                a_low(("oT", l, 1), 2)
                copy_pT(3)
                a_low(("oT", l, 2), 4)
                a_low(("oT", l, 3), 6)
                residual("o", l, dve, note, result, link, free_bank)
                normalise(h, hn, rstd, rstd_ready, hn_ready)
                if l == 0:
                    x_low("hT3", l, ROW_FFN)
                    for b in range(FBLK + 1):
                        for t in range(TT):
                            if b < FBLK:
                                u = 2 * b + t
                                n = ("fgu", b, t)
                                result(n)
                                note(sil_ready, 1)
                                evac(n, V.tensor_tensor(h1[:, u % 4, :], sil[:, u % 4, :], bank(AT[n])[:, 256:512],
                                                        ALU.mult), h1_ready)
                        if b >= 1:
                            piece = [b <= x for x in FPIECE_END].index(True)
                            a_low(("fT", b - 1), 2 * (b - 1 - (FPIECE_END[piece - 1] if piece else 0)))
                        if b in FPIECE_END:
                            piece = FPIECE_END.index(b)
                            for t in range(TT):
                                for n_ in range(2):
                                    n = ("fdn", piece, t, n_)
                                    o = result(n)
                                    dst = h[:, t, n_ * BLK:(n_ + 1) * BLK]
                                    evac(n, V.tensor_tensor(dst, dst, o, ALU.add))
                                    if piece == len(FPIECE_END) - 1:
                                        V.sem_inc(h_ready, 1)

            for i in range(4):
                n = ("hT3", L - 1, i)
                o = result(n)
                gain = cols[:, L - 1, ROW_FFN + 2 * i:ROW_FFN + 2 * i + 2].unsqueeze(2).to_broadcast([P, 2, T])
                evac(n, V.tensor_tensor(xTf[:, 2 * i:2 * i + 2, :], o.rearrange("p (j n) -> p j n", j=2), gain, ALU.mult),
                     xTf_ready)
            note(late_loaded, 64)
            note(late_consts, 1)
            split.first_experts(0, 2)
            link(V.memset(mask[:, :, :], 0.0))
            link(V.memset(gate[:, :, :], 0.0))
            link(V.memset(slot[:, :, :], -1.0))

            n = ("rt",)
            o = result(n)
            def both(x):
                return x.unsqueeze(1).to_broadcast([P, TT, NE]) if x.shape[1] == NE else \
                    x.unsqueeze(2).to_broadcast([P, TT, NE])

            link(V.tensor_tensor(lg[:, :, :], o[:, 0:TT * NE].rearrange("p (t n) -> p t n", t=TT), both(rb), ALU.add))
            free_bank(n)
            for t in range(TT):
                steps.by(V.max(top[:, t, :], lg[:, t, :]))
            settle()
            for t in range(TT):
                steps.by(V.max_index(topu[:, t, :], top[:, t, :], lg[:, t, :]))
            steps.by(V.tensor_tensor(tw[:, 0, :], top[:, :, 1], top[:, :, 0], ALU.subtract))
            settle()
            V.sem_inc(topd_ready, 1)
            link(V.tensor_copy(topi[:, :, :], topu[:, :, :]))
            for i in range(2):
                steps.by(V.tensor_tensor(oneh[:, i, :, :], both(iota[:, 0:NE]), both(topi[:, :, i]), ALU.is_equal))
            settle()
            link(V.tensor_tensor(mask[:, :, 0:NE], oneh[:, 0, :, :], oneh[:, 1, :, :], ALU.add))
            V.sem_inc(mask_ready, 1)
            note(tope_ready, 1)
            link(V.tensor_scalar(tw[:, 2, :], tw[:, 1, :], 1.0, None, ALU.add))
            link(V.reciprocal(tw[:, 2, :], tw[:, 2, :]))
            link(V.tensor_tensor(tw[:, 3, :], tw[:, 1, :], tw[:, 2, :], ALU.mult))
            steps.by(V.tensor_copy(mask[:, :, NE:2 * NE], mask[:, :, 0:NE]))
            for i in range(2):
                steps.by(V.tensor_tensor(oneh[:, i, :, :], oneh[:, i, :, :], both(tw[:, 2 + i, :]), ALU.mult))
            settle()
            link(V.tensor_tensor(gate[:, :, 0:NE], oneh[:, 0, :, :], oneh[:, 1, :, :], ALU.add))
            steps.by(V.tensor_copy(gate[:, :, NE:2 * NE], gate[:, :, 0:NE]))
            n = ("pos",)
            o = result(n)
            pos = o[:, 0:TT * NE].rearrange("p (t n) -> p t n", t=TT)
            steps.by(V.tensor_copy(slot[:, :, 0:NE], pos))
            steps.by(V.tensor_scalar(slot[:, :, NE:2 * NE], pos, float(P), None, ALU.subtract))
            link(V.tensor_reduce(tot[:, 0:1], o[:, 2 * NE:3 * NE], AX_X, ALU.max))
            free_bank(n)
            link(V.tensor_copy(over[:, :], tot[:, 0:1]))
            V.sem_inc(over_ready, 1)

            def one(e):
                return bass.ds(e, 1)

            for t in range(TT):
                link(V.tensor_scalar(pick[:, t, :], iota, slot[:, t, 0:1], mask[:, t, 0:1], ALU.is_equal, ALU.mult))
            V.sem_inc(pick_ready, 1)

            def xg_low(i, done):
                dve.wait_ge(xg_hi_ready, done)
                V.tensor_tensor(xg_lo[:, 4 * i:4 * i + 4, :].rearrange("p k n -> p (k n)"), ps[:, 6 + i, :],
                                xg_hi[:, 4 * i:4 * i + 4, :].rearrange("p k n -> p (k n)").bitcast(F32),
                                ALU.subtract).then_inc(xg_lo_ready, 1)
                dve.wait_ge(xg_lo_ready, done)
                V.sem_inc(ga_read, 1)

            split.first_experts(2, 5)
            for i in range(2):
                xg_low(i, i + 1)
            split.first_experts(5)
            most = dve.value_load(over[0:1, 0:1], min_val=0, max_val=T)
            base = steps.n
            sil_0, h1_0, a_0 = 2 * FBLK, 2 * FBLK, FBLK + L * H

            def expert(it):
                k = [0]
                nxt = [HSLOTS]

                def ahead(name):
                    while nxt[0] < min(EXPERT.bound[name] + AHEAD_H, EH + HSLOTS):
                        split.expert(it, nxt[0])
                        nxt[0] += 1

                def llink(ins):
                    ins.then_inc(dve_step, 1)
                    k[0] += 1
                    dve.wait_ge(dve_step, it * DVE_STEPS + (base + k[0]))

                def lresult(name):
                    ahead(name)
                    dve.wait_ge(mm_done, it * PER + LAT[name] + 1)
                    return bank(LAT[name])

                def lfree(name):
                    V.sem_inc(bank_free[LAT[name] % RING_BANKS], 1)

                for t in range(TT):
                    llink(V.tensor_scalar(pickg[:, t, :], iota, slot[:, t, one(it)], gate[:, t, one(it)],
                                          ALU.is_equal, ALU.mult))
                V.sem_inc(pickg_ready, 1)
                for t in range(TT):
                    llink(V.tensor_scalar(pick[:, t, :], iota, slot[:, t, one(it + 1)], mask[:, t, one(it + 1)],
                                          ALU.is_equal, ALU.mult))
                V.sem_inc(pick_ready, 1)
                for name in LOOP:
                    if name[0] == "gu":
                        b = name[1]
                        ahead(name)
                        dve.wait_ge(sil_ready, it * EBLK + (sil_0 + b + 1))
                        o = bank(LAT[name])
                        V.tensor_tensor(h1[:, b % 4, :], sil[:, b % 4, :], o[:, 256:512], ALU.mult).then_inc(h1_ready, 1)
                        dve.wait_ge(h1_ready, it * EBLK + (h1_0 + b + 1))
                        lfree(name)
                    elif name[0] == "eT":
                        j = name[1]
                        f = 4 * j if 2 * j < EPIECES[0][1] else 4 * j - 2 * EPIECES[1][0]
                        o = lresult(name)
                        dve.wait_ge(a_hi_ready, it * (EBLK // 2) + (a_0 + j + 1))
                        V.tensor_tensor(e_lo[:, f:f + 4, :].rearrange("p f n -> p (f n)"), o,
                                        e_hi[:, f:f + 4, :].rearrange("p f n -> p (f n)").bitcast(F32),
                                        ALU.subtract).then_inc(a_lo_ready, 1)
                        dve.wait_ge(a_lo_ready, it * (EBLK // 2) + (a_0 + j + 1))
                        lfree(name)
                    elif name[0] == "edn" and name[1] == 1:
                        n_ = name[2]
                        o = lresult(name)
                        dve.wait_ge(ye_ready, it * 4 + (2 + n_))
                        dst = ye[:, n_ * BLK:(n_ + 1) * BLK]
                        V.tensor_tensor(dst, dst, o, ALU.add).then_inc(ye_ready, 1)
                        dve.wait_ge(ye_ready, it * 4 + (3 + n_))
                        lfree(name)
                        if n_ == 1:
                            xg_low(1, it * 2 + 4)
                    elif name[0] == "gT":
                        o = lresult(name)
                        llink(V.tensor_copy(gT[:, :, :].rearrange("p t n -> p (t n)"), o[:, 0:TT * P]))
                        V.sem_inc(gT_ready, 1)
                        lfree(name)
                        xg_low(0, it * 2 + 3)
                    elif name[0] == "add":
                        _, t, n_ = name
                        o = lresult(name)
                        dst = h[:, t, n_ * BLK:(n_ + 1) * BLK]
                        llink(V.tensor_tensor(dst, dst, o, ALU.add))
                        lfree(name)
                while nxt[0] < EH + HSLOTS:
                    split.expert(it, nxt[0])
                    nxt[0] += 1
                assert k[0] == DVE_STEPS, k[0]

            DVE_STEPS = 2 * TT + 1 + 2 * TT
            with dve.Fori(0, NE) as e:
                expert(e)
            with dve.If(most > P):
                with dve.Fori(0, NE) as e:
                    expert(e + NE)
            for _ in range(2 * TT):
                V.sem_inc(h_ready, 1)
            for t in range(TT):
                note(rstd_ready, 1)
                V.tensor_scalar(hn[:, t, :], h[:, t, :], rstd[:, t:t + 1], None, ALU.mult).then_inc(hn_ready, 1)
                dve.wait_ge(hn_ready, (3 * L + 1) * TT - TT + t + 1)
                V.tensor_tensor(hn[:, t, :], hn[:, t, :], fg, ALU.mult).then_inc(out_ready, 1)

        @block.gpsimd
        def _(pool):
            GP = nc.gpsimd
            steps = Signal(pool_step)
            cnt = {}

            def link(ins):
                pool.wait_ge(pool_step, steps.by(ins))

            def settle():
                pool.wait_ge(pool_step, steps.n)

            def note(sema, k):
                cnt[id(sema)] = cnt.get(id(sema), 0) + k
                pool.wait_ge(sema, cnt[id(sema)])

            def load_bc(l):
                for r, name in enumerate(("ssm_b_re", "ssm_b_im")):
                    src = a[name][l].rearrange("(j q) s h -> (q s) j h", q=2)
                    pool.dma_start(braw[:, r, :, :], src).then_inc(bc_loaded, 16)
                for r, name in enumerate(("ssm_c_re", "ssm_c_im")):
                    src = a[name][l].rearrange("(i g) h s -> (g h) i s", i=CT_)
                    pool.dma_start(craw[:, r, :, :], src).then_inc(bc_loaded, 16)

            load_bc(0)
            link(GP.memset(ident[:, :], 0.0))
            link(GP.affine_select(out=ident[:, :], in_=ident[:, :], compare_op=ALU.not_equal, fill=1.0, base=0,
                                  pattern=[[-1, P]], channel_multiplier=1))
            link(GP.memset(ones[:, :], 1.0))
            link(GP.memset(blkm[:, :], 1.0))
            link(GP.affine_select(out=blkm[:, :], in_=blkm[:, :], compare_op=ALU.is_ge, fill=0.0, base=0,
                                  pattern=[[-GH, 8]], channel_multiplier=1))
            link(GP.affine_select(out=blkm[:, :], in_=blkm[:, :], compare_op=ALU.is_ge, fill=0.0, base=GH - 1,
                                  pattern=[[GH, 8]], channel_multiplier=-1))
            link(GP.memset(neg_half[:, :], -0.5))
            split = Splitter(GP, "pool")
            GP.sem_inc(consts_ready, 1)

            def rms(src, dst, ready, done):
                for t in range(TT):
                    note(ready, 1)
                    link(GP.tensor_scalar(dst[:, t:t + 1], src[:, t:t + 1], 1.0 / D, RMS_EPS, ALU.mult, ALU.add))
                    GP.tensor_tensor(dst[:, t:t + 1], dst[:, t:t + 1], neg_half[:, 0:1], ALU.pow).then_inc(done, 1)

            def late_setup():
                link(GP.affine_select(out=tri, in_=ones[:, :], compare_op=ALU.is_gt, fill=0.0, base=0,
                                      pattern=[[1, P]], channel_multiplier=-1))
                link(GP.iota(iota_i, pattern=[[1, P]], base=0, channel_multiplier=0))
                link(GP.tensor_copy(iota, iota_i))
                GP.sem_inc(late_consts, 1)
                pool.dma_start(fgain, a["norm_ffn_g"][L - 1:L, :].to_broadcast([P, D])).then_inc(late_loaded, 16)
                pool.dma_start(rw, a["router_w"][0].rearrange("(k p) n -> p k n", p=P)).then_inc(late_loaded, 16)
                pool.dma_start(rb, a["router_b"][0:1, :].to_broadcast([P, NE])).then_inc(late_loaded, 16)
                pool.dma_start(fg, a["final_norm_g"].unsqueeze(0).to_broadcast([P, D])).then_inc(late_loaded, 16)

            def h_rms():
                for t in range(TT):
                    note(ssq_ready, 3 if t == 0 else 1)
                    link(GP.tensor_tensor(rstd[:, t:t + 1], ssq[:, t, 0:1], ssq[:, t, 1:2], ALU.add))
                    link(GP.tensor_scalar(rstd[:, t:t + 1], rstd[:, t:t + 1], 1.0 / D, RMS_EPS, ALU.mult, ALU.add))
                    GP.tensor_tensor(rstd[:, t:t + 1], rstd[:, t:t + 1], neg_half[:, 0:1], ALU.pow).then_inc(rstd_ready, 1)

            h_rms()
            rms(mssq, mrstd, mssq_ready, mrstd_ready)
            note(trig_seed, 1)
            for j0 in (ST // 2, ST // 2 + 4):
                trig(GP, steps.by, settle, 0, j0, 4, [ptmp[:, k, :] for k in range(4)], 1)
                GP.sem_inc(trig_pool, 1)
            for l in range(L):
                if l > 0:
                    h_rms()
                tap = [0]

                def conv_taps(k):
                    for _ in range(k):
                        u = l * (TAPS - 1) + tap[0]
                        tap[0] += 1
                        pool.wait_ge(product_ready, u + 1)
                        if u > 0:
                            pool.wait_ge(product_added, u)
                        GP.tensor_tensor(conv[:, CT_ - 1, :], conv[:, CT_ - 1, :], ptmp[:, u % 4, :],
                                         ALU.add).then_inc(product_added, 1)
                    if tap[0] == TAPS - 1:
                        pool.wait_ge(product_added, (l + 1) * (TAPS - 1))
                        GP.sem_inc(conv_ready, 1)

                conv_taps(TAPS - 1 - 4 * (PAIRS - 1))
                split.to(splits_before(TRUNK.bound[("bu", l, 0, 0)] + RAW))
                for p in range(PAIRS):
                    kind, n = FILLERS[p]
                    m_to = splits_before(TRUNK.bound[(kind, l, n, 1)] + AHEAD)
                    note(rot_in, 4)
                    GP.tensor_tensor(tp[:, 0, :], tp[:, 0, :], tp[:, 1, :], ALU.add).then_inc(rin_ready, 1)
                    GP.tensor_tensor(tp[:, 2, :], tp[:, 2, :], tp[:, 3, :], ALU.subtract).then_inc(rin_ready, 1)
                    if p < PAIRS - 1:
                        conv_taps(2)
                    split.to(m_to if p == 0 else max(split.m, m_to - 1))
                    note(rot_out, 4)
                    q = l * PAIRS + p
                    if q >= 1:
                        pool.wait_ge(y_done, q)
                    GP.tensor_tensor(hst[:, 0, :], tp[:, 0, :], tp[:, 1, :], ALU.subtract).then_inc(hst_ready, 1)
                    GP.tensor_tensor(hst[:, 1, :], tp[:, 3, :], tp[:, 2, :], ALU.add).then_inc(hst_ready, 1)
                    if p < PAIRS - 1:
                        conv_taps(2)
                    split.to(m_to)
                split.upto(("zg", l, 0, 1))
                note(var_ready, 1)
                GP.tensor_tensor(tp[:, 2, TT:2 * TT], tp[:, 2, 0:TT], neg_half[:, 0:1].to_broadcast([P, TT]),
                                 ALU.pow).then_inc(pow_ready, 1)
                if l == 0:
                    pool.wait_ge(y_done, PAIRS)
                    load_bc(1)
                split.upto(("out", l, 1, 1))
                h_rms()
                if l == L - 1:
                    late_setup()
                split.upto(("o", l, 1, 1))
                h_rms()
                if l == 0:
                    for j0 in range(0, ST, 4):
                        trig(GP, steps.by, settle, 1, j0, 4, [ptmp[:, k, :] for k in range(4)], 1)
                        GP.sem_inc(trig_pool, 1)
                    split.upto(("fdn", len(FPIECE_END) - 1, 1, 1))
            split.to(len(SPLIT_AT))
            pool.wait_ge(mm_done, AT[("hT3", L - 1, 3)] + 1)
            pool.wait_ge(late_loaded, 64)
            for t in range(TT):
                GP.tensor_tensor(hn[:, t, :], hn[:, t, :], fgain, ALU.mult).then_inc(gained_ready, 1)

            def expert(it):
                for u in range(HSLOTS, EH + HSLOTS):
                    split.expert(it, u)

            split.first_experts()
            pool.wait_ge(over_ready, 1)
            most = pool.value_load(over[0:1, 0:1], min_val=0, max_val=T)
            with pool.Fori(0, NE) as e:
                expert(e)
            with pool.If(most > P):
                with pool.Fori(0, NE) as e:
                    expert(e + NE)
            h_rms()


_INS = ["x", "mem", "mem_norm_g", "norm_mix_g", "w_in", "conv_w", "conv_b", "conv_ln_g", "conv_ln_b", "w_conv_pw",
        "ssm_lambda_re", "ssm_lambda_im", "ssm_log_dt", "ssm_b_re", "ssm_b_im", "ssm_c_re", "ssm_c_im", "ssm_d",
        "w_ssm_glu", "w_out", "norm_xattn_g", "w_q", "w_kv", "w_o", "norm_ffn_g", "ffn_w_gate_up", "ffn_w_down",
        "router_w", "router_b", "moe_w_gate_up", "moe_w_down", "final_norm_g"]


def kernel(**inputs):
    import numpy as np
    import concourse.bacc as bacc
    from concourse.bass_utils import run_bass_kernel_spmd

    nc = bacc.Bacc("TRN2", target_bir_lowering=False, num_devices=1)
    arrays, aps = {}, {}
    for name in _INS:
        x = np.ascontiguousarray(inputs[name])
        arrays[f"in_{name}"] = x
        aps[name] = nc.dram_tensor(f"in_{name}", x.shape, mybir.dt.from_np(x.dtype), kind="ExternalInput").ap()
    out = nc.dram_tensor("out_dram", (1, T, D), F32, kind="ExternalOutput").ap()
    trunk_kernel(nc, aps, out)
    r = run_bass_kernel_spmd(nc, [arrays], core_ids=[0])
    return r.results[0]["out_dram"]
```
